# Optimizing a Trainium2 kernel written in Bass

```python
import math
import jax, jax.numpy as jnp
from jax import lax
import numpy as np

D_MODEL = 1024
BATCH = 1
SEQ = 512
DEPTH = 1

A_HEADS = 8
A_HEAD_DIM = 64
A_WIDTH = A_HEADS * A_HEAD_DIM
IDX_HEADS = 8
IDX_DIM = 32
TOPK_MAX = 256
DSA_BLOCK = 64
S5_WIDTH = 512
S5_GROUP = 16
S5_GROUPS = S5_WIDTH // S5_GROUP
S5_STATE = 64
DT_MIN = 0.001
DT_MAX = 0.1
GLA_HEADS = 4
GLA_DK = 64
GLA_DV = 128
GLA_QK = GLA_HEADS * GLA_DK
GLA_VW = GLA_HEADS * GLA_DV
GLA_RANK = 16
GLA_TAU = 16.0
GLA_CHUNK = 64
N_BRANCH = 3
BRANCH_WIDTH = 512
D_FF = 2816
CONV_W = 3
EPS = 1e-6

IN_SPLITS = (A_WIDTH, A_WIDTH, A_WIDTH,
             IDX_HEADS * IDX_DIM, IDX_DIM, IDX_HEADS,
             S5_WIDTH,
             GLA_QK, GLA_QK, GLA_VW, GLA_VW,
             GLA_RANK,
             N_BRANCH * D_MODEL)
D_IN = sum(IN_SPLITS)

kernel_name = 'hybrid_gated_dsa_s5_gla_trunk'

def rmsnorm(x, g):
    xf = x.astype(jnp.float32)
    y = xf * lax.rsqrt(jnp.mean(xf * xf, axis=-1, keepdims=True) + EPS)
    return (y * g.astype(jnp.float32)).astype(x.dtype)

def adaln(c, w, b):
    m = jax.nn.silu(c) @ w + b
    shift, scale, gate = jnp.split(m[:, None, :], 3, axis=-1)
    return shift, scale, gate

def dsa_attention(q, k, v, qi, ki, wi):
    B, T = q.shape[0], q.shape[1]
    K = min(TOPK_MAX, T // 4)
    nb = T // DSA_BLOCK

    def blocks(a):
        return a.reshape((B, nb, DSA_BLOCK) + a.shape[2:]).swapaxes(0, 1)

    starts = jnp.arange(nb, dtype=jnp.int32) * DSA_BLOCK
    kif = ki.astype(jnp.float32)
    key_pos = jnp.arange(T, dtype=jnp.int32)
    gather = jax.vmap(lambda a, i: a[i])

    def one_block(args):
        qb, qib, wb, t0 = args
        t = t0 + jnp.arange(DSA_BLOCK, dtype=jnp.int32)
        dots = jnp.einsum('bqhd,bsd->bqhs', qib.astype(jnp.float32), kif)
        score = jnp.einsum('bqh,bqhs->bqs', wb.astype(jnp.float32), jax.nn.relu(dots))
        causal = key_pos[None, :] <= t[:, None]
        score = jnp.where(causal[None], score, -jnp.inf)
        _, idx = lax.top_k(score, K)
        valid = idx <= t[None, :, None]
        kg = gather(k, idx)
        vg = gather(v, idx)
        logits = jnp.einsum('bqhd,bqkhd->bqhk', qb, kg,
                            preferred_element_type=jnp.float32) * (A_HEAD_DIM ** -0.5)
        logits = jnp.where(valid[:, :, None, :], logits, -jnp.inf)
        p = jax.nn.softmax(logits, axis=-1).astype(v.dtype)
        return jnp.einsum('bqhk,bqkhd->bqhd', p, vg)

    out = lax.map(one_block, (blocks(q), blocks(qi), blocks(wi), starts))
    return out.swapaxes(0, 1).reshape(B, T, A_WIDTH)

def s5_mixer(u, lam_re, lam_im, log_dt, b_re, b_im, c_re, c_im, d_skip, w_glu):
    B, T = u.shape[0], u.shape[1]
    f32 = jnp.float32
    dt = jnp.exp(log_dt.astype(f32))[:, None]
    lr, li = lam_re.astype(f32), lam_im.astype(f32)
    mag = jnp.exp(lr * dt)
    ab_re, ab_im = mag * jnp.cos(li * dt), mag * jnp.sin(li * dt)
    den = lr * lr + li * li
    nr, ni = ab_re - 1.0, ab_im
    f_re = (nr * lr + ni * li) / den
    f_im = (ni * lr - nr * li) / den
    br, bi = b_re.astype(f32), b_im.astype(f32)
    bb_re = f_re[..., None] * br - f_im[..., None] * bi
    bb_im = f_re[..., None] * bi + f_im[..., None] * br
    ug = u.astype(f32).reshape(B, T, S5_GROUPS, S5_GROUP)
    bu_re = jnp.einsum('gnp,btgp->btgn', bb_re, ug)
    bu_im = jnp.einsum('gnp,btgp->btgn', bb_im, ug)
    a_re = jnp.broadcast_to(ab_re, bu_re.shape)
    a_im = jnp.broadcast_to(ab_im, bu_im.shape)

    def combine(e1, e2):
        a1r, a1i, b1r, b1i = e1
        a2r, a2i, b2r, b2i = e2
        return (a2r * a1r - a2i * a1i,
                a2r * a1i + a2i * a1r,
                a2r * b1r - a2i * b1i + b2r,
                a2r * b1i + a2i * b1r + b2i)

    _, _, x_re, x_im = lax.associative_scan(combine, (a_re, a_im, bu_re, bu_im), axis=1)
    y = (jnp.einsum('gpn,btgn->btgp', c_re.astype(f32), x_re)
         - jnp.einsum('gpn,btgn->btgp', c_im.astype(f32), x_im))
    y = y.reshape(B, T, S5_WIDTH) + d_skip.astype(f32) * u.astype(f32)
    g = jax.nn.gelu(y).astype(u.dtype)
    ga, gb = jnp.split(g @ w_glu, 2, axis=-1)
    return ga * jax.nn.sigmoid(gb)

def gla_mixer(q, k, v, r, lr_feat, w_gate, b_gate, norm_g):
    B, T = q.shape[0], q.shape[1]
    f32 = jnp.float32
    C = GLA_CHUNK
    nc = T // C

    def chunks(a, d):
        return a.reshape(B, nc, C, GLA_HEADS, d).transpose(0, 3, 1, 2, 4)

    log_a = jax.nn.log_sigmoid((lr_feat @ w_gate + b_gate).astype(f32)) / GLA_TAU
    qc = chunks(q.astype(f32), GLA_DK) * (GLA_DK ** -0.5)
    kc = chunks(k.astype(f32), GLA_DK)
    vc = chunks(v.astype(f32), GLA_DV)
    cum = jnp.cumsum(chunks(log_a, GLA_DK), axis=3)
    last = cum[:, :, :, -1:, :]
    q_dec = qc * jnp.exp(cum)
    k_inv = kc * jnp.exp(-cum)
    k_tail = kc * jnp.exp(last - cum)
    tri = jnp.tril(jnp.ones((C, C), dtype=bool))
    att = jnp.where(tri, jnp.einsum('bhncd,bhnsd->bhncs', q_dec, k_inv), 0.0)
    o_intra = jnp.einsum('bhncs,bhnse->bhnce', att, vc)
    kv_chunk = jnp.einsum('bhnsd,bhnse->bhnde', k_tail, vc)
    decay = jnp.exp(last[:, :, :, 0, :])

    def step(S, inp):
        dec, kv = inp
        return dec[..., None] * S + kv, S

    S0 = jnp.zeros((B, GLA_HEADS, GLA_DK, GLA_DV), f32)
    _, S_prev = lax.scan(step, S0, (jnp.moveaxis(decay, 2, 0), jnp.moveaxis(kv_chunk, 2, 0)))
    S_prev = jnp.moveaxis(S_prev, 0, 2)
    o_inter = jnp.einsum('bhncd,bhnde->bhnce', q_dec, S_prev)
    o = (o_intra + o_inter).transpose(0, 2, 3, 1, 4).reshape(B, T, GLA_HEADS, GLA_DV)
    o = rmsnorm(o, norm_g).reshape(B, T, GLA_VW).astype(q.dtype)
    return o * jax.nn.silu(r)

def token_mixing(h, w_in, s5_lam_re, s5_lam_im, s5_log_dt, s5_b_re, s5_b_im, s5_c_re, s5_c_im,
                 s5_d, s5_w_glu, gla_w_gate, gla_b_gate, gla_norm_g, w_branch, w_out):
    B, T = h.shape[0], h.shape[1]
    proj = h @ w_in
    split_at = [int(i) for i in np.cumsum(IN_SPLITS)[:-1]]
    aq, ak, av, iq, ik, iw, s5u, gq, gk, gv, gr, glr, gl = jnp.split(proj, split_at, axis=-1)
    y_a = dsa_attention(aq.reshape(B, T, A_HEADS, A_HEAD_DIM),
                        ak.reshape(B, T, A_HEADS, A_HEAD_DIM),
                        av.reshape(B, T, A_HEADS, A_HEAD_DIM),
                        iq.reshape(B, T, IDX_HEADS, IDX_DIM), ik,
                        iw * ((IDX_HEADS * IDX_DIM) ** -0.5))
    y_b = s5_mixer(s5u, s5_lam_re, s5_lam_im, s5_log_dt, s5_b_re, s5_b_im, s5_c_re, s5_c_im,
                   s5_d, s5_w_glu)
    y_c = gla_mixer(gq, gk, gv, gr, glr, gla_w_gate, gla_b_gate, gla_norm_g)
    ys = jnp.stack([y_a, y_b.astype(h.dtype), y_c], axis=2)
    branch = jnp.einsum('btie,ied->btid', ys, w_branch)
    gate = jax.nn.sigmoid(gl.reshape(B, T, N_BRANCH, D_MODEL).astype(jnp.float32)).astype(h.dtype)
    merged = jnp.sum(gate * branch, axis=2)
    return merged @ w_out

def causal_dwconv(x, w, b):
    T = x.shape[1]
    xp = jnp.pad(x, ((0, 0), (CONV_W - 1, 0), (0, 0)))
    return sum(w[j] * xp[:, j:j + T] for j in range(CONV_W)) + b

def conv_ffn(h, w_up, conv_w, conv_b, w_down):
    u = causal_dwconv(h @ w_up, conv_w, conv_b)
    g, val = jnp.split(u, 2, axis=-1)
    return (jax.nn.gelu(g, approximate=True) * val) @ w_down

def setup_inputs(seed: int = 0) -> dict:
    key = jax.random.key(seed)
    ks = iter(jax.random.split(key, 32))
    f32 = jnp.float32

    def nrm(shape, scale):
        return jax.random.normal(next(ks), shape, f32) * scale

    L, D = DEPTH, D_MODEL
    n_idx = jnp.arange(S5_STATE, dtype=f32)
    return {
        'x': nrm((BATCH, SEQ, D), 1.0),
        'c': nrm((BATCH, D), 1.0),
        'mix_mod_w': nrm((L, D, 3 * D), D ** -0.5),
        'mix_mod_b': nrm((L, 3 * D), 0.01),
        'mix_pre_g': 1.0 + nrm((L, D), 0.02),
        'mix_post_g': 1.0 + nrm((L, D), 0.02),
        'w_in': nrm((L, D, D_IN), D ** -0.5),
        's5_lam_re': -0.5 + nrm((L, S5_GROUPS, S5_STATE), 0.01),
        's5_lam_im': jnp.pi * n_idx + nrm((L, S5_GROUPS, S5_STATE), 0.01),
        's5_log_dt': jax.random.uniform(next(ks), (L, S5_GROUPS), f32,
                                        math.log(DT_MIN), math.log(DT_MAX)),
        's5_b_re': nrm((L, S5_GROUPS, S5_STATE, S5_GROUP), (2.0 * S5_GROUP) ** -0.5),
        's5_b_im': nrm((L, S5_GROUPS, S5_STATE, S5_GROUP), (2.0 * S5_GROUP) ** -0.5),
        's5_c_re': nrm((L, S5_GROUPS, S5_GROUP, S5_STATE), (2.0 * S5_STATE) ** -0.5),
        's5_c_im': nrm((L, S5_GROUPS, S5_GROUP, S5_STATE), (2.0 * S5_STATE) ** -0.5),
        's5_d': nrm((L, S5_WIDTH), 1.0),
        's5_w_glu': nrm((L, S5_WIDTH, 2 * S5_WIDTH), S5_WIDTH ** -0.5),
        'gla_w_gate': nrm((L, GLA_RANK, GLA_QK), GLA_RANK ** -0.5),
        'gla_b_gate': nrm((L, GLA_QK), 0.01),
        'gla_norm_g': 1.0 + nrm((L, GLA_HEADS, GLA_DV), 0.02),
        'w_branch': nrm((L, N_BRANCH, BRANCH_WIDTH, D), BRANCH_WIDTH ** -0.5),
        'w_out': nrm((L, D, D), D ** -0.5),
        'ffn_mod_w': nrm((L, D, 3 * D), D ** -0.5),
        'ffn_mod_b': nrm((L, 3 * D), 0.01),
        'ffn_pre_g': 1.0 + nrm((L, D), 0.02),
        'ffn_post_g': 1.0 + nrm((L, D), 0.02),
        'ffn_w_up': nrm((L, D, 2 * D_FF), D ** -0.5),
        'ffn_conv_w': nrm((L, CONV_W, 2 * D_FF), CONV_W ** -0.5),
        'ffn_conv_b': nrm((L, 2 * D_FF), 0.01),
        'ffn_w_down': nrm((L, D_FF, D), D_FF ** -0.5),
    }

def reference(x, c, mix_mod_w, mix_mod_b, mix_pre_g, mix_post_g, w_in,
              s5_lam_re, s5_lam_im, s5_log_dt, s5_b_re, s5_b_im, s5_c_re, s5_c_im, s5_d, s5_w_glu,
              gla_w_gate, gla_b_gate, gla_norm_g, w_branch, w_out,
              ffn_mod_w, ffn_mod_b, ffn_pre_g, ffn_post_g, ffn_w_up, ffn_conv_w, ffn_conv_b,
              ffn_w_down):
    for l in range(DEPTH):
        shift, scale, gate = adaln(c, mix_mod_w[l], mix_mod_b[l])
        h = rmsnorm(x, mix_pre_g[l]) * (1.0 + scale) + shift
        y = token_mixing(h, w_in[l], s5_lam_re[l], s5_lam_im[l], s5_log_dt[l], s5_b_re[l],
                         s5_b_im[l], s5_c_re[l], s5_c_im[l], s5_d[l], s5_w_glu[l],
                         gla_w_gate[l], gla_b_gate[l], gla_norm_g[l], w_branch[l], w_out[l])
        x = x + gate * rmsnorm(y, mix_post_g[l])
        shift, scale, gate = adaln(c, ffn_mod_w[l], ffn_mod_b[l])
        h = rmsnorm(x, ffn_pre_g[l]) * (1.0 + scale) + shift
        y = conv_ffn(h, ffn_w_up[l], ffn_conv_w[l], ffn_conv_b[l], ffn_w_down[l])
        x = x + gate * rmsnorm(y, ffn_post_g[l])
    return x


_drawn_inputs = setup_inputs


def setup_inputs(seed=0):
    import zlib

    import numpy as np

    out = dict(_drawn_inputs(seed))
    spreads = {}
    factors = {'mix_mod_b': 2.709,
     'mix_post_g': 4.687,
     's5_lam_re': 64.0,
     's5_lam_im': 24.2,
     's5_log_dt': 31.448,
     's5_b_re': 34.088,
     's5_b_im': 39.264,
     's5_c_re': 35.744,
     's5_c_im': 35.68,
     'gla_b_gate': 8.0,
     'gla_norm_g': 22.309,
     'ffn_mod_b': 5.483,
     'ffn_pre_g': 5.103,
     'ffn_post_g': 23.679,
     'ffn_conv_b': 30.165}
    for name, (base, spread) in spreads.items():
        noise = np.random.default_rng([zlib.crc32(name.encode()), seed]).standard_normal(out[name].shape)
        drawn = base * np.exp(spread * noise) if base else spread * noise
        out[name] = __import__('jax').numpy.asarray(drawn.astype(out[name].dtype))
    for name, factor in factors.items():
        out[name] = (out[name] * factor).astype(out[name].dtype)
    return out
```

```python
from contextlib import ExitStack
import math

import concourse.bass as bass
from concourse import mybir

F32 = mybir.dt.float32
F32R = mybir.dt.float32r
U32 = mybir.dt.uint32
ALU = mybir.AluOpType
ACT = mybir.ActivationFunctionType
AX = mybir.AxisListType

P = 128
T = 512
D = 1024
NT = T // P
NK = D // P
HA, DH = 8, 64
HI, DI = 8, 32
TOPK = min(256, T // 4)
BW = 512
NB = BW // P
NBR = 3
SG, SP_, SN = 32, 16, 64
GP = SG // 2
L = P // SP_
NM = T // L
GH, GDK, GDV, GC = 4, 64, 128, 64
NC = T // GC
RANK = 16
TAU = 16.0
FF = 2816
NF = FF // P
EPS = 1e-6
BIG = 1.0e30
TAKEN = -3.4e38
NEVER = -3.3e38

C_AQ, C_AK, C_AV, C_IQ, C_IK, C_IW = 0, 512, 1024, 1536, 1792, 1824
C_U, C_GQ, C_GK, C_GV, C_GR, C_LR, C_GL = 1832, 2344, 2600, 2856, 3368, 3880, 3896

V_MB, V_PRE, V_POST, V_C, V_SD, V_GB, V_GN, V_FMB, V_FPRE, V_FPOST = 0, 24, 32, 40, 48, 52, 54, 58, 82, 90
V_CW, V_CB, V_LR, V_LI, V_N = 98, 230, 274, 290, 306

RING = 3
SW = 256


def count_up(parts):
    at, n = {}, 0
    for name, uses in parts:
        at[name] = n
        n += uses
    return at


SLAB = count_up([("mod", 8), ("iq", 1), ("u", 2), ("q", 2), ("k", 2), ("v", 2), ("modg", 4), ("gq", 1), ("gk", 1),
                 ("gv", 2), ("gr", 2), ("glu", 2), ("merge", 24), ("out", 4), ("up", 22), ("down", 11), ("end", 0)])
PARTS = ((0, 0), (0, 1), (1, 0))
ACC = count_up([("x", NK), ("iq", 2), ("ik", 1), ("lr", 1), ("iw", 1), ("u", 4), ("q", 4), ("k", 4), ("v", 4),
                ("gq", 2), ("gk", 2), ("gv", 4), ("gr", 4), ("glu", 8), ("merge", 48), ("out", 8), ("up", 44),
                ("down", 4), ("xo", 8)])
SIDE = count_up([("vec", 1), ("ctr", 2), ("mod", 1), ("dots", 24), ("w1", 8), ("lag", 2), ("shift", 8), ("state", 4),
                 ("modg", 1), ("y", 4), ("z", 2), ("att", 64), ("ya", 4), ("kt", 2), ("kv", 4), ("gatt", 4),
                 ("o", 4), ("ot", 4), ("fmod", 12), ("down", 3)])
SLOW = count_up([("rms0", 1), ("pv", 4), ("rms1", 1), ("rms2", 1), ("down", 1), ("rms3", 1)])


def s_use(i):
    return SIDE["att"] + max(2 * i - 1, 0)


def pt_use(i):
    return SIDE["att"] + min(2 * i + 2, 2 * NT * HA - 1)


DOWN_ORDER = (7, 0, 1, 2, 3, 4, 5, 6)


class Steps:

    def __init__(self, eng, sem):
        self.eng, self.sem, self.n = eng, sem, 0

    def do(self, ins):
        ins.then_inc(self.sem, 1)
        self.n += 1

    def settle(self):
        self.eng.wait_ge(self.sem, self.n)


def trunk_kernel(nc, x, c, mix_mod_w, mix_mod_b, mix_pre_g, mix_post_g, w_in, s5_lam_re, s5_lam_im, s5_log_dt,
                 s5_b_re, s5_b_im, s5_c_re, s5_c_im, s5_d, s5_w_glu, gla_w_gate, gla_b_gate, gla_norm_g, w_branch,
                 w_out, ffn_mod_w, ffn_mod_b, ffn_pre_g, ffn_post_g, ffn_w_up, ffn_conv_w, ffn_conv_b, ffn_w_down,
                 out):
    ctx = ExitStack()
    with ctx:
        def sb(name, shape, dt=F32):
            return ctx.enter_context(nc.sbuf_tensor(name, shape, dt))

        def sem(name):
            return ctx.enter_context(nc.semaphore(name))

        def sems(name, n):
            return [sem(f"{name}{i}") for i in range(n)]

        with ExitStack() as early:
            def region(stack, name, shape, dt=F32):
                return stack.enter_context(nc.sbuf_tensor(name, shape, dt))

            ring = region(early, "ring", [P, RING, NK * SW])
            ys = region(early, "ys", [P, NBR, NB, T])
            hT = region(early, "hT", [P, NK, T])
            arena = region(early, "arena", [P, 12288])
            a_w1t = region(early, "a_w1t", [P, 4352])[:, :]
            a_ph = region(early, "a_ph", [P, 2048])[:, :]
            a_tmp = region(early, "a_tmp", [P, 2048])[:, :]
            a_s5 = region(early, "a_s5", [P, 2560])[:, :]
            a_k = region(early, "a_k", [P, 2048])[:, :]
            a_v = region(early, "a_v", [P, 2048])[:, :]
            mb = region(early, "mb", [P, NT, T])
            a_idx = region(early, "a_idx", [P, 2048])[:, :]
        w_lo = sb("w_lo", [P, RING, NK * SW], F32R)
        ys_lo = sb("ys_lo", [P, NBR, NB, T], F32R)
        h_lo = sb("h_lo", [P, NK, T], F32R)
        m_lo = sb("m_lo", [P, NK, T], F32R)
        m_hi = sb("m_hi", [P, NK, T], F32R)
        fmod_slab = sb("fmod_slab", [P, NK, SW])
        ys_hi0 = sb("ys_hi0", [P, NB, T], F32R)
        sb("x_again", [P, 4352])
        w_hi = sb("w_hi", [P, 2, NK * SW], F32R)
        ff_hi = sb("ff_hi", [P, 2, 2 * T], F32R)
        sb("a_s5_rest", [P, 512])
        ys_hi1 = sb("ys_hi1", [P, NB, T], F32R)
        ys_hi2 = sb("ys_hi2", [P, NB, T], F32R)
        h_hi = sb("h_hi", [P, NK, T], F32R)
        ys_hi = (ys_hi0, ys_hi1, ys_hi2)
        ff_lo = ys_lo[:, 2].rearrange("p (s a) t -> p s (a t)", s=2)
        a_w1, a_w2, a_u, a_ub, a_q = (arena[:, 0:4096], arena[:, 4096:6144], arena[:, 6144:8192],
                                      arena[:, 8192:10240], arena[:, 10240:12288])
        vT = sb("vT", [P, V_N])
        ident = sb("ident", [P, P])
        wide = sb("wide", [P, (L - 1) * SP_ + P])
        mean = sb("mean", [P, P])
        chunkmask = sb("chunkmask", [P, P])
        csil = sb("csil", [P, NK])
        mod = sb("mod", [P, 24])
        fmod = sb("fmod", [P, 24])
        pre = sb("pre", [P, NK])
        post = sb("post", [P, NK])
        fpre = sb("fpre", [P, NK])
        fpost = sb("fpost", [P, NK])
        a_wk = sb("a_wk", [P, 1536])[:, :]
        stat = sb("stat", [P, 64])
        amax = sb("amax", [P, NT, HA])
        asum = sb("asum", [P, NT, HA])
        cs = sb("cs", [P, 3, 4, 4])
        iw = sb("iw", [P, NT, HI])
        wgate = sb("wgate", [RANK, GH * GDK])
        cT = sb("cT", [P, 3, GP, SP_])
        apw = sb("apw", [P, 2, GP, L + 1])
        sc = sb("sc", [P, 28, GP])
        gemv = sb("gemv", [P, 2, SW])

        bank = [ctx.enter_context(nc.psum_tensor(f"bank{i}", [P, 512], F32)) for i in range(8)]
        x_keep = nc.dram_tensor("x_keep", (P, NK, T), F32).ap()
        u_dram = nc.dram_tensor("u_dram", (SG, SP_, L, NM), F32).ap()
        y_dram = nc.dram_tensor("y_dram", (SG, SP_, L, NM), F32).ap()

        def tiles(region, n):
            return region.rearrange("p (a t) -> p a t", a=n)

        q_sb, k_sb, v_sb = tiles(a_q, NB), tiles(a_k, NB), tiles(a_v, NT)
        vrow = a_k[:, 0:3 * P].rearrange("p (a b) -> p a b", a=3)
        wsmall = a_k[:, 512:512 + NK * 152].rearrange("p (k n) -> p k n", k=NK)
        xtok = a_w1t[:, 0:4096].rearrange("p (a d) -> p a d", a=NT)
        xT = tiles(a_w1, NK)
        sq = tiles(a_wk[:, 0:1024], 2)
        rb = a_wk[:, 1024:1536]
        iqT, ikT, lrT = tiles(a_idx[:, 0:1024], 2), a_idx[:, 1024:1536], a_idx[0:RANK, 1536:2048]
        relu, work = tiles(a_wk[:, 0:1024], 2), a_wk[:, 1024:1536]
        uP = a_u.rearrange("p (a j m) -> p a j m", a=NB, j=L)
        ub = a_ub.rearrange("p (g m) -> p g m", g=SG)
        w1T = a_w1t[:, 0:4096].rearrange("p (c g i q) -> p c g i q", c=2, g=GP, i=L)
        zst = a_w1t[:, 0:2048].rearrange("p (c g m) -> p c g m", c=2, g=GP)
        xst = a_w1t[:, 2048:2048 + 2 * GP * (NM + 1)].rearrange("p (c g m) -> p c g m", c=2, g=GP)
        w1 = a_w1.rearrange("p (c g n) -> p c g n", c=2, g=GP)
        w2 = [ys[:, 2].rearrange("p a t -> p (a t)").rearrange("p (g j q) -> p g j q", g=GP, j=L),
              a_w2.rearrange("p (g j q) -> p g j q", g=GP, j=L)]
        toep = ys[:, 0:2].rearrange("p b a t -> p (b a t)").rearrange("p (g j q) -> p g j q", g=SG, j=L)
        ph = a_ph.rearrange("p (c g m) -> p c g m", c=2, g=GP)
        yblk = a_tmp.rearrange("p (g m) -> p g m", g=SG)
        yback = tiles(a_ph, NB)
        rho = a_s5[:, 0:1024].rearrange("p (g m) -> p g m", g=GP)
        brow = a_s5[:, 1024:1536].rearrange("p (c g q) -> p c g q", c=2, g=GP)
        bb = a_s5[:, 1536:2048].rearrange("p (c g q) -> p c g q", c=2, g=GP)
        lag = a_s5[:, 2048:2560]
        crow = a_q[:, 0:1024].rearrange("p (c r d n) -> p c r d n", c=2, r=4, d=2)
        gq, gk, cum, e1 = (tiles(a_w1[:, 1024 * i:1024 * i + 1024], 2) for i in range(4))
        e2, e3 = (tiles(a_w1t[:, 1024 * i:1024 * i + 1024], 2) for i in range(2))
        ktok = a_w1t[:, 2048:3072].rearrange("p (a d) -> p a d", a=NT)
        tail = tiles(a_w1t[:, 3072:4096], 2)
        gv, sr, og = tiles(a_ub, NT), tiles(a_w2, GH), tiles(a_u, NT)
        sprev = ys[:, 2].rearrange("p a t -> p (a t)").rearrange("p (a c e) -> p a c e", a=2, c=NC)
        gatt = a_tmp.rearrange("p (h t q) -> p h t q", h=GH, t=NT)
        keep, osq = a_s5[:, 0:512], a_s5[:, 512:1024]
        logit, prob = tiles(a_idx[:, 0:1024], 2), tiles(a_wk[:, 0:1024], 2)
        probT = tiles(a_s5[:, 1536:2560], 2)
        ytok = tiles(a_ph, NT)
        merged, x1 = tiles(a_w1, NK), a_w1t[:, 0:4096].rearrange("p (k t) -> p k t", k=NK)
        msig, mtmp = tiles(a_wk[:, 0:1024], 2), a_wk[:, 1024:1536]
        yT = ys[:, 0:2].rearrange("p b a t -> p (b a) t")
        ff = tiles(arena[:, 0:NF * T], NF)
        cb, gl = tiles(a_k, 4), tiles(a_v[:, 0:1024], 2)
        xo = arena[:, 0:NT * D].rearrange("p (t d) -> p t d", t=NT)
        slab_in = sems("slab_in", RING)
        slab_used = sem("slab_used")
        w_top, w_ready = sem("w_top"), sem("w_ready")
        half_top, half_ready = sem("half_top"), sem("half_ready")
        h_top, h_split = sem("h_top"), sem("h_split")
        y2_top, y2_ready = sem("y2_top"), sem("y2_ready")
        m_split = sem("m_split")
        h2_top, h2_ready = sem("h2_top"), sem("h2_ready")
        ff_top, ff_split = sem("ff_top"), sem("ff_split")
        fmod_in = sem("fmod_in")
        gemv_k = sem("gemv_k")
        acc_done = sem("acc_done")
        acc_out = sems("acc_out", 4)
        side_done = sem("side_done")
        side_out = sems("side_out", 3)
        slow_done = sem("slow_done")
        slow_out = sem("slow_out")
        vstep, astep, gstep = sem("vstep"), sem("astep"), sem("gstep")
        x_in, vec_in, c_in, b_in, dt_in, small_in = (sem(n) for n in (
            "x_in", "vec_in", "c_in", "b_in", "dt_in", "small_in"))
        x_kept, x_back, u_store, ub_in, y_store, y_in, out_st = (sem(n) for n in (
            "x_kept", "x_back", "u_store", "ub_in", "y_store", "y_in", "out_st"))
        consts = sem("consts")
        sq_used = sem("sq_used")
        rms_root, rinv = sem("rms_root"), sem("rinv")
        sq_ready = sem("sq_ready")
        c_sig, c_silu = sem("c_sig"), sem("c_silu")
        mod_ready, post_ready = sem("mod_ready"), sem("post_ready")
        hx, h_ready = sem("hx"), sem("h_ready")
        dt_exp, s5_ang, s5_trig, s5_pow = sem("dt_exp"), sem("s5_ang"), sem("s5_trig"), sem("s5_pow")
        s5_tables, w2_ready = sem("s5_tables"), sem("w2_ready")
        score_mul = sem("score_mul")
        score_masked = sem("score_masked")
        mask0_ready, mask_ready = sem("mask0_ready"), sem("mask_ready")
        state_ready = sem("state_ready")
        yd_ready, g_ready = sem("yd_ready"), sem("g_ready")
        p_ready = sem("p_ready")
        r_sig = sem("r_sig")
        f_abs, f_exp, f_cum, f_tail = sem("f_abs"), sem("f_exp"), sem("f_cum"), sem("f_tail")
        g_zero, g_dec, g_k = sem("g_zero"), sem("g_dec"), sem("g_k")
        carried = sem("carried")
        o_sum, o_root, o_inv, o_norm = sem("o_sum"), sem("o_root"), sem("o_inv"), sem("o_norm")
        merge_sum = sem("merge_sum")
        fmod_ready = sem("fmod_ready")
        x1_ready, x2_ready = sem("x1_ready"), sem("x2_ready")
        taps = sem("taps")
        conv_0, conv_1, gelu_out, ff_ready = sem("conv_0"), sem("conv_1"), sem("gelu_out"), sem("ff_ready")

        def acc(n):
            return bank[n % 4]

        def side(n):
            return bank[4 + n % 3]

        slow = bank[7]

        def acc_read(eng, n):
            eng.wait_ge(acc_done, n + 1)

        def acc_copied(eng, n):
            eng.wait_ge(acc_out[n % 4], n // 4 + 1)

        def side_read(eng, n):
            eng.wait_ge(side_done, n + 1)

        def side_copied(eng, n):
            eng.wait_ge(side_out[n % 3], n // 3 + 1)

        def slow_read(eng, n):
            eng.wait_ge(slow_done, n + 1)

        def slow_copied(eng, n):
            eng.wait_ge(slow_out, n + 1)

        def down_bank(m):
            if m < 4:
                return acc(ACC["down"] + m)
            return side(SIDE["down"] + m - 4) if m < 7 else slow

        def slab_k(s, cols=SW):
            return ring[:, s % RING, :].rearrange("p (k n) -> p k n", n=cols)

        def rows(w):
            return w.rearrange("(k p) n -> p k n", p=P)

        def split_no(s):
            return s - SLAB["merge"]

        block = ctx.enter_context(nc.Block())

        def o_part(b):
            return og[:, 2 * (b // 2):2 * (b // 2) + 2, :].rearrange("p t (h d e) -> p t d h e", h=2, d=2)[:, :, b % 2]

        @block.sync
        def _(sp):
            def load(s, view, src):
                if s >= RING:
                    sp.wait_ge(slab_used, s - RING + 1)
                sp.dma_start(view, src).then_inc(slab_in[s % RING], 16)

            def slabs(name, w, col, n):
                for j in range(n):
                    load(SLAB[name] + j, slab_k(SLAB[name] + j), rows(w[:, col + SW * j:col + SW * j + SW]))

            def half_slabs(name, w, col):
                for j in range(2):
                    load(SLAB[name] + j, slab_k(SLAB[name] + j, BW), rows(w[BW * j:BW * j + BW, col:col + BW]))

            win = w_in[0]
            slabs("mod", mix_mod_w[0], 0, 8)
            slabs("iq", win, C_IQ, 1)
            slabs("u", win, C_U, 2)
            slabs("q", win, C_AQ, 2)
            slabs("k", win, C_AK, 2)
            half_slabs("v", win, C_AV)
            slabs("modg", mix_mod_w[0], 2 * D, 4)
            slabs("gq", win, C_GQ, 1)
            slabs("gk", win, C_GK, 1)
            half_slabs("gv", win, C_GV)
            slabs("gr", win, C_GR, 2)
            for j in range(2):
                load(SLAB["glu"] + j, slab_k(SLAB["glu"] + j, BW), rows(s5_w_glu[0][:, BW * j:BW * j + BW]))
            for n in range(SIDE["o"], SIDE["o"] + 4):
                side_read(sp, n)
            with sp.Fori(1, 3) as it:
                for step in range(6):
                    jj, i = step // NBR, step % NBR
                    for m, (w, kt, col) in enumerate(((win, NK, C_GL + D * i), (w_branch[0, i], NB, 0))):
                        s = SLAB["merge"] + 2 * step + m
                        sp.wait_ge(slab_used, it * 12 + (s - RING + 1 - 12))
                        sp.dma_start(slab_k(s)[:, 0:kt, :], rows(w[:, bass.ds(it * (2 * SW) + (col + SW * (jj - 2)), SW)])
                                     ).then_inc(slab_in[s % RING], 16)
                    sp.wait_ge(gemv_k, it * (6 * NK) + NK * (step - 6 + 1))
                    sp.dma_start(fmod_slab[:, :, :], rows(ffn_mod_w[0][:, bass.ds(it * (6 * SW) + SW * (step - 6), SW)])
                                 ).then_inc(fmod_in, 16)
            slabs("out", w_out[0], 0, 4)
            up = ffn_w_up[0]
            with sp.Fori(0, 3) as it:
                for m in range(6):
                    s, half, pair = SLAB["up"] + m, m % 2, m // 2
                    at = sp.snap(it * (3 * SW) + (FF * half + SW * pair))
                    free = sp.snap(it * 6 + (s - RING + 1))
                    sp.wait_ge(slab_used, free)
                    sp.dma_start(slab_k(s), rows(up[:, bass.ds(at, SW)])).then_inc(slab_in[s % RING], 16)
            for m in range(18, 22):
                s, col = SLAB["up"] + m, FF * (m % 2) + SW * (m // 2)
                load(s, slab_k(s), rows(up[:, col:col + SW]))
            for j in range(NF // 2):
                s = SLAB["down"] + j
                load(s, slab_k(s, D), rows(ffn_w_down[0][2 * P * j:2 * P * j + 2 * P, :]))
            for tt in range(NT):
                for half in range(2):
                    acc_copied(sp, ACC["xo"] + 2 * tt + half)
                sp.dma_start(out[0, P * tt:P * tt + P, :], xo[:, tt, :]).then_inc(out_st, 16)
            sp.wait_ge(out_st, 16 * NT)

        @block.gpsimd
        def _(pool):
            st = Steps(pool, gstep)
            small = rows(w_in[0])
            for half in range(2):
                for cc, w in enumerate((s5_c_re, s5_c_im)):
                    pool.dma_start(crow[:, cc, :, half, :],
                                   w[0].rearrange("(r g) p n -> (g p) r n", r=4)).then_inc(c_in, 16)
            for cc, w in enumerate((s5_b_re, s5_b_im)):
                pool.dma_start(brow[:, cc, :, :], w[0].rearrange("(g d) n p -> (d n) g p", d=2)).then_inc(b_in, 16)
            for at, col, n in ((4 * DI, C_IW, HI), (4 * DI + HI, C_LR, RANK), *((DI * r, C_IK, DI) for r in range(4))):
                pool.dma_start(wsmall[:, :, at:at + n], small[:, :, col:col + n]).then_inc(small_in, 16)
            pool.dma_start(wgate[:, :], gla_w_gate[0]).then_inc(small_in, 16)
            st.do(pool.memset(ident[:, :], 0.0))
            st.do(pool.memset(wide[:, :], 0.0))
            st.do(pool.memset(chunkmask[:, :], 1.0))
            pool.memset(mean[:, :], 1.0 / D).then_inc(consts, 1)
            st.settle()
            for m, width in ((ident, P), (wide, (L - 1) * SP_ + P)):
                pool.affine_select(out=m[:, :], in_=m[:, :], compare_op=ALU.not_equal, fill=1.0, base=0,
                                   pattern=[[-1, width]], channel_multiplier=1).then_inc(consts, 1)
            st.do(pool.affine_select(out=chunkmask[:, :], in_=chunkmask[:, :], compare_op=ALU.is_ge, fill=0.0,
                                     base=0, pattern=[[1, P]], channel_multiplier=-1))
            st.settle()
            pool.memset(chunkmask[0:GC, GC:P], 0.0).then_inc(consts, 1)
            for k in range(NK - 4, NK):
                acc_copied(pool, ACC["x"] + k)
            pool.dma_start(x_keep, xT).then_inc(x_kept, 16)
            pool.wait_ge(s5_pow, 1)
            side_copied(pool, SIDE["ctr"])
            side_copied(pool, SIDE["ctr"] + 1)
            for j in range(L):
                ar, ai = (apw[:, cc, :, j + 1:j + 2].broadcast_to([P, GP, SP_]) for cc in range(2))
                t = [a_v[:, 1024 * (j % 2) + 256 * i:1024 * (j % 2) + 256 * i + 256].rearrange(
                    "p (g q) -> p g q", g=GP) for i in range(4)]
                st.do(pool.tensor_tensor(t[0], cT[:, 0], ar, ALU.mult))
                st.do(pool.tensor_tensor(t[1], cT[:, 1], ai, ALU.mult))
                st.do(pool.tensor_tensor(t[2], cT[:, 0], ai, ALU.mult))
                st.do(pool.tensor_tensor(t[3], cT[:, 2], ar, ALU.mult))
                st.settle()
                st.do(pool.tensor_tensor(w2[0][:, :, j, :], t[0], t[1], ALU.subtract))
                st.do(pool.tensor_tensor(w2[1][:, :, j, :], t[3], t[2], ALU.subtract))
            pool.memset(mb[:, 0, 0:P], 0.0).then_inc(w2_ready, 1)
            pool.wait_ge(w2_ready, 1)
            pool.affine_select(out=mb[:, 0, 0:P], in_=mb[:, 0, 0:P], compare_op=ALU.is_ge, fill=-BIG, base=0,
                               pattern=[[-1, P]], channel_multiplier=1).then_inc(mask0_ready, 1)
            for a in range(NB):
                acc_copied(pool, ACC["u"] + a)
            pool.dma_start(u_dram.rearrange("(a g) p j m -> (g p) a (j m)", a=NB),
                           a_u.rearrange("p (a t) -> p a t", a=NB)).then_inc(u_store, 16)
            pool.wait_ge(u_store, 16)
            pool.wait_ge(x_kept, 16)
            for j in range(L):
                pool.dma_start(ub[SP_ * j:SP_ * j + SP_, :, :],
                               u_dram[:, :, j, :].rearrange("g p m -> p g m")).then_inc(ub_in, 16)
            for tt in range(1, NT):
                pool.wait_ge(score_mul, HI * tt)
                d = mb[:, tt, P * tt:P * tt + P]
                pool.affine_select(out=d, in_=d, compare_op=ALU.is_ge, fill=NEVER, base=0,
                                   pattern=[[-1, P]], channel_multiplier=1).then_inc(score_masked, 1)
            for b in range(4):
                side_copied(pool, SIDE["y"] + b)
            for j in range(L):
                pool.dma_start(y_dram[:, :, j, :].rearrange("g p m -> p g m"),
                               yblk[SP_ * j:SP_ * j + SP_, :, :]).then_inc(y_store, 16)
            pool.wait_ge(y_store, 16 * L)
            pool.dma_start(yback, y_dram.rearrange("(a g) p j m -> (g p) a (j m)", a=NB)).then_inc(y_in, 16)
            pool.memset(a_tmp, 0.0).then_inc(g_zero, 1)
            pool.memset(sprev[:, :, 0, :], 0.0).then_inc(g_zero, 1)
            st.do(pool.memset(keep, 1.0))
            st.settle()
            pool.memset(keep.rearrange("p (c t) -> p c t", c=NC)[:, :, 0:1], 0.0).then_inc(g_zero, 1)
            acc_read(pool, ACC["gr"] + GH - 1)
            side_copied(pool, s_use(NT * HA - 1))
            pool.wait_ge(p_ready, NT * HA)
            parts = [(hT, h_hi, h_lo), (ys[:, 0], ys_hi0, ys_lo[:, 0]), (ys[:, 1], ys_hi1, ys_lo[:, 1])]
            for i, (src, hi, lo) in enumerate(parts):
                if i == 1:
                    for tt in range(NT):
                        side_copied(pool, SIDE["ya"] + tt)
                if i == 2:
                    acc_copied(pool, ACC["glu"] + 6)
                pool.tensor_copy(hi[:, :, :], src[:, :, :] if i == 0 else src).then_inc(h_top, 1)
                pool.wait_ge(h_top, i + 1)
                pool.tensor_tensor(lo[:, :, :] if i == 0 else lo, src[:, :, :] if i == 0 else src,
                                   hi[:, :, :].bitcast(F32), ALU.subtract).then_inc(h_split, 1)
            side_copied(pool, SIDE["ot"])
            pool.dma_start(x1, x_keep).then_inc(x_back, 16)
            cols = vT[:, V_CW:V_CW + 8 * NF].rearrange("p (j h n) -> p j h n", j=4, h=2)
            dst = [cs[:, s].rearrange("p j (h n) -> p j h n", h=2) for s in range(3)]
            for s in range(3):
                pool.tensor_copy(dst[s], cols[:, :, :, 2 * s:2 * s + 2]).then_inc(taps, 1)
            with pool.Fori(1, 3) as it:
                for s in range(3):
                    n = ACC["up"] + 4 * s - 9
                    pool.wait_ge(acc_out[n % 4], it * 3 + (n // 4 + 1))
                    pool.tensor_copy(dst[s], cols[:, :, :, bass.ds(it * 6 + 2 * s, 2)]).then_inc(taps, 1)
            for s in range(2):
                acc_copied(pool, ACC["up"] + 4 * (6 + s) + 3)
                pool.tensor_copy(dst[s], cols[:, :, :, 18 + 2 * s:20 + 2 * s]).then_inc(taps, 1)

        @block.scalar
        def _(act):
            st = Steps(act, astep)

            def copy(dst, src, signal, scale=1.0):
                act.activation(dst, src, ACT.Copy, scale=scale).then_inc(signal, 1)

            def acc_copy(n, dst, src=None, scale=1.0):
                acc_read(act, n)
                copy(dst, acc(n)[:, :] if src is None else src, acc_out[n % 4], scale)

            def side_copy(n, dst, src=None, scale=1.0):
                side_read(act, n)
                copy(dst, side(n)[:, :] if src is None else src, side_out[n % 3], scale)

            def squares(k, src, norm, signal):
                if k >= 2:
                    act.wait_ge(sq_used, (NK - 1) * norm + k - 1)
                act.activation(sq[:, k % 2], src, ACT.Square).then_inc(signal, 1)

            def root(name):
                slow_copied(act, SLOW[name])
                act.activation(rb, rb, ACT.Sqrt).then_inc(rms_root, 1)

            act.dma_start(xtok, x[0].rearrange("(a p) d -> p a d", p=P)).then_inc(x_in, 16)
            at = 0
            for v, n in ((mix_mod_b, 24), (mix_pre_g, 8), (mix_post_g, 8), (c, 8), (s5_d, 4), (gla_b_gate, 2),
                         (gla_norm_g, 4), (ffn_mod_b, 24), (ffn_pre_g, 8), (ffn_post_g, 8)):
                src = v[0] if n != 4 or v.shape[-1] != GDV else v[0].rearrange("a b -> (a b)")
                act.dma_start(vrow[at:at + n, 0, :], src.rearrange("(a b) -> a b", b=P)).then_inc(vec_in, 16)
                at += n
            taps_rows = ffn_conv_w[0].rearrange("j (n b) -> (j n) b", b=P)
            act.dma_start(vrow[:, 1, :], taps_rows[0:P, :]).then_inc(vec_in, 16)
            act.dma_start(vrow[0:4, 2, :], taps_rows[P:P + 4, :]).then_inc(vec_in, 16)
            act.dma_start(vrow[4:48, 2, :], ffn_conv_b[0].rearrange("(n b) -> n b", b=P)).then_inc(vec_in, 16)
            for i, v in enumerate((s5_lam_re, s5_lam_im)):
                act.dma_start(vrow[48 + 16 * i:64 + 16 * i, 2, :],
                              v[0].rearrange("(g d) n -> g (d n)", d=2)).then_inc(vec_in, 16)
            log_dt = sc[:, 24:26, :].rearrange("p a g -> p (a g)")
            act.dma_start(log_dt, s5_log_dt[0].partition_broadcast(P)).then_inc(dt_in, 16)

            act.wait_ge(dt_in, 16)
            for d in range(2):
                part = slice(SN * d, SN * d + SN)
                act.activation(sc[part, 1, :], log_dt[part].rearrange("p (g d) -> p d g", d=2)[:, d, :], ACT.Exp
                               ).then_inc(dt_exp, 1)
            side_copy(SIDE["vec"], vT[:, :], side(SIDE["vec"])[:, 0:V_N])
            side_copied(act, SIDE["vec"])
            act.activation(csil[:, :], vT[:, V_C:V_C + NK], ACT.Sigmoid).then_inc(c_sig, 1)
            for cc in range(2):
                n = SIDE["ctr"] + cc
                side_read(act, n)
                for d in range(2):
                    part = slice(SN * d, SN * d + SN)
                    src = side(n)[part, :].rearrange("p (r d q) -> p r d q", d=2, q=SP_)[:, :, d, :]
                    if cc:
                        st.do(act.activation(cT[part, 2], src, ACT.Copy, scale=-1.0))
                    if d:
                        copy(cT[part, cc], src, side_out[n % 3])
                    else:
                        st.do(act.activation(cT[part, cc], src, ACT.Copy))
            for k in range(NK):
                n = ACC["x"] + k
                acc_read(act, n)
                st.do(act.activation(xT[:, k], acc(n)[:, :], ACT.Copy))
                squares(k, acc(n)[:, :], 0, acc_out[n % 4])
            act.wait_ge(s5_ang, 1)
            act.activation(sc[:, 4, :], sc[:, 2, :], ACT.Exp).then_inc(s5_trig, 1)
            act.wait_ge(s5_ang, 2)
            act.activation(sc[:, 6, :], sc[:, 7, :], ACT.Sin).then_inc(s5_trig, 1)
            act.activation(sc[:, 5, :], sc[:, 3, :], ACT.Sin).then_inc(s5_trig, 1)
            root("rms0")
            act.wait_ge(mod_ready, 1)
            for k in range(NK):
                act.wait_ge(hx, k + 1)
                act.activation(hT[:, k], hT[:, k], ACT.Identity, scale=pre[:, k:k + 1],
                               bias=mod[:, k:k + 1]).then_inc(h_ready, 1)
            for a in range(2):
                acc_copy(ACC["iq"] + a, iqT[:, a])
            acc_copy(ACC["ik"], ikT)
            acc_copy(ACC["lr"], lrT, acc(ACC["lr"])[0:RANK, :])
            acc_copy(ACC["iw"], iw.rearrange("p t h -> p (t h)"), acc(ACC["iw"])[:, 0:NT * HI], (HI * DI) ** -0.5)
            for a in range(3 * NB):
                name, i = ("u", "q", "k")[a // NB], a % NB
                n = ACC[name] + i
                if name == "u":
                    acc_copy(n, uP[:, i], acc(n)[:, :].rearrange("p (m j) -> p j m", j=L))
                else:
                    acc_copy(n, (q_sb if name == "q" else k_sb)[:, i])
                for d in (2 * a, 2 * a + 1):
                    side_read(act, SIDE["dots"] + d)
                    if d >= 2:
                        act.wait_ge(score_mul, d - 1)
                    w = P * (2 + d // HI)
                    act.activation(relu[:, d % 2, 0:w], side(SIDE["dots"] + d)[:, 0:w], ACT.Relu
                                   ).then_inc(side_out[(SIDE["dots"] + d) % 3], 1)
            act.wait_ge(w2_ready, 1)
            for a in range(NT):
                acc_copy(ACC["v"] + a, v_sb[:, a])
            act.wait_ge(x_kept, 16)
            for b in range(8):
                cc, g = b // 4, 4 * (b % 4)
                side_copy(SIDE["w1"] + b, w1[:, cc, g:g + 4, :].rearrange("p g n -> p (g n)"))
            for d in range(2):
                n = SIDE["lag"] + d
                side_copy(n, lag[:, 256 * d:256 * d + 256], side(n)[:, 0:256])
            for j in range(L):
                n = SIDE["shift"] + j
                side_copy(n, toep[:, :, j, :].rearrange("p (g d) q -> p d g q", d=2),
                          side(n)[:, :].rearrange("p (d g q) -> p d g q", d=2, g=GP))
            act.wait_ge(state_ready, 1)
            for b in range(4):
                side_copy(SIDE["y"] + b, yblk.rearrange("p (g d) m -> p d g m", d=2)[:, b % 2, 8 * (b // 2):8 * (b // 2) + 8],
                          side(SIDE["y"] + b)[:, :].rearrange("p (g m) -> p g m", g=8))
            for name, dst, n in (("gq", gq, 2), ("gk", gk, 2), ("gv", gv, 4)):
                for a in range(n):
                    acc_copy(ACC[name] + a, dst[:, a])
            for a in range(GH):
                acc_read(act, ACC["gr"] + a)
                act.activation(sr[:, a], acc(ACC["gr"] + a)[:, :], ACT.Sigmoid).then_inc(r_sig, 1)
            for a in range(2):
                n = SIDE["z"] + a
                side_read(act, n)
                act.activation(e1[:, a], side(n)[:, :], ACT.Abs, bias=vT[:, V_GB + a:V_GB + a + 1]).then_inc(f_abs, 1)
            act.wait_ge(f_abs, 2)
            act.activation(e1, e1, ACT.Exp, scale=-1.0).then_inc(f_exp, 1)
            act.wait_ge(f_exp, 1)
            act.activation(e1, e1, ACT.Ln, bias=1.0).then_inc(f_exp, 1)
            for a in range(NB):
                act.wait_ge(yd_ready, a + 1)
                act.activation(yback[:, a], yback[:, a], ACT.Gelu_apprx_tanh).then_inc(g_ready, 1)
            for a in range(NB):
                n = ACC["glu"] + 2 * a + 1
                acc_read(act, n)
                if a >= 2:
                    acc_copied(act, n - 5)
                act.activation(msig[:, a % 2], acc(n)[:, :], ACT.Sigmoid).then_inc(acc_out[n % 4], 1)
            acc_copied(act, ACC["glu"] + 6)
            act.wait_ge(f_cum, 2)
            act.activation(e1, cum, ACT.Exp, scale=1.0 / TAU).then_inc(g_dec, 1)
            act.activation(e2, cum, ACT.Exp, scale=-1.0 / TAU).then_inc(g_dec, 1)
            act.wait_ge(f_tail, 1)
            act.activation(e3, tail, ACT.Exp, scale=1.0 / TAU).then_inc(g_dec, 1)
            for i in range(NT * HA + 1):
                if i < NT * HA:
                    tt, h = i // HA, i % HA
                    w = P * (tt + 1)
                    side_copied(act, s_use(i))
                    if i >= 2:
                        side_read(act, pt_use(i - 2))
                    act.activation(prob[:, i % 2, 0:w], logit[:, i % 2, 0:w], ACT.Exp, scale=-1.0,
                                   bias=amax[:, tt, h:h + 1], accum_out=asum[:, tt, h:h + 1]).then_inc(p_ready, 1)
                if i >= 1:
                    n, w = pt_use(i - 1), P * ((i - 1) // HA + 1)
                    side_copy(n, probT[:, (i - 1) % 2, 0:w], side(n)[:, 0:w])
            for tt in range(NT):
                n = SIDE["ya"] + tt
                side_copy(n, ys[:, 0, :, P * tt:P * tt + P], side(n)[:, :].rearrange("p (a q) -> p a q", a=NB))
            for a in range(2):
                n = SIDE["kt"] + a
                side_copy(n, ktok[:, :, P * a:P * a + P], side(n)[:, :].rearrange("p (t d) -> p t d", t=NT))
            for b in range(4):
                n = SIDE["o"] + b
                side_read(act, n)
                st.do(act.activation(o_part(b), side(n)[:, :].rearrange("p (t h e) -> p t h e", t=2, h=2), ACT.Copy))
                if b:
                    act.wait_ge(o_sum, b)
                act.activation(osq, side(n)[:, :], ACT.Square).then_inc(side_out[n % 3], 1)
            act.wait_ge(o_sum, NT + 1)
            act.activation(stat[:, 16:32], stat[:, 16:32], ACT.Sqrt).then_inc(o_root, 1)
            def top(s, per=0, it=0, kt=NK):
                act.wait_ge(slab_in[s % RING], it * (16 * per // RING) + 16 * (s // RING + 1))
                if split_no(s) >= 2:
                    act.wait_ge(slab_used, it * per + (s - 1))
                act.activation(w_hi[:, split_no(s) % 2, 0:kt * SW], ring[:, s % RING, 0:kt * SW], ACT.Copy
                               ).then_inc(w_top, 1)

            top(SLAB["merge"])
            top(SLAB["merge"] + 1, kt=NB)
            with act.Fori(0, 2) as it:
                for step in range(6):
                    for q in range(2):
                        n = ACC["merge"] + 4 * step + q
                        act.wait_ge(acc_done, it * 24 + (n + 1))
                        act.wait_ge(acc_out[(n - 2) % 4], it * 6 + ((n - 2) // 4 + 1))
                        act.activation(msig[:, q], acc(n)[:, :], ACT.Sigmoid).then_inc(acc_out[n % 4], 1)
                    s = SLAB["merge"] + 2 * step + 2
                    top(s, 12, it)
                    top(s + 1, 12, it, NB)
            act.wait_ge(slab_in[(s + 1) % RING], 16 * ((SLAB["out"] + 1) // RING + 1))
            act.activation(w_hi[:, 1, NB * SW:], ring[:, (s + 1) % RING, NB * SW:], ACT.Copy).then_inc(half_top, 1)
            for k in range(NK):
                n = ACC["out"] + k
                acc_read(act, n)
                st.do(act.activation(yT[:, k], acc(n)[:, :], ACT.Copy))
                if k < 2:
                    acc_copied(act, ACC["merge"] + 46 + k)
                squares(k, acc(n)[:, :], 1, acc_out[n % 4])
                if k % 2 and k < NK - 1:
                    top(SLAB["out"] + 2 + k // 2)
            root("rms1")
            for k in range(NK):
                act.wait_ge(x1_ready, k + 1)
                if k < 2:
                    slow_read(act, SLOW["rms1"])
                squares(k, x1[:, k], 2, sq_ready)
            root("rms2")
            act.wait_ge(fmod_ready, 1)
            for k in range(NK):
                act.wait_ge(hx, NK + k + 1)
                for dst in (h_hi, hT):
                    act.activation(dst[:, k], hT[:, k], ACT.Identity, scale=fpre[:, k:k + 1],
                                   bias=fmod[:, k:k + 1]).then_inc(h2_top, 1)

            top(SLAB["up"] + 1)
            act.sem_inc(gelu_out, 2)

            def up_pair(it, pair, s):
                act.wait_ge(taps, it * 3 + (pair + 1))
                slab = SLAB["up"] + 2 * pair + 2
                for r in range(4):
                    n = ACC["up"] + 4 * pair + r
                    act.wait_ge(acc_done, it * 12 + (n + 1))
                    act.wait_ge(gelu_out if r < 2 else ff_ready, it * 6 + (2 * pair + r % 2 + 1))
                    act.activation(cb[:, r], acc(n)[:, :], ACT.Identity, scale=cs[:, s, 2, r:r + 1],
                                   bias=cs[:, s, 3, r:r + 1]).then_inc(conv_0, 1)
                    if r == 1:
                        top(slab, 6, it)
                        for q in range(2):
                            n = ACC["up"] + 4 * pair + q
                            act.wait_ge(acc_out[n % 4], it * 3 + (n // 4 + 1))
                            act.wait_ge(ff_ready, it * 6 + (2 * pair + q + 1))
                            act.activation(gl[:, q], cb[:, q], ACT.Gelu_apprx_tanh).then_inc(gelu_out, 1)
                top(slab + 1, 6, it)

            def ff_top_part(j):
                act.wait_ge(ff_ready, 2 + 2 * j + 2)
                act.activation(ff_hi[:, j % 2], arena[:, 2 * T * j:2 * T * j + 2 * T], ACT.Copy).then_inc(ff_top, 1)

            with act.Fori(0, 3) as it:
                for s in range(3):
                    up_pair(it, s, s)
            up_pair(0, 9, 0)
            for j in range(2):
                ff_top_part(j)
            up_pair(0, 10, 1)
            for j in range(2, NF // 2):
                top(SLAB["down"] + j)
                ff_top_part(j)
            for i, m in enumerate(DOWN_ORDER):
                if m < 4:
                    acc_read(act, ACC["down"] + m)
                    signal = acc_out[(ACC["down"] + m) % 4]
                elif m < 7:
                    side_read(act, SIDE["down"] + m - 4)
                    signal = side_out[(SIDE["down"] + m - 4) % 3]
                else:
                    slow_read(act, SLOW["down"])
                    signal = slow_out
                st.do(act.activation(yT[:, m], down_bank(m)[:, :], ACT.Copy))
                if i < 2:
                    slow_read(act, SLOW["rms2"])
                squares(i, down_bank(m)[:, :], 3, signal)
            root("rms3")
            for n in range(1, 8, 2):
                acc_copy(ACC["xo"] + n, xo[:, n // 2, BW:D])

        @block.vector
        def _(dve):
            st = Steps(dve, vstep)
            tt_, ts, stt = dve.tensor_tensor, dve.tensor_scalar, dve.scalar_tensor_tensor

            def cmul(out_r, out_i, ar, ai, br, bi, t):
                st.do(tt_(t[0], ar, br, ALU.mult))
                st.do(tt_(t[1], ai, bi, ALU.mult))
                st.do(tt_(t[2], ar, bi, ALU.mult))
                st.do(tt_(t[3], ai, br, ALU.mult))
                st.settle()
                st.do(tt_(out_r, t[0], t[1], ALU.subtract))
                st.do(tt_(out_i, t[2], t[3], ALU.add))

            def inverse_rms(norm, n):
                slow_read(dve, n)
                ts(rb, slow[:, :], EPS, None, ALU.add).then_inc(slow_out, 1)
                dve.wait_ge(rms_root, norm + 1)
                dve.reciprocal(rb, rb).then_inc(rinv, 1)
                dve.wait_ge(rinv, norm + 1)

            S = [sc[:, i, :] for i in range(28)]
            side_copied(dve, SIDE["vec"])
            dve.wait_ge(c_sig, 1)
            tt_(csil[:, :], csil[:, :], vT[:, V_C:V_C + NK], ALU.mult).then_inc(c_silu, 1)
            lr, li = vT[:, V_LR:V_LR + GP], vT[:, V_LI:V_LI + GP]
            dve.wait_ge(dt_exp, 2)
            tt_(S[2], lr, S[1], ALU.mult).then_inc(s5_ang, 1)
            st.do(tt_(S[8], li, S[1], ALU.mult))
            st.do(tt_(S[10], lr, lr, ALU.mult))
            st.do(tt_(S[11], li, li, ALU.mult))
            st.settle()
            ROUND = 1.5 * 2.0 ** 23
            st.do(ts(S[9], S[8], 1.0 / (2.0 * math.pi), None, ALU.mult))
            st.do(tt_(S[10], S[10], S[11], ALU.add))
            st.settle()
            st.do(ts(S[9], S[9], ROUND, None, ALU.add))
            st.do(dve.reciprocal(S[11], S[10]))
            st.settle()
            st.do(ts(S[9], S[9], -ROUND, None, ALU.add))
            st.settle()
            for part in (6.28125, 0.001934051513671875, 1.2556659314782e-06):
                st.do(stt(S[8], S[9], -part, S[8], ALU.mult, ALU.add))
                st.settle()
            st.do(ts(S[3], S[8], 3.1415925, -3.1415925, ALU.min, ALU.max))
            st.settle()
            st.do(ts(S[7], S[3], -1.0, None, ALU.mult))
            st.settle()
            st.do(tt_(S[7], S[7], S[3], ALU.max))
            st.settle()
            ts(S[7], S[7], -1.0, math.pi / 2, ALU.mult, ALU.add).then_inc(s5_ang, 1)
            dve.wait_ge(s5_trig, 3)
            apr, api = (apw[:, cc] for cc in range(2))
            st.do(dve.memset(apr[:, :, 0:1], 1.0))
            st.do(dve.memset(api[:, :, 0:1], 0.0))
            col = [s.unsqueeze(2) for s in S]
            st.do(tt_(apr[:, :, 1:2], col[4], col[6], ALU.mult))
            st.do(tt_(api[:, :, 1:2], col[4], col[5], ALU.mult))
            st.do(dve.memset(ph[:, 0, :, 0:1], 1.0))
            st.do(dve.memset(ph[:, 1, :, 0:1], 0.0))
            st.settle()
            for m in (1, 2, 4):
                t = [a_tmp[:, 64 * i:64 * i + GP * m].rearrange("p (g m) -> p g m", g=GP) for i in range(4)]
                a = [p[:, :, 1:m + 1] for p in (apr, api)]
                b = [p[:, :, m:m + 1].broadcast_to([P, GP, m]) for p in (apr, api)]
                cmul(apr[:, :, m + 1:2 * m + 1], api[:, :, m + 1:2 * m + 1], *a, *b, t)
                st.settle()
            st.do(ts(S[12], apr[:, :, 1], -1.0, None, ALU.add))
            st.settle()
            st.do(tt_(S[13], S[12], lr, ALU.mult))
            st.do(tt_(S[14], api[:, :, 1], li, ALU.mult))
            st.do(tt_(S[15], api[:, :, 1], lr, ALU.mult))
            st.do(tt_(S[16], S[12], li, ALU.mult))
            st.settle()
            st.do(tt_(S[13], S[13], S[14], ALU.add))
            st.do(tt_(S[15], S[15], S[16], ALU.subtract))
            st.settle()
            st.do(tt_(S[13], S[13], S[11], ALU.mult))
            tt_(S[15], S[15], S[11], ALU.mult).then_inc(s5_pow, 1)
            st.settle()
            dve.wait_ge(s5_pow, 1)
            dve.wait_ge(b_in, 32)
            f = [col[13].broadcast_to([P, GP, SP_]), col[15].broadcast_to([P, GP, SP_])]
            t = [a_tmp[:, 256 * i:256 * i + 256].rearrange("p (g q) -> p g q", g=GP) for i in range(4)]
            cmul(bb[:, 0], bb[:, 1], *f, brow[:, 0], brow[:, 1], t)
            st.settle()
            inverse_rms(0, SLOW["rms0"])
            for k in range(NK):
                tt_(hT[:, k], xT[:, k], rb, ALU.mult).then_inc(hx, 1)
            dve.wait_ge(x_in, 16)
            acc_copied(dve, ACC["x"] + NK - 1)
            for i in range(L):
                t = [a_tmp[:, 1024 * (i % 2) + 256 * n:1024 * (i % 2) + 256 * n + 256].rearrange(
                    "p (g q) -> p g q", g=GP) for n in range(4)]
                a = [p[:, :, L - 1 - i:L - i].broadcast_to([P, GP, SP_]) for p in (apr, api)]
                cmul(w1T[:, 0, :, i, :], w1T[:, 1, :, i, :], *a, bb[:, 0], bb[:, 1], t)
            side_read(dve, SIDE["mod"])
            tt_(mod[:, 0:16], side(SIDE["mod"])[:, 0:16], vT[:, V_MB:V_MB + 16], ALU.add
                ).then_inc(side_out[SIDE["mod"] % 3], 1)
            side_copied(dve, SIDE["mod"])
            stt(pre[:, :], mod[:, 8:16], 1.0, vT[:, V_PRE:V_PRE + NK], ALU.add, ALU.mult).then_inc(mod_ready, 1)
            mag, pc, ps = S[17], S[18], S[19]
            st.do(tt_(mag, S[4], S[4], ALU.mult))
            src = (S[6], S[5])
            for n in range(3):
                st.do(tt_(S[20], src[0], src[0], ALU.mult))
                st.do(tt_(S[21], src[1], src[1], ALU.mult))
                st.do(tt_(S[22], src[0], src[1], ALU.mult))
                st.settle()
                st.do(tt_(pc, S[20], S[21], ALU.subtract))
                st.do(ts(ps, S[22], 2.0, None, ALU.mult))
                if n < 2:
                    st.do(tt_(mag, mag, mag, ALU.mult))
                st.settle()
                src = (pc, ps)
            st.do(dve.tensor_copy(rho, mag.unsqueeze(2).broadcast_to([P, GP, NM])))
            for m in (1, 2, 4, 8, 16, 32):
                t = [a_tmp[:, 512 * i:512 * i + GP * m].rearrange("p (g m) -> p g m", g=GP) for i in range(4)]
                a = [ph[:, cc, :, 0:m] for cc in range(2)]
                b = [s.unsqueeze(2).broadcast_to([P, GP, m]) for s in (pc, ps)]
                cmul(ph[:, 0, :, m:2 * m], ph[:, 1, :, m:2 * m], *a, *b, t)
                if m < 32:
                    st.do(tt_(S[20], pc, pc, ALU.mult))
                    st.do(tt_(S[21], ps, ps, ALU.mult))
                    st.do(tt_(S[22], pc, ps, ALU.mult))
                    st.settle()
                    st.do(tt_(pc, S[20], S[21], ALU.subtract))
                    st.do(ts(ps, S[22], 2.0, None, ALU.mult))
                st.settle()
            dve.memset(rho[:, :, 0:1], 0.0).then_inc(s5_tables, 1)
            acc_copied(dve, ACC["iw"])
            for d in range(HI * (NT - 1)):
                tt, h = 1 + d // HI, d % HI
                w = P * (tt + 1)
                side_copied(dve, SIDE["dots"] + d)
                if h == 0:
                    ts(mb[:, tt, 0:w], relu[:, d % 2, 0:w], iw[:, tt, h:h + 1], None, ALU.mult).then_inc(score_mul, 1)
                else:
                    dve.wait_ge(score_mul, d)
                    stt(mb[:, tt, 0:w], relu[:, d % 2, 0:w], iw[:, tt, h:h + 1], mb[:, tt, 0:w],
                        ALU.mult, ALU.add).then_inc(score_mul, 1)
            for tt in range(1, NT):
                w = P * (tt + 1)
                dve.wait_ge(score_masked, tt)
                src = mb[:, tt, 0:w]
                for r in range(TOPK // 8):
                    st.do(dve.max(out=stat[:, 0:8], in_=src))
                    st.settle()
                    st.do(dve.match_replace(out=work[:, 0:w], in_to_replace=stat[:, 0:8], in_values=src,
                                            imm_value=TAKEN))
                    st.settle()
                    src = work[:, 0:w]
                st.do(tt_(work[:, 0:w], work[:, 0:w], mb[:, tt, 0:w], ALU.not_equal))
                st.settle()
                ts(mb[:, tt, 0:w], work[:, 0:w], -1.0, BIG, ALU.add, ALU.mult).then_inc(mask_ready, 1)
            side_read(dve, SIDE["lag"] + 1)
            for hf in range(2):
                nr, ni = SIDE["state"] + 2 * hf, SIDE["state"] + 2 * hf + 1
                g = slice(8 * hf, 8 * hf + 8)
                vr, vi = (side(n)[:, :].rearrange("p (g m) -> p g m", g=8) for n in (nr, ni))
                t = [a_tmp[:, 512 * i:512 * i + 512].rearrange("p (g m) -> p g m", g=8) for i in range(4)]
                side_read(dve, ni)
                st.do(tt_(t[0], vr, ph[:, 0, g], ALU.mult))
                st.do(tt_(t[1], vi, ph[:, 1, g], ALU.mult))
                tt_(t[2], vr, ph[:, 1, g], ALU.mult).then_inc(side_out[nr % 3], 1)
                tt_(t[3], vi, ph[:, 0, g], ALU.mult).then_inc(side_out[ni % 3], 1)
                st.settle()
                side_copied(dve, nr)
                side_copied(dve, ni)
                st.do(tt_(zst[:, 0, g], t[0], t[1], ALU.add))
                st.do(tt_(zst[:, 1, g], t[3], t[2], ALU.subtract))
                st.settle()
            for cc in range(2):
                z = zst[:, cc].rearrange("p g m -> p (g m)")
                st.do(dve.tensor_tensor_scan(z, rho.rearrange("p g m -> p (g m)"), z, 0.0, ALU.mult, ALU.add))
            st.settle()
            for hf in range(2):
                g = slice(8 * hf, 8 * hf + 8)
                t = [a_tmp[:, 512 * i:512 * i + 512].rearrange("p (g m) -> p g m", g=8) for i in range(4)]
                cmul(xst[:, 0, g, 1:], xst[:, 1, g, 1:], zst[:, 0, g], zst[:, 1, g], ph[:, 0, g], ph[:, 1, g], t)
                st.settle()
            dve.memset(xst[:, :, :, 0:1], 0.0).then_inc(state_ready, 1)
            side_read(dve, SIDE["modg"])
            tt_(mod[:, 16:24], side(SIDE["modg"])[:, 0:8], vT[:, V_MB + 16:V_MB + 24], ALU.add
                ).then_inc(side_out[SIDE["modg"] % 3], 1)
            side_copied(dve, SIDE["modg"])
            tt_(post[:, :], mod[:, 16:24], vT[:, V_POST:V_POST + NK], ALU.mult).then_inc(post_ready, 1)
            for a in range(GH):
                n = ACC["gr"] + a
                dve.wait_ge(r_sig, a + 1)
                tt_(sr[:, a], sr[:, a], acc(n)[:, :], ALU.mult).then_inc(acc_out[n % 4], 1)
            for a in range(2):
                n = SIDE["z"] + a
                side_read(dve, n)
                dve.wait_ge(f_abs, a + 1)
                ts(cum[:, a], side(n)[:, :], vT[:, V_GB + a:V_GB + a + 1], 0.0, ALU.add, ALU.min
                   ).then_inc(side_out[n % 3], 1)
            side_copied(dve, SIDE["z"])
            side_copied(dve, SIDE["z"] + 1)
            dve.wait_ge(f_exp, 2)
            st.do(tt_(cum, cum, e1, ALU.subtract))
            st.settle()
            dve.wait_ge(g_zero, 3)
            for a in range(2):
                dve.tensor_tensor_scan(cum[:, a], keep, cum[:, a], 0.0, ALU.mult, ALU.add).then_inc(f_cum, 1)
            dve.wait_ge(f_cum, 2)
            cc = cum.rearrange("p a t -> p (a t)").rearrange("p (c t) -> p c t", t=GC)
            tt_(tail.rearrange("p a t -> p (a t)").rearrange("p (c t) -> p c t", t=GC),
                cc[:, :, GC - 1:GC].broadcast_to([P, 2 * NC, GC]), cc, ALU.subtract).then_inc(f_tail, 1)
            dve.wait_ge(y_in, 16)
            for a in range(NB):
                stt(yback[:, a], tiles(a_u, NB)[:, a], vT[:, V_SD + a:V_SD + a + 1], yback[:, a],
                    ALU.mult, ALU.add).then_inc(yd_ready, 1)
            for a in range(NB):
                n = ACC["glu"] + 2 * a
                acc_copied(dve, n + 1)
                tt_(ys[:, 1, a].rearrange("p (m j) -> p j m", j=L),
                    acc(n)[:, :].rearrange("p (j m) -> p j m", j=L),
                    msig[:, a % 2].rearrange("p (j m) -> p j m", j=L), ALU.mult).then_inc(acc_out[n % 4], 1)
            dve.wait_ge(g_dec, 3)
            for a in range(2):
                acc_copied(dve, ACC["gq"] + a)
                acc_copied(dve, ACC["gk"] + a)
            stt(gq, gq, GDK ** -0.5, e1, ALU.mult, ALU.mult).then_inc(g_k, 1)
            tt_(e2, gk, e2, ALU.mult).then_inc(g_k, 1)
            tt_(e3, gk, e3, ALU.mult).then_inc(g_k, 1)
            dve.wait_ge(mask0_ready, 1)
            dve.wait_ge(mask_ready, NT - 1)
            for i in range(NT * HA + 2):
                if i >= 2 and (i - 2) % HA == HA - 1:
                    tt = (i - 2) // HA
                    dve.wait_ge(p_ready, HA * (tt + 1))
                    st.do(dve.reciprocal(asum[:, tt], asum[:, tt]))
                    st.settle()
                    slow_read(dve, SLOW["pv"] + tt)
                    tt_(ytok[:, tt].rearrange("p (h d) -> p h d", h=HA), slow[:, :].rearrange("p (h d) -> p h d", h=HA),
                        asum[:, tt].unsqueeze(2).broadcast_to([P, HA, DH]), ALU.mult).then_inc(slow_out, 1)
                if i >= NT * HA:
                    continue
                tt, h = i // HA, i % HA
                w, n = P * (tt + 1), s_use(i)
                side_read(dve, n)
                if i >= 2:
                    dve.wait_ge(p_ready, i - 1)
                dve.tensor_tensor_reduce(logit[:, i % 2, 0:w], side(n)[:, 0:w], mb[:, tt, 0:w], -(DH ** -0.5), 3.0e38,
                                         ALU.add, ALU.min, amax[:, tt, h:h + 1]).then_inc(side_out[n % 3], 1)
            for pr in range(2):
                side_read(dve, SIDE["kv"] + 2 * pr + 1)
                for ch in range(NC - 1):
                    n, cl = SIDE["kv"] + 2 * pr + ch % 2, ch // 2
                    ins = stt(sprev[:, pr, ch + 1, :], sprev[:, pr, ch, :],
                              e1[:, pr, GC * ch + GC - 1:GC * ch + GC], side(n)[:, GDV * cl:GDV * cl + GDV],
                              ALU.mult, ALU.add)
                    if ch >= NC - 3:
                        ins.then_inc(side_out[n % 3], 1)
                        side_copied(dve, n)
                    else:
                        st.do(ins)
                        st.settle()
            for h in range(GH):
                n = SIDE["gatt"] + h
                side_read(dve, n)
                dve.copy_predicated(gatt[:, h], chunkmask[:, :].bitcast(U32).unsqueeze(1).broadcast_to([P, NT, P]),
                                    side(n)[:, :].rearrange("p (t q) -> p t q", t=NT)).then_inc(side_out[n % 3], 1)
            for b in range(4):
                side_copied(dve, SIDE["o"] + b)
                dve.tensor_reduce(stat[:, 16 + 4 * b:20 + 4 * b], osq.rearrange("p (h e) -> p h e", h=GH),
                                  AX.X, ALU.add).then_inc(o_sum, 1)
            dve.wait_ge(o_sum, NT)
            ts(stat[:, 16:32], stat[:, 16:32], 1.0 / GDV, EPS, ALU.mult, ALU.add).then_inc(o_sum, 1)
            dve.wait_ge(o_root, 1)
            dve.reciprocal(stat[:, 16:32], stat[:, 16:32]).then_inc(o_inv, 1)
            dve.wait_ge(o_inv, 1)
            for b in range(4):
                for i in range(2):
                    v, col = o_part(b)[:, i], 16 + 4 * b + 2 * i
                    tt_(v, v, stat[:, col:col + 2].unsqueeze(2).broadcast_to([P, 2, GDV]), ALU.mult).then_inc(o_norm, 1)
            def rest(s, per=0, it=0, kt=NK):
                dve.wait_ge(w_top, it * per + (split_no(s) + 1))
                tt_(w_lo[:, s % RING, 0:kt * SW], ring[:, s % RING, 0:kt * SW],
                    w_hi[:, split_no(s) % 2, 0:kt * SW].bitcast(F32), ALU.subtract).then_inc(w_ready, 1)

            dve.sem_inc(gemv_k, NK)
            slow_read(dve, SLOW["pv"] + NT - 1)
            for h in range(GH):
                n = SIDE["ot"] + h
                side_read(dve, n)
                stt(ys[:, 2, h], side(n)[:, :], vT[:, V_GN + h:V_GN + h + 1], sr[:, h], ALU.mult, ALU.mult
                    ).then_inc(side_out[n % 3], 1)
            rest(SLAB["merge"])
            rest(SLAB["merge"] + 1, kt=NB)
            for h in range(GH):
                side_copied(dve, SIDE["ot"] + h)
                dve.tensor_copy(ys_hi2[:, h], ys[:, 2, h]).then_inc(y2_top, 1)
            for h in range(GH):
                dve.wait_ge(y2_top, h + 1)
                tt_(ys_lo[:, 2, h], ys[:, 2, h], ys_hi2[:, h].bitcast(F32), ALU.subtract).then_inc(y2_ready, 1)

            def modulate(part, slab, count, it=0, per=0):
                for k in range(NK):
                    if k == 0:
                        ts(part, slab[:, 0, :], csil[:, 0:1], None, ALU.mult).then_inc(gemv_k, 1)
                    else:
                        dve.wait_ge(gemv_k, it * per + (count + k))
                        stt(part, slab[:, k, :], csil[:, k:k + 1], part, ALU.mult, ALU.add).then_inc(gemv_k, 1)

            with dve.Fori(0, 2) as it:
                for step in range(6):
                    jj, i = step // NBR, step % NBR
                    dve.wait_ge(fmod_in, it * 96 + 16 * (step + 1))
                    n = SIDE["fmod"] + step
                    dve.wait_ge(side_out[(n - 2) % 3], it * 2 + ((n - 2) // 3 + 1))
                    modulate(gemv[:, step % 2], fmod_slab, NK * (step + 1), it, 6 * NK)
                    for q in range(2):
                        n = ACC["merge"] + 4 * step + q
                        m = merged[:, bass.ds(it * 4 + (2 * jj + q), 1), :].squeeze(1)
                        dve.wait_ge(acc_done, it * 24 + (n + 3))
                        dve.wait_ge(acc_out[n % 4], it * 6 + (n // 4 + 1))
                        dst = m if i == 0 else mtmp
                        tt_(dst, acc(n + 2)[:, :], msig[:, q], ALU.mult).then_inc(acc_out[(n + 2) % 4], 1)
                        dve.wait_ge(acc_out[(n + 2) % 4], it * 6 + ((n + 2) // 4 + 1))
                        if i:
                            tt_(m, m, mtmp, ALU.add).then_inc(merge_sum, 1)
                            dve.wait_ge(merge_sum, it * 8 + (4 * jj + 2 * (i - 1) + q + 1))
                        if i == 2:
                            hi, lo = (x[:, bass.ds(it * 4 + (2 * jj + q), 1), :].squeeze(1) for x in (m_hi, m_lo))
                            dve.tensor_copy(hi, m).then_inc(m_split, 1)
                            dve.wait_ge(m_split, it * 8 + (4 * jj + 2 * q + 1))
                            tt_(lo, m, hi.bitcast(F32), ALU.subtract).then_inc(m_split, 1)
                        s = SLAB["merge"] + 2 * step + 2 + q
                        rest(s, 12, it, NB if q else NK)
                    n = SIDE["fmod"] + step
                    dve.wait_ge(side_done, it * 6 + (n + 1))
                    stt(fmod[:, bass.ds(it * 12 + 2 * step, 2)], side(n)[:, 0:2], float(D),
                        vT[:, bass.ds(it * 12 + (V_FMB + 2 * step), 2)], ALU.mult, ALU.add).then_inc(side_out[n % 3], 1)
            dve.wait_ge(half_top, 1)
            s = SLAB["out"] + 1
            tt_(w_lo[:, s % RING, NB * SW:], ring[:, s % RING, NB * SW:], w_hi[:, 1, NB * SW:].bitcast(F32), ALU.subtract
                ).then_inc(half_ready, 1)
            for s in range(SLAB["out"] + 2, SLAB["out"] + 4):
                rest(s)
            for step in range(9, 12):
                side_copied(dve, SIDE["fmod"] + step)
            st.do(tt_(fpost[:, :], fmod[:, 16:24], vT[:, V_FPOST:V_FPOST + NK], ALU.mult))
            stt(fpre[:, :], fmod[:, 8:16], 1.0, vT[:, V_FPRE:V_FPRE + NK], ALU.add, ALU.mult).then_inc(fmod_ready, 1)
            def residual(factor, signal):
                for k in range(NK):
                    st.do(tt_(yT[:, k], yT[:, k], rb, ALU.mult))
                for k in range(NK):
                    dve.wait_ge(vstep, st.n - NK + k + 1)
                    stt(x1[:, k], yT[:, k], factor[:, k:k + 1], x1[:, k], ALU.mult, ALU.add).then_inc(signal, 1)

            inverse_rms(1, SLOW["rms1"])
            dve.wait_ge(x_back, 16)
            residual(post, x1_ready)
            rest(SLAB["up"])
            dve.wait_ge(x1_ready, NK)
            inverse_rms(2, SLOW["rms2"])
            for k in range(NK):
                tt_(hT[:, k], x1[:, k], rb, ALU.mult).then_inc(hx, 1)
            for k in range(NK):
                dve.wait_ge(h2_top, 2 * k + 2)
                tt_(h_lo[:, k], hT[:, k], h_hi[:, k].bitcast(F32), ALU.subtract).then_inc(h2_ready, 1)
            rest(SLAB["up"] + 1)

            dve.sem_inc(ff_ready, 2)

            def up_pair(it, pair, s):
                for r in range(4):
                    n, j = ACC["up"] + 4 * pair + r, 4 * pair + r
                    dve.wait_ge(conv_0, it * 12 + (j + 1))
                    stt(cb[:, r, 1:], acc(n)[:, 0:T - 1], cs[:, s, 1, r:r + 1], cb[:, r, 1:], ALU.mult, ALU.add
                        ).then_inc(conv_1, 1)
                    dve.wait_ge(conv_1, it * 12 + (j + 1))
                    stt(cb[:, r, 2:], acc(n)[:, 0:T - 2], cs[:, s, 0, r:r + 1], cb[:, r, 2:], ALU.mult, ALU.add
                        ).then_inc(acc_out[n % 4], 1)
                    if r == 1:
                        rest(SLAB["up"] + 2 * pair + 2, 6, it)
                for q in range(2):
                    n = ACC["up"] + 4 * pair + 2 + q
                    dve.wait_ge(acc_out[n % 4], it * 3 + (n // 4 + 1))
                    dve.wait_ge(gelu_out, it * 6 + (2 * pair + q + 3))
                    dst = ff[:, bass.ds(it * 6 + (2 * pair + q), 1), :].squeeze(1) if pair < 9 else ff[:, 2 * pair + q]
                    tt_(dst, gl[:, q], cb[:, 2 + q], ALU.mult).then_inc(ff_ready, 1)
                rest(SLAB["up"] + 2 * pair + 3, 6, it)

            def ff_rest(j):
                dve.wait_ge(ff_top, j + 1)
                tt_(ff_lo[:, j % 2], arena[:, 2 * T * j:2 * T * j + 2 * T], ff_hi[:, j % 2].bitcast(F32), ALU.subtract
                    ).then_inc(ff_split, 1)

            with dve.Fori(0, 3) as it:
                for s in range(3):
                    up_pair(it, s, s)
            up_pair(0, 9, 0)
            for j in range(2):
                ff_rest(j)
            up_pair(0, 10, 1)
            for j in range(2, NF // 2):
                rest(SLAB["down"] + j)
                ff_rest(j)
            inverse_rms(3, SLOW["rms3"])
            residual(fpost, x2_ready)
            for n in range(0, 8, 2):
                acc_read(dve, ACC["xo"] + n)
                dve.tensor_copy(xo[:, n // 2, 0:BW], acc(ACC["xo"] + n)[:, :]).then_inc(acc_out[(ACC["xo"] + n) % 4], 1)

        @block.tensor
        def _(pe):
            def mm(dst, w, moving, start, stop, signal=None, **kw):
                ins = pe.matmul(dst, w, moving, start=start, stop=stop, **kw)
                if signal is not None:
                    ins.then_inc(signal, 1)

            def take(s):
                pe.wait_ge(slab_in[s % RING], 16 * (s // RING + 1))

            def acc_free(n):
                if n >= 4:
                    acc_copied(pe, n - 4)

            def side_free(n):
                if n >= 3:
                    side_copied(pe, n - 3)

            def channel_tile(n, s, q, moving, kt=NK, cols=SW):
                acc_free(n)
                for k in range(kt):
                    mm(acc(n)[:, :], slab_k(s, cols)[:, k, P * q:P * q + P], moving[:, k], k == 0, k == kt - 1,
                       slab_used if k == 0 and q == 0 else acc_done if k == kt - 1 else None)

            def split_tile(n, s, q, moving, kt=NK, used=True, dst=None):
                for k in range(kt):
                    for i, (wp, mp) in enumerate(PARTS):
                        w = (w_hi[:, split_no(s) % 2], w_lo[:, s % RING])[wp].rearrange("p (k n) -> p k n", n=SW)
                        first, last = k == i == 0, k == kt - 1 and i == 2
                        mm(acc(n)[:, :], w[:, k, P * q:P * q + P], moving[mp][:, k], first, last,
                           acc_done if last else slab_used if first and q == 0 else None)

            def project(name, a):
                s = SLAB[name] + a // 2
                if a % 2 == 0:
                    take(s)
                channel_tile(ACC[name] + a, s, a % 2, hT)

            def token_tiles(name):
                for half in range(2):
                    s = SLAB[name] + half
                    take(s)
                    for tt in range(NT):
                        n = ACC[name] + tt
                        if half == 0:
                            acc_free(n)
                        for k in range(4):
                            mm(acc(n)[:, :], hT[:, 4 * half + k, P * tt:P * tt + P], slab_k(s, BW)[:, k, :],
                               half == k == 0, half == 1 and k == 3,
                               slab_used if tt == k == 0 else acc_done if half == 1 and k == 3 else None)

            def modulate(name, slabs, use):
                side_free(use)
                for j in range(slabs):
                    take(SLAB[name] + j)
                    for q in range(2):
                        for k in range(NK):
                            last = j == slabs - 1 and q == 1 and k == NK - 1
                            mm(side(use)[:, 2 * j + q:2 * j + q + 1], slab_k(SLAB[name] + j)[:, k, P * q:P * q + P],
                               csil[:, k:k + 1], k == 0, k == NK - 1,
                               side_done if last else slab_used if q == k == 0 and SLAB[name] + j else None)

            def sum_squares(k, name):
                mm(slow[:, :], mean[:, :], sq[:, k % 2], k == 0, k == NK - 1,
                   slow_done if k == NK - 1 else sq_used)

            def dots(d):
                n, tt, h = SIDE["dots"] + d, 1 + d // HI, d % HI
                part, w = slice(DI * (h % 4), DI * (h % 4) + DI), P * (tt + 1)
                side_free(n)
                mm(side(n)[:, 0:w], iqT[part, h // 4, P * tt:P * tt + P], ikT[part, 0:w], True, True, side_done)

            pe.wait_ge(consts, 4)
            pe.wait_ge(vec_in, 16 * 15)
            n = SIDE["vec"]
            pe.transpose(side(n)[:, 0:V_CW], vrow[0:V_CW, 0, :], ident[0:V_CW, 0:V_CW])
            pe.transpose(side(n)[:, V_CW:V_CW + P], vrow[:, 1, :], ident[:, :])
            pe.transpose(side(n)[:, V_CW + P:V_N], vrow[0:V_N - V_CW - P, 2, :],
                         ident[0:V_N - V_CW - P, 0:V_N - V_CW - P]).then_inc(side_done, 1)
            pe.wait_ge(c_in, 64)
            for cc in range(2):
                n = SIDE["ctr"] + cc
                for r in range(4):
                    ins = pe.transpose(side(n)[:, P * r:P * r + P],
                                       crow[:, cc, r].rearrange("p d n -> p (d n)"), ident[:, :])
                ins.then_inc(side_done, 1)
            pe.wait_ge(x_in, 16)
            for k in range(NK + 1):
                if k < NK:
                    n = ACC["x"] + k
                    acc_free(n)
                    for tt in range(NT):
                        ins = pe.transpose(acc(n)[:, P * tt:P * tt + P], xtok[:, tt, P * k:P * k + P], ident[:, :])
                    ins.then_inc(acc_done, 1)
                if k:
                    acc_copied(pe, ACC["x"] + k - 1)
                    sum_squares(k - 1, "rms0")
            pe.wait_ge(c_silu, 1)
            modulate("mod", 8, SIDE["mod"])
            pe.wait_ge(h_ready, NK)
            project("iq", 0)
            project("iq", 1)
            pe.wait_ge(small_in, 16 * 7)
            for name, c0, w in (("ik", 0, P), ("lr", 4 * DI + HI, RANK)):
                n = ACC[name]
                acc_free(n)
                for k in range(NK):
                    mm(acc(n)[0:w, :], wsmall[:, k, c0:c0 + w], hT[:, k], k == 0, k == NK - 1,
                       acc_done if k == NK - 1 else None)
            n = ACC["iw"]
            acc_free(n)
            for tt in range(NT):
                for k in range(NK):
                    mm(acc(n)[:, HI * tt:HI * tt + HI], hT[:, k, P * tt:P * tt + P],
                       wsmall[:, k, 4 * DI:4 * DI + HI], k == 0, k == NK - 1,
                       acc_done if tt == NT - 1 and k == NK - 1 else None)
            for a in range(3 * NB):
                project(("u", "q", "k")[a // NB], a % NB)
                if a == 0:
                    acc_copied(pe, ACC["iq"] + 1)
                    acc_copied(pe, ACC["ik"])
                dots(2 * a)
                dots(2 * a + 1)
            token_tiles("v")
            pe.wait_ge(s5_tables, 1)
            for b in range(8):
                n, cc = SIDE["w1"] + b, b // 4
                side_free(n)
                for i in range(4):
                    ins = pe.transpose(side(n)[:, P * i:P * i + P],
                                       w1T[:, cc, 4 * (b % 4) + i].rearrange("p i q -> p (i q)"), ident[:, :])
                ins.then_inc(side_done, 1)
            for d in range(2):
                n, part = SIDE["lag"] + d, slice(SN * d, SN * d + SN)
                side_free(n)
                for g in range(GP):
                    for cc in range(2):
                        mm(side(n)[:, SP_ * g:SP_ * g + SP_], w1T[part, cc, g].rearrange("p i q -> p (i q)"),
                           cT[part, 2 * cc, g], cc == 0, cc == 1, side_done if g == GP - 1 and cc else None)
            for d in range(2):
                side_copied(pe, SIDE["lag"] + d)
            for j in range(L):
                n, c0 = SIDE["shift"] + j, SP_ * (L - 1 - j)
                side_free(n)
                mm(side(n)[:, :], wide[:, c0:c0 + P], lag, True, True, side_done)
            pe.wait_ge(ub_in, 16 * L)
            for hf in range(2):
                for cc in range(2):
                    n = SIDE["state"] + 2 * hf + cc
                    side_free(n)
                    for g in range(16 * hf, 16 * hf + 16):
                        part = slice(SN * (g % 2), SN * (g % 2) + SN)
                        col = NM * (g // 2 % 8)
                        mm(side(n)[part, col:col + NM], w1[:, cc, g // 2, part], ub[:, g], True, True,
                           side_done if g == 16 * hf + 15 else None)
            modulate("modg", 4, SIDE["modg"])
            project("gq", 0)
            project("gq", 1)
            project("gk", 0)
            project("gk", 1)
            pe.wait_ge(state_ready, 1)
            for b in range(4):
                n = SIDE["y"] + b
                side_free(n)
                part = slice(SN * (b % 2), SN * (b % 2) + SN)
                for i in range(8):
                    g = 2 * (8 * (b // 2) + i) + b % 2
                    dst = side(n)[:, NM * i:NM * i + NM]
                    mm(dst, toep[:, g].rearrange("p j q -> p (j q)"), ub[:, g], True, False)
                    for cc in range(2):
                        mm(dst, w2[cc][part, g // 2].rearrange("p j q -> p (j q)"), xst[part, cc, g // 2, 0:NM],
                           False, cc == 1, side_done if cc and i == 7 else None)
            token_tiles("gv")
            for a in range(GH):
                project("gr", a)
            for a in range(2):
                n = SIDE["z"] + a
                side_free(n)
                mm(side(n)[:, :], wgate[:, P * a:P * a + P], lrT, True, True, side_done)
            for half in range(2):
                take(SLAB["glu"] + half)
            pe.wait_ge(g_ready, NB)
            for a in range(NB):
                for half in range(2):
                    n, s = ACC["glu"] + 2 * a + half, SLAB["glu"] + half
                    acc_free(n)
                    for k in range(NB):
                        mm(acc(n)[:, :], slab_k(s, BW)[:, k, P * a:P * a + P], yback[:, k], k == 0, k == NB - 1,
                           acc_done if k == NB - 1 else slab_used if k == 0 and a == 0 and half == 0
                           else slab_used if k == 0 and a == NB - 1 and half == 1 else None)
            for i in range(NT * HA + 2):
                if i < NT * HA:
                    n, tt, h = s_use(i), i // HA, i % HA
                    part, w = slice(DH * (h % 2), DH * (h % 2) + DH), P * (tt + 1)
                    side_free(n)
                    mm(side(n)[:, 0:w], q_sb[part, h // 2, P * tt:P * tt + P], k_sb[part, h // 2, 0:w], True, True,
                       side_done)
                if 1 <= i <= NT * HA:
                    n = pt_use(i - 1)
                    side_free(n)
                    pe.wait_ge(p_ready, i)
                    for j in range((i - 1) // HA + 1):
                        ins = pe.transpose(side(n)[:, P * j:P * j + P], prob[:, (i - 1) % 2, P * j:P * j + P],
                                           ident[:, :])
                    ins.then_inc(side_done, 1)
                if i >= 2:
                    tt, h = (i - 2) // HA, (i - 2) % HA
                    if h == 0:
                        slow_copied(pe, SLOW["pv"] + tt - 1)
                    side_copied(pe, pt_use(i - 2))
                    for j in range(tt + 1):
                        mm(slow[:, DH * h:DH * h + DH], probT[:, i % 2, P * j:P * j + P],
                           v_sb[:, j, DH * h:DH * h + DH], j == 0, j == tt,
                           slow_done if h == HA - 1 and j == tt else None)
            for tt in range(NT):
                n = SIDE["ya"] + tt
                side_free(n)
                slow_copied(pe, SLOW["pv"] + tt)
                for a in range(NB):
                    ins = pe.transpose(side(n)[:, P * a:P * a + P], ytok[:, tt, P * a:P * a + P], ident[:, :])
                ins.then_inc(side_done, 1)
            pe.wait_ge(g_k, 3)
            for a in range(2):
                n = SIDE["kt"] + a
                side_free(n)
                for tt in range(NT):
                    ins = pe.transpose(side(n)[:, P * tt:P * tt + P], e3[:, a, P * tt:P * tt + P], ident[:, :])
                ins.then_inc(side_done, 1)
            for pr in range(2):
                side_copied(pe, SIDE["kt"] + pr)
                for hf in range(2):
                    n, rws = SIDE["kv"] + 2 * pr + hf, slice(GC * hf, GC * hf + GC)
                    side_free(n)
                    for cl in range(4 - hf):
                        ch = 2 * cl + hf
                        for d in range(2):
                            part = slice(GDK * d, GDK * d + GDK)
                            mm(side(n)[part, GDV * cl:GDV * cl + GDV],
                               ktok[rws, ch // 2, P * pr + GDK * d:P * pr + GDK * d + GDK],
                               gv[rws, ch // 2, GDV * (2 * pr + d):GDV * (2 * pr + d) + GDV], True, True,
                               side_done if cl == 3 - hf and d else None)
            for h in range(GH):
                n, part = SIDE["gatt"] + h, slice(GDK * (h % 2), GDK * (h % 2) + GDK)
                side_free(n)
                for tt in range(NT):
                    tok = slice(P * tt, P * tt + P)
                    mm(side(n)[:, tok], e2[part, h // 2, tok], gq[part, h // 2, tok], True, True,
                       side_done if tt == NT - 1 else None)
            for h in range(GH):
                side_copied(pe, SIDE["gatt"] + h)
            for b in range(4):
                n, part = SIDE["o"] + b, slice(GDK * (b % 2), GDK * (b % 2) + GDK)
                side_free(n)
                for i in range(4):
                    tt, h = 2 * (b // 2) + i // 2, b % 2 + 2 * (i % 2)
                    col = slice(GDV * i, GDV * i + GDV)
                    mm(side(n)[:, col], gatt[:, h, tt, :], gv[:, tt, GDV * h:GDV * h + GDV], True, False,
                       skip_group_check=True)
                    for hf in range(2):
                        ch = 2 * tt + hf
                        if ch:
                            mm(side(n)[GC * hf:GC * hf + GC, col], gq[part, h // 2, GC * ch:GC * ch + GC],
                               sprev[part, h // 2, ch, :], False, True,
                               side_done if i == 3 and hf else None, skip_group_check=True)
            pe.wait_ge(o_norm, 8)
            for h in range(GH):
                n = SIDE["ot"] + h
                side_free(n)
                for tt in range(NT):
                    ins = pe.transpose(side(n)[:, P * tt:P * tt + P], og[:, tt, GDV * h:GDV * h + GDV], ident[:, :])
                ins.then_inc(side_done, 1)
            for n in range(SIDE["ya"], SIDE["ya"] + NT):
                side_copied(pe, n)
            for n in range(SIDE["ot"], SIDE["ot"] + GH):
                side_copied(pe, n)
            acc_copied(pe, ACC["glu"] + 6)
            pe.wait_ge(h_split, 3)
            pe.wait_ge(y2_ready, GH)
            with pe.Fori(0, 2) as it:
                for step in range(6):
                    i, s = step % NBR, SLAB["merge"] + 2 * step
                    for m, moving, kt in ((0, (h_hi, h_lo), NK), (1, (ys_hi[i], ys_lo[:, i]), NB)):
                        pe.wait_ge(w_ready, it * 12 + (split_no(s) + m + 1))
                        for q in range(2):
                            n = ACC["merge"] + 4 * step + 2 * m + q
                            pe.wait_ge(acc_out[n % 4], it * 6 + n // 4)
                            split_tile(n, s + m, q, moving, kt)
                    n = SIDE["fmod"] + step
                    pe.wait_ge(gemv_k, it * (6 * NK) + NK * (step + 2))
                    pe.wait_ge(side_out[n % 3], it * 2 + n // 3)
                    for q in range(2):
                        mm(side(n)[:, q:q + 1], gemv[:, step % 2, P * q:P * q + P], mean[:, 0:1], True, True,
                           side_done if q else None)
            pe.wait_ge(m_split, 2 * NK)
            for k in range(NK + 1):
                if k < NK:
                    s = SLAB["out"] + k // 2
                    if k % 2 == 0:
                        pe.wait_ge(w_ready, split_no(s) + 1)
                    if k == 2:
                        pe.wait_ge(half_ready, 1)
                    acc_free(ACC["out"] + k)
                    split_tile(ACC["out"] + k, s, k % 2, (m_hi, m_lo))
                if k:
                    acc_copied(pe, ACC["out"] + k - 1)
                    sum_squares(k - 1, "rms1")
            for k in range(NK):
                pe.wait_ge(sq_ready, k + 1)
                if k == 0:
                    slow_copied(pe, SLOW["rms1"])
                sum_squares(k, "rms2")
            pe.wait_ge(h2_ready, NK)

            def up_pair(it, pair):
                for r in range(4):
                    n, s = ACC["up"] + 4 * pair + r, SLAB["up"] + 2 * pair + r // 2
                    if r % 2 == 0:
                        pe.wait_ge(w_ready, it * 6 + (split_no(s) + 1))
                    pe.wait_ge(acc_out[n % 4], it * 3 + n // 4)
                    split_tile(n, s, r % 2, (h_hi, h_lo))

            with pe.Fori(0, 3) as it:
                for pair in range(3):
                    up_pair(it, pair)
            for pair in range(9, 11):
                up_pair(0, pair)
            for m in range(4):
                acc_free(ACC["down"] + m)
            for m in range(3):
                side_free(SIDE["down"] + m)
            slow_copied(pe, SLOW["rms2"])
            for j in range(NF // 2):
                s = SLAB["down"] + j
                pe.wait_ge(w_ready, split_no(s) + 1)
                pe.wait_ge(ff_split, j + 1)
                for kk in range(2):
                    tok = slice(T * kk, T * kk + T)
                    for m in range(NK):
                        col = slice(D * kk + P * m, D * kk + P * m + P)
                        done = acc_done if m < 4 else side_done if m < 7 else slow_done
                        for i, (wp, mp) in enumerate(PARTS):
                            w, f = (w_hi[:, split_no(s) % 2], w_lo[:, s % RING])[wp], (ff_hi, ff_lo)[mp][:, j % 2]
                            last = j == NF // 2 - 1 and kk == 1 and i == 2
                            mm(down_bank(m)[:, :], w[:, col], f[:, tok], j == kk == i == 0, last,
                               done if last else slab_used if kk == m == i == 0 else None)
            for i, m in enumerate(DOWN_ORDER):
                if m < 4:
                    acc_copied(pe, ACC["down"] + m)
                elif m < 7:
                    side_copied(pe, SIDE["down"] + m - 4)
                else:
                    slow_copied(pe, SLOW["down"])
                sum_squares(i, "rms3")
            pe.wait_ge(x2_ready, NK)
            for n in range(8):
                acc_free(ACC["xo"] + n)
                for i in range(4):
                    k = 4 * (n % 2) + i
                    ins = pe.transpose(acc(ACC["xo"] + n)[:, P * i:P * i + P], x1[:, k, P * (n // 2):P * (n // 2) + P],
                                       ident[:, :])
                ins.then_inc(acc_done, 1)


_INS = ['x', 'c', 'mix_mod_w', 'mix_mod_b', 'mix_pre_g', 'mix_post_g', 'w_in', 's5_lam_re', 's5_lam_im', 's5_log_dt', 's5_b_re', 's5_b_im', 's5_c_re', 's5_c_im', 's5_d', 's5_w_glu', 'gla_w_gate', 'gla_b_gate', 'gla_norm_g', 'w_branch', 'w_out', 'ffn_mod_w', 'ffn_mod_b', 'ffn_pre_g', 'ffn_post_g', 'ffn_w_up', 'ffn_conv_w', 'ffn_conv_b', 'ffn_w_down']
_OUTS = [((1, T, D), 'float32')]


def kernel(**inputs):
    import numpy as _np
    import concourse.bacc as _bacc
    from concourse import mybir as _mybir
    from concourse.bass_utils import run_bass_kernel_spmd as _run

    nc = _bacc.Bacc("TRN2", target_bir_lowering=False, num_devices=1)
    arrays, args = {}, []
    for name in _INS:
        a = _np.ascontiguousarray(inputs[name])
        arrays[f"in_{name}_dram"] = a
        args.append(nc.dram_tensor(f"in_{name}_dram", a.shape, _mybir.dt.from_np(a.dtype), kind="ExternalInput").ap())
    for i, (shape, dtype) in enumerate(_OUTS):
        dt = _mybir.dt.from_np(_np.dtype(dtype))
        args.append(nc.dram_tensor(f"out_{i}_dram", shape, dt, kind="ExternalOutput").ap())
    trunk_kernel(nc, *args)
    r = _run(nc, [arrays], core_ids=[0])
    return r.results[0]["out_0_dram"]
```

```python
from contextlib import ExitStack
import math

import concourse.bass as bass
from concourse import mybir

F32 = mybir.dt.float32
F32R = mybir.dt.float32r
U32 = mybir.dt.uint32
ALU = mybir.AluOpType
ACT = mybir.ActivationFunctionType
AX = mybir.AxisListType

P = 128
T = 512
D = 1024
NT = T // P
NK = D // P
HA, DH = 8, 64
HI, DI = 8, 32
TOPK = min(256, T // 4)
BW = 512
NB = BW // P
NBR = 3
SG, SP_, SN = 32, 16, 64
GP = SG // 2
L = P // SP_
NM = T // L
GH, GDK, GDV, GC = 4, 64, 128, 64
NC = T // GC
RANK = 16
TAU = 16.0
FF = 2816
NF = FF // P
EPS = 1e-6
BIG = 1.0e30
TAKEN = -3.4e38
NEVER = -3.3e38

C_AQ, C_AK, C_AV, C_IQ, C_IK, C_IW = 0, 512, 1024, 1536, 1792, 1824
C_U, C_GQ, C_GK, C_GV, C_GR, C_LR, C_GL = 1832, 2344, 2600, 2856, 3368, 3880, 3896

V_MB, V_PRE, V_POST, V_C, V_SD, V_GB, V_GN, V_FMB, V_FPRE, V_FPOST = 0, 24, 32, 40, 48, 52, 54, 58, 82, 90
V_CW, V_CB, V_LR, V_LI, V_N = 98, 230, 274, 290, 306

RING = 3
SW = 256


def count_up(parts):
    at, n = {}, 0
    for name, uses in parts:
        at[name] = n
        n += uses
    return at


SLAB = count_up([("mod", 8), ("iq", 1), ("u", 2), ("q", 2), ("k", 2), ("v", 2), ("gq", 1), ("gk", 1),
                 ("gv", 2), ("gr", 2), ("glu", 2), ("merge", 24), ("out", 4), ("up", 22), ("down", 11), ("end", 0)])
PARTS = ((0, 0), (0, 1), (1, 0))
ACC = count_up([("x", NK), ("iq", 2), ("ik", 1), ("lr", 1), ("iw", 1), ("u", 4), ("q", 4), ("k", 4), ("v", 4),
                ("gq", 2), ("gk", 2), ("gv", 4), ("gr", 4), ("glu", 8), ("kt", 2), ("gatt", 4), ("kv", 4), ("o", 4), ("ot", 4), ("merge", 48), ("out", 8), ("up", 44),
                ("down", 4), ("xo", 8)])
SIDE = count_up([("vec", 1), ("mod", 1), ("ctr", 2), ("dots", 24), ("w1", 8), ("lag", 2), ("shift", 8), ("state", 4),
                 ("y", 4), ("z", 2), ("att", 64), ("ya", 4), ("fmod", 12), ("modg", 1), ("down", 3)])
SLOW = count_up([("rms0", 1), ("pv", 4), ("rms1", 1), ("rms2", 1), ("down", 1), ("rms3", 1)])


def s_use(i):
    return SIDE["att"] + max(2 * i - 1, 0)


def pt_use(i):
    return SIDE["att"] + min(2 * i + 2, 2 * NT * HA - 1)


PE_GLA = {3: ("kt", 0), 4: ("kt", 1), 6: ("gatt", 0), 7: ("gatt", 1), 8: ("gatt", 2), 9: ("gatt", 3), 11: ("kv", 0),
          12: ("kv", 1), 20: ("o", 0), 21: ("o", 1), 22: ("o", 2), 23: ("o", 3), 28: ("ot", 0), 29: ("ot", 1),
          30: ("ot", 2), 31: ("ot", 3)}
ACT_GLA = {0: ("decay", 0), 4: ("kt", 0), 5: ("kt", 1), 21: ("o", 0), 22: ("o", 1), 23: ("o", 2), 24: ("o", 3),
           25: ("root", 0)}
DVE_GLA = {1: ("decay", 0), 8: ("gatt", 0), 9: ("gatt", 1), 10: ("gatt", 2), 11: ("gatt", 3), 12: ("kv", 0),
           13: ("kv", 1), 14: ("kv", 2), 15: ("kv", 3), 16: ("kv", 4), 17: ("kv", 5), 18: ("kv", 6), 21: ("sum", 0),
           22: ("sum", 1), 23: ("sum", 2), 24: ("sum", 3), 25: ("inverse", 0), 26: ("norm", 0), 27: ("norm", 1),
           29: ("out", 0), 30: ("out", 1), 31: ("out", 2), 32: ("out", 3)}


DOWN_ORDER = (7, 0, 1, 2, 3, 4, 5, 6)


class Steps:

    def __init__(self, eng, sem):
        self.eng, self.sem, self.n = eng, sem, 0

    def do(self, ins):
        ins.then_inc(self.sem, 1)
        self.n += 1

    def settle(self):
        self.eng.wait_ge(self.sem, self.n)


def trunk_kernel(nc, x, c, mix_mod_w, mix_mod_b, mix_pre_g, mix_post_g, w_in, s5_lam_re, s5_lam_im, s5_log_dt,
                 s5_b_re, s5_b_im, s5_c_re, s5_c_im, s5_d, s5_w_glu, gla_w_gate, gla_b_gate, gla_norm_g, w_branch,
                 w_out, ffn_mod_w, ffn_mod_b, ffn_pre_g, ffn_post_g, ffn_w_up, ffn_conv_w, ffn_conv_b, ffn_w_down,
                 out):
    ctx = ExitStack()
    with ctx:
        def sb(name, shape, dt=F32):
            return ctx.enter_context(nc.sbuf_tensor(name, shape, dt))

        def sem(name):
            return ctx.enter_context(nc.semaphore(name))

        def sems(name, n):
            return [sem(f"{name}{i}") for i in range(n)]

        with ExitStack() as early:
            def region(stack, name, shape, dt=F32):
                return stack.enter_context(nc.sbuf_tensor(name, shape, dt))

            ring = region(early, "ring", [P, RING, NK * SW])
            ys = region(early, "ys", [P, NBR, NB, T])
            hT = region(early, "hT", [P, NK, T])
            arena = region(early, "arena", [P, 12288])
            a_w1t = region(early, "a_w1t", [P, 4352])[:, :]
            a_ph = region(early, "a_ph", [P, 2048])[:, :]
            a_tmp = region(early, "a_tmp", [P, 2048])[:, :]
            a_s5 = region(early, "a_s5", [P, 2560])[:, :]
            a_k = region(early, "a_k", [P, 2048])[:, :]
            a_v = region(early, "a_v", [P, 2048])[:, :]
            mb = region(early, "mb", [P, NT, T])
            a_idx = region(early, "a_idx", [P, 2048])[:, :]
        w_lo = sb("w_lo", [P, RING, NK * SW], F32R)
        ys_lo = sb("ys_lo", [P, NBR, NB, T], F32R)
        h_lo = sb("h_lo", [P, NK, T], F32R)
        m_lo = sb("m_lo", [P, NK, T], F32R)
        m_hi = sb("m_hi", [P, NK, T], F32R)
        fmod_slab = sb("fmod_slab", [P, NK, SW])
        ys_hi0 = sb("ys_hi0", [P, NB, T], F32R)
        sb("x_again", [P, 4352])
        w_hi = sb("w_hi", [P, 2, NK * SW], F32R)
        ff_hi = sb("ff_hi", [P, 2, 2 * T], F32R)
        sb("a_s5_rest", [P, 512])
        ys_hi1 = sb("ys_hi1", [P, NB, T], F32R)
        ys_hi2 = sb("ys_hi2", [P, NB, T], F32R)
        h_hi = sb("h_hi", [P, NK, T], F32R)
        ys_hi = (ys_hi0, ys_hi1, ys_hi2)
        ff_lo = ys_lo[:, 2].rearrange("p (s a) t -> p s (a t)", s=2)
        a_w1, a_w2, a_u, a_ub, a_q = (arena[:, 0:4096], arena[:, 4096:6144], arena[:, 6144:8192],
                                      arena[:, 8192:10240], arena[:, 10240:12288])
        vT = sb("vT", [P, V_N])
        ident = sb("ident", [P, P])
        wide = sb("wide", [P, (L - 1) * SP_ + P])
        mean = sb("mean", [P, P])
        chunkmask = sb("chunkmask", [P, P])
        csil = sb("csil", [P, NK])
        mod = sb("mod", [P, 24])
        fmod = sb("fmod", [P, 24])
        pre = sb("pre", [P, NK])
        post = sb("post", [P, NK])
        fpre = sb("fpre", [P, NK])
        fpost = sb("fpost", [P, NK])
        a_wk = sb("a_wk", [P, 1536])[:, :]
        stat = sb("stat", [P, 64])
        amax = sb("amax", [P, NT, HA])
        asum = sb("asum", [P, NT, HA])
        cs = sb("cs", [P, 3, 4, 4])
        iw = sb("iw", [P, NT, HI])
        wgate = sb("wgate", [RANK, GH * GDK])
        cT = sb("cT", [P, 3, GP, SP_])
        apw = sb("apw", [P, 2, GP, L + 1])
        sc = sb("sc", [P, 28, GP])
        gemv = sb("gemv", [P, 2, SW])

        bank = [ctx.enter_context(nc.psum_tensor(f"bank{i}", [P, 512], F32)) for i in range(8)]
        x_keep = nc.dram_tensor("x_keep", (P, NK, T), F32).ap()
        u_dram = nc.dram_tensor("u_dram", (SG, SP_, L, NM), F32).ap()
        y_dram = nc.dram_tensor("y_dram", (SG, SP_, L, NM), F32).ap()

        def tiles(region, n):
            return region.rearrange("p (a t) -> p a t", a=n)

        q_sb, k_sb, v_sb = tiles(a_q, NB), tiles(a_k, NB), tiles(a_v, NT)
        vrow = a_k[:, 0:3 * P].rearrange("p (a b) -> p a b", a=3)
        wsmall = a_k[:, 512:512 + NK * 152].rearrange("p (k n) -> p k n", k=NK)
        xtok = a_w1t[:, 0:4096].rearrange("p (a d) -> p a d", a=NT)
        xT = tiles(a_w1, NK)
        sq = tiles(a_wk[:, 0:1024], 2)
        rb = a_wk[:, 1024:1536]
        iqT, ikT, lrT = tiles(a_idx[:, 0:1024], 2), a_idx[:, 1024:1536], a_idx[0:RANK, 1536:2048]
        relu, work = tiles(a_wk[:, 0:1024], 2), a_wk[:, 1024:1536]
        uP = a_u.rearrange("p (a j m) -> p a j m", a=NB, j=L)
        ub = a_ub.rearrange("p (g m) -> p g m", g=SG)
        w1T = a_w1t[:, 0:4096].rearrange("p (c g i q) -> p c g i q", c=2, g=GP, i=L)
        zst = a_w1t[:, 0:2048].rearrange("p (c g m) -> p c g m", c=2, g=GP)
        xst = a_w1t[:, 2048:2048 + 2 * GP * (NM + 1)].rearrange("p (c g m) -> p c g m", c=2, g=GP)
        w1 = a_w1.rearrange("p (c g n) -> p c g n", c=2, g=GP)
        w2 = [ys[:, 2].rearrange("p a t -> p (a t)").rearrange("p (g j q) -> p g j q", g=GP, j=L),
              a_w2.rearrange("p (g j q) -> p g j q", g=GP, j=L)]
        toep = ys[:, 0:2].rearrange("p b a t -> p (b a t)").rearrange("p (g j q) -> p g j q", g=SG, j=L)
        ph = a_ph.rearrange("p (c g m) -> p c g m", c=2, g=GP)
        yblk = a_tmp.rearrange("p (g m) -> p g m", g=SG)
        yback = tiles(a_ph, NB)
        rho = a_s5[:, 0:1024].rearrange("p (g m) -> p g m", g=GP)
        brow = a_s5[:, 1024:1536].rearrange("p (c g q) -> p c g q", c=2, g=GP)
        bb = a_s5[:, 1536:2048].rearrange("p (c g q) -> p c g q", c=2, g=GP)
        lag = a_s5[:, 2048:2560]
        crow = a_q[:, 0:1024].rearrange("p (c r d n) -> p c r d n", c=2, r=4, d=2)
        gq, gk, cum, e1 = (tiles(a_w1[:, 1024 * i:1024 * i + 1024], 2) for i in range(4))
        e2, e3 = (tiles(a_w1t[:, 1024 * i:1024 * i + 1024], 2) for i in range(2))
        ktok = a_w1t[:, 2048:3072].rearrange("p (a d) -> p a d", a=NT)
        tail = tiles(a_w1t[:, 3072:4096], 2)
        gv, sr, og = tiles(a_ub, NT), tiles(a_w2, GH), tiles(a_u, NT)
        sprev = ys[:, 2].rearrange("p a t -> p (a t)").rearrange("p (a c e) -> p a c e", a=2, c=NC)
        gatt = a_tmp.rearrange("p (h t q) -> p h t q", h=GH, t=NT)
        keep, osq = a_s5[:, 0:512], a_s5[:, 512:1024]
        logit, prob = tiles(a_idx[:, 0:1024], 2), tiles(a_wk[:, 0:1024], 2)
        probT = tiles(a_s5[:, 1536:2560], 2)
        ytok = tiles(a_ph, NT)
        merged, x1 = tiles(a_w1, NK), a_w1t[:, 0:4096].rearrange("p (k t) -> p k t", k=NK)
        modg_slab = a_v.rearrange("p (k n) -> p k n", k=NK)
        msig, mtmp = tiles(a_wk[:, 0:1024], 2), a_wk[:, 1024:1536]
        yT = ys[:, 0:2].rearrange("p b a t -> p (b a) t")
        ff = tiles(arena[:, 0:NF * T], NF)
        cb, gl = tiles(a_k, 4), tiles(a_v[:, 0:1024], 2)
        xo = arena[:, 0:NT * D].rearrange("p (t d) -> p t d", t=NT)
        slab_in = sems("slab_in", RING)
        slab_used = sem("slab_used")
        w_top, w_ready = sem("w_top"), sem("w_ready")
        half_top, half_ready = sem("half_top"), sem("half_ready")
        h_top, h_split = sem("h_top"), sem("h_split")
        y_top, y_split = sem("y_top"), sem("y_split")
        m_split = sem("m_split")
        h2_top, h2_ready = sem("h2_top"), sem("h2_ready")
        ff_top, ff_split = sem("ff_top"), sem("ff_split")
        fmod_in, modg_in = sem("fmod_in"), sems("modg_in", 2)
        fmod_used = sem("fmod_used")
        mod_k, gemv_k = sem("mod_k"), sem("gemv_k")
        acc_done = sem("acc_done")
        acc_out = sems("acc_out", 4)
        side_done = sem("side_done")
        side_out = sems("side_out", 3)
        slow_done = sem("slow_done")
        slow_out = sem("slow_out")
        vstep, astep, gstep = sem("vstep"), sem("astep"), sem("gstep")
        x_in, vec_in, c_in, b_in, dt_in, small_in = (sem(n) for n in (
            "x_in", "vec_in", "c_in", "b_in", "dt_in", "small_in"))
        x_kept, x_back, u_store, ub_in, y_store, y_in, out_st = (sem(n) for n in (
            "x_kept", "x_back", "u_store", "ub_in", "y_store", "y_in", "out_st"))
        consts = sem("consts")
        sq_used = sem("sq_used")
        rms_root, rinv = sem("rms_root"), sem("rinv")
        y_copied = sem("y_copied")
        sq_ready = sem("sq_ready")
        c_sig, c_silu = sem("c_sig"), sem("c_silu")
        mod_ready = sem("mod_ready")
        hx, h_ready = sem("hx"), sem("h_ready")
        dt_exp, s5_ang, s5_trig, s5_pow = sem("dt_exp"), sem("s5_ang"), sem("s5_trig"), sem("s5_pow")
        s5_tables, w2_ready = sem("s5_tables"), sem("w2_ready")
        score_mul = sem("score_mul")
        score_masked = sem("score_masked")
        mask0_ready, mask_ready = sem("mask0_ready"), sem("mask_ready")
        state_ready = sem("state_ready")
        yd_ready, g_ready = sem("yd_ready"), sem("g_ready")
        p_ready = sem("p_ready")
        r_sig = sem("r_sig")
        f_abs, f_exp, f_cum, f_tail = sem("f_abs"), sem("f_exp"), sem("f_cum"), sem("f_tail")
        g_zero, g_dec, g_k = sem("g_zero"), sem("g_dec"), sem("g_k")
        carried = sem("carried")
        o_sum, o_root, o_inv, o_norm = sem("o_sum"), sem("o_root"), sem("o_inv"), sem("o_norm")
        merge_sum = sem("merge_sum")
        fmod_ready = sem("fmod_ready")
        x1_ready, x2_ready = sem("x1_ready"), sem("x2_ready")
        taps = sem("taps")
        conv_0, conv_1, gelu_out, ff_ready = sem("conv_0"), sem("conv_1"), sem("gelu_out"), sem("ff_ready")

        def acc(n):
            return bank[n % 4]

        def side(n):
            return bank[4 + n % 3]

        slow = bank[7]

        def acc_read(eng, n):
            eng.wait_ge(acc_done, n + 1)

        def acc_copied(eng, n):
            eng.wait_ge(acc_out[n % 4], n // 4 + 1)

        def side_read(eng, n):
            eng.wait_ge(side_done, n + 1)

        def side_copied(eng, n):
            eng.wait_ge(side_out[n % 3], n // 3 + 1)

        def slow_read(eng, n):
            eng.wait_ge(slow_done, n + 1)

        def slow_copied(eng, n):
            eng.wait_ge(slow_out, n + 1)

        def down_bank(m):
            if m < 4:
                return acc(ACC["down"] + m)
            return side(SIDE["down"] + m - 4) if m < 7 else slow

        def slab_k(s, cols=SW):
            return ring[:, s % RING, :].rearrange("p (k n) -> p k n", n=cols)

        def rows(w):
            return w.rearrange("(k p) n -> p k n", p=P)

        def split_no(s):
            return s - SLAB["merge"]

        block = ctx.enter_context(nc.Block())

        def o_part(b):
            return og[:, 2 * (b // 2):2 * (b // 2) + 2, :].rearrange("p t (h d e) -> p t d h e", h=2, d=2)[:, :, b % 2]

        @block.sync
        def _(sp):
            def load(s, view, src):
                if s >= RING:
                    sp.wait_ge(slab_used, s - RING + 1)
                sp.dma_start(view, src).then_inc(slab_in[s % RING], 16)

            def slabs(name, w, col, n):
                for j in range(n):
                    load(SLAB[name] + j, slab_k(SLAB[name] + j), rows(w[:, col + SW * j:col + SW * j + SW]))

            def half_slabs(name, w, col):
                for j in range(2):
                    load(SLAB[name] + j, slab_k(SLAB[name] + j, BW), rows(w[BW * j:BW * j + BW, col:col + BW]))

            win = w_in[0]
            slabs("mod", mix_mod_w[0], 0, 8)
            slabs("iq", win, C_IQ, 1)
            slabs("u", win, C_U, 2)
            slabs("q", win, C_AQ, 2)
            slabs("k", win, C_AK, 2)
            half_slabs("v", win, C_AV)
            slabs("gq", win, C_GQ, 1)
            slabs("gk", win, C_GK, 1)
            half_slabs("gv", win, C_GV)
            slabs("gr", win, C_GR, 2)
            for j in range(2):
                load(SLAB["glu"] + j, slab_k(SLAB["glu"] + j, BW), rows(s5_w_glu[0][:, BW * j:BW * j + BW]))
            acc_read(sp, ACC["o"] + 3)
            sp.sem_inc(fmod_used, 1)
            with sp.Fori(1, 3) as it:
                for step in range(6):
                    jj, i = step // NBR, step % NBR
                    for m, (w, kt, col) in enumerate(((win, NK, C_GL + D * i), (w_branch[0, i], NB, 0))):
                        s = SLAB["merge"] + 2 * step + m
                        sp.wait_ge(slab_used, it * 12 + (s - RING + 1 - 12))
                        sp.dma_start(slab_k(s)[:, 0:kt, :], rows(w[:, bass.ds(it * (2 * SW) + (col + SW * (jj - 2)), SW)])
                                     ).then_inc(slab_in[s % RING], 16)
                    sp.wait_ge(fmod_used, it * 6 + (step - 5))
                    sp.dma_start(fmod_slab[:, :, :], rows(ffn_mod_w[0][:, bass.ds(it * (6 * SW) + SW * (step - 6), SW)])
                                 ).then_inc(fmod_in, 16)
            slabs("out", w_out[0], 0, 4)
            up = ffn_w_up[0]
            with sp.Fori(0, 3) as it:
                for m in range(6):
                    s, half, pair = SLAB["up"] + m, m % 2, m // 2
                    at = sp.snap(it * (3 * SW) + (FF * half + SW * pair))
                    free = sp.snap(it * 6 + (s - RING + 1))
                    sp.wait_ge(slab_used, free)
                    sp.dma_start(slab_k(s), rows(up[:, bass.ds(at, SW)])).then_inc(slab_in[s % RING], 16)
            for m in range(18, 22):
                s, col = SLAB["up"] + m, FF * (m % 2) + SW * (m // 2)
                load(s, slab_k(s), rows(up[:, col:col + SW]))
            for j in range(NF // 2):
                s = SLAB["down"] + j
                load(s, slab_k(s, D), rows(ffn_w_down[0][2 * P * j:2 * P * j + 2 * P, :]))
            for n in range(8):
                acc_copied(sp, ACC["xo"] + n)
                tok, col = slice(P * (n % NT), P * (n % NT) + P), slice(BW * (n // NT), BW * (n // NT) + BW)
                sp.dma_start(out[0, tok, col], xo[:, n % NT, col]).then_inc(out_st, 16)
            sp.wait_ge(out_st, 16 * 8)

        @block.gpsimd
        def _(pool):
            st = Steps(pool, gstep)
            st.do(pool.memset(ident[:, :], 0.0))
            st.do(pool.memset(wide[:, :], 0.0))
            st.do(pool.memset(chunkmask[:, :], 1.0))
            pool.memset(mean[:, :], 1.0 / D).then_inc(consts, 1)
            st.settle()
            for m, width in ((ident, P), (wide, (L - 1) * SP_ + P)):
                pool.affine_select(out=m[:, :], in_=m[:, :], compare_op=ALU.not_equal, fill=1.0, base=0,
                                   pattern=[[-1, width]], channel_multiplier=1).then_inc(consts, 1)
            st.do(pool.affine_select(out=chunkmask[:, :], in_=chunkmask[:, :], compare_op=ALU.is_ge, fill=0.0,
                                     base=0, pattern=[[1, P]], channel_multiplier=-1))
            st.settle()
            pool.memset(chunkmask[0:GC, GC:P], 0.0).then_inc(consts, 1)
            small = rows(w_in[0])
            for half in range(2):
                for cc, w in enumerate((s5_c_re, s5_c_im)):
                    pool.dma_start(crow[:, cc, :, half, :],
                                   w[0].rearrange("(r g) p n -> (g p) r n", r=4)).then_inc(c_in, 16)
            for cc, w in enumerate((s5_b_re, s5_b_im)):
                pool.dma_start(brow[:, cc, :, :], w[0].rearrange("(g d) n p -> (d n) g p", d=2)).then_inc(b_in, 16)
            for at, col, n in ((4 * DI, C_IW, HI), (4 * DI + HI, C_LR, RANK), *((DI * r, C_IK, DI) for r in range(4))):
                pool.dma_start(wsmall[:, :, at:at + n], small[:, :, col:col + n]).then_inc(small_in, 16)
            pool.dma_start(wgate[:, :], gla_w_gate[0]).then_inc(small_in, 16)
            for k in range(NK - 4, NK):
                acc_copied(pool, ACC["x"] + k)
            pool.dma_start(x_keep, xT).then_inc(x_kept, 16)
            pool.wait_ge(s5_pow, 1)
            side_copied(pool, SIDE["ctr"])
            side_copied(pool, SIDE["ctr"] + 1)
            for j in range(L):
                ar, ai = (apw[:, cc, :, j + 1:j + 2].broadcast_to([P, GP, SP_]) for cc in range(2))
                t = [a_v[:, 1024 * (j % 2) + 256 * i:1024 * (j % 2) + 256 * i + 256].rearrange(
                    "p (g q) -> p g q", g=GP) for i in range(4)]
                st.do(pool.tensor_tensor(t[0], cT[:, 0], ar, ALU.mult))
                st.do(pool.tensor_tensor(t[1], cT[:, 1], ai, ALU.mult))
                st.do(pool.tensor_tensor(t[2], cT[:, 0], ai, ALU.mult))
                st.do(pool.tensor_tensor(t[3], cT[:, 2], ar, ALU.mult))
                st.settle()
                st.do(pool.tensor_tensor(w2[0][:, :, j, :], t[0], t[1], ALU.subtract))
                st.do(pool.tensor_tensor(w2[1][:, :, j, :], t[3], t[2], ALU.subtract))
            pool.memset(mb[:, 0, 0:P], 0.0).then_inc(w2_ready, 1)
            pool.wait_ge(w2_ready, 1)
            pool.affine_select(out=mb[:, 0, 0:P], in_=mb[:, 0, 0:P], compare_op=ALU.is_ge, fill=-BIG, base=0,
                               pattern=[[-1, P]], channel_multiplier=1).then_inc(mask0_ready, 1)
            for a in range(NB):
                acc_copied(pool, ACC["u"] + a)
            pool.dma_start(u_dram.rearrange("(a g) p j m -> (g p) a (j m)", a=NB),
                           a_u.rearrange("p (a t) -> p a t", a=NB)).then_inc(u_store, 16)
            pool.wait_ge(u_store, 16)
            pool.wait_ge(x_kept, 16)
            for j in range(L):
                pool.dma_start(ub[SP_ * j:SP_ * j + SP_, :, :],
                               u_dram[:, :, j, :].rearrange("g p m -> p g m")).then_inc(ub_in, 16)
            for tt in range(1, NT):
                pool.wait_ge(score_mul, HI * tt)
                d = mb[:, tt, P * tt:P * tt + P]
                pool.affine_select(out=d, in_=d, compare_op=ALU.is_ge, fill=NEVER, base=0,
                                   pattern=[[-1, P]], channel_multiplier=1).then_inc(score_masked, 1)
            for b in range(4):
                side_copied(pool, SIDE["y"] + b)
            for j in range(L):
                pool.dma_start(y_dram[:, :, j, :].rearrange("g p m -> p g m"),
                               yblk[SP_ * j:SP_ * j + SP_, :, :]).then_inc(y_store, 16)
            pool.wait_ge(y_store, 16 * L)
            pool.dma_start(yback, y_dram.rearrange("(a g) p j m -> (g p) a (j m)", a=NB)).then_inc(y_in, 16)
            pool.memset(a_tmp, 0.0).then_inc(g_zero, 1)
            pool.memset(sprev[:, :, 0, :], 0.0).then_inc(g_zero, 1)
            st.do(pool.memset(keep, 1.0))
            st.settle()
            pool.memset(keep.rearrange("p (c t) -> p c t", c=NC)[:, :, 0:1], 0.0).then_inc(g_zero, 1)
            acc_copied(pool, ACC["ot"])
            pool.dma_start(x1, x_keep).then_inc(x_back, 16)
            side_copied(pool, s_use(NT * HA - 1))
            slow_read(pool, SLOW["pv"] + NT - 1)
            for i in range(NBR):
                if i == 0:
                    for tt in range(NT):
                        side_copied(pool, SIDE["ya"] + tt)
                if i == 1:
                    acc_copied(pool, ACC["glu"] + 6)
                if i == 2:
                    for h in range(GH):
                        acc_copied(pool, ACC["ot"] + h)
                pool.tensor_copy(ys_hi[i][:, :, :], ys[:, i]).then_inc(y_top, 1)
                pool.wait_ge(y_top, i + 1)
                pool.tensor_tensor(ys_lo[:, i], ys[:, i], ys_hi[i][:, :, :].bitcast(F32), ALU.subtract
                                   ).then_inc(y_split, 1)
            for j in range(4):
                pool.wait_ge(fmod_used, max(13, 12 + j))
                pool.dma_start((fmod_slab[:, :, :], modg_slab)[j % 2], rows(mix_mod_w[0][:, 2 * D + SW * j:2 * D + SW * j + SW])
                               ).then_inc(modg_in[j % 2], 16)
            cols = vT[:, V_CW:V_CW + 8 * NF].rearrange("p (j h n) -> p j h n", j=4, h=2)
            dst = [cs[:, s].rearrange("p j (h n) -> p j h n", h=2) for s in range(3)]
            for s in range(3):
                pool.tensor_copy(dst[s], cols[:, :, :, 2 * s:2 * s + 2]).then_inc(taps, 1)
            with pool.Fori(1, 3) as it:
                for s in range(3):
                    n = ACC["up"] + 4 * s - 9
                    pool.wait_ge(acc_out[n % 4], it * 3 + (n // 4 + 1))
                    pool.tensor_copy(dst[s], cols[:, :, :, bass.ds(it * 6 + 2 * s, 2)]).then_inc(taps, 1)
            for s in range(2):
                acc_copied(pool, ACC["up"] + 4 * (6 + s) + 3)
                pool.tensor_copy(dst[s], cols[:, :, :, 18 + 2 * s:20 + 2 * s]).then_inc(taps, 1)

        @block.scalar
        def _(act):
            st = Steps(act, astep)

            def copy(dst, src, signal, scale=1.0):
                act.activation(dst, src, ACT.Copy, scale=scale).then_inc(signal, 1)

            def acc_copy(n, dst, src=None, scale=1.0):
                acc_read(act, n)
                copy(dst, acc(n)[:, :] if src is None else src, acc_out[n % 4], scale)

            def side_copy(n, dst, src=None, scale=1.0):
                side_read(act, n)
                copy(dst, side(n)[:, :] if src is None else src, side_out[n % 3], scale)

            def squares(k, src, norm, signal):
                if k >= 2:
                    act.wait_ge(sq_used, (NK - 1) * norm + k - 1)
                act.activation(sq[:, k % 2], src, ACT.Square).then_inc(signal, 1)

            def root(name):
                slow_copied(act, SLOW[name])
                act.activation(rb, rb, ACT.Sqrt).then_inc(rms_root, 1)

            at = 0
            for v, n in ((mix_mod_b, 24), (mix_pre_g, 8), (mix_post_g, 8), (c, 8), (s5_d, 4), (gla_b_gate, 2),
                         (gla_norm_g, 4), (ffn_mod_b, 24), (ffn_pre_g, 8), (ffn_post_g, 8)):
                src = v[0] if n != 4 or v.shape[-1] != GDV else v[0].rearrange("a b -> (a b)")
                act.dma_start(vrow[at:at + n, 0, :], src.rearrange("(a b) -> a b", b=P)).then_inc(vec_in, 16)
                at += n
            taps_rows = ffn_conv_w[0].rearrange("j (n b) -> (j n) b", b=P)
            act.dma_start(vrow[:, 1, :], taps_rows[0:P, :]).then_inc(vec_in, 16)
            act.dma_start(vrow[0:4, 2, :], taps_rows[P:P + 4, :]).then_inc(vec_in, 16)
            act.dma_start(vrow[4:48, 2, :], ffn_conv_b[0].rearrange("(n b) -> n b", b=P)).then_inc(vec_in, 16)
            for i, v in enumerate((s5_lam_re, s5_lam_im)):
                act.dma_start(vrow[48 + 16 * i:64 + 16 * i, 2, :],
                              v[0].rearrange("(g d) n -> g (d n)", d=2)).then_inc(vec_in, 16)
            act.dma_start(xtok, x[0].rearrange("(a p) d -> p a d", p=P)).then_inc(x_in, 16)
            log_dt = sc[:, 24:26, :].rearrange("p a g -> p (a g)")
            act.dma_start(log_dt, s5_log_dt[0].partition_broadcast(P)).then_inc(dt_in, 16)

            side_copy(SIDE["vec"], vT[:, :], side(SIDE["vec"])[:, 0:V_N])
            side_copied(act, SIDE["vec"])
            act.activation(csil[:, :], vT[:, V_C:V_C + NK], ACT.Sigmoid).then_inc(c_sig, 1)
            act.wait_ge(dt_in, 16)
            for d in range(2):
                part = slice(SN * d, SN * d + SN)
                act.activation(sc[part, 1, :], log_dt[part].rearrange("p (g d) -> p d g", d=2)[:, d, :], ACT.Exp
                               ).then_inc(dt_exp, 1)
            for k in range(NK):
                n = ACC["x"] + k
                acc_read(act, n)
                st.do(act.activation(xT[:, k], acc(n)[:, :], ACT.Copy))
                squares(k, acc(n)[:, :], 0, acc_out[n % 4])
            root("rms0")
            act.wait_ge(mod_ready, 1)
            for k in range(NK):
                act.wait_ge(hx, k + 1)
                act.activation(hT[:, k], hT[:, k], ACT.Identity, scale=pre[:, k:k + 1],
                               bias=mod[:, k:k + 1]).then_inc(h_ready, 1)
            for cc in range(2):
                n = SIDE["ctr"] + cc
                side_read(act, n)
                for d in range(2):
                    part = slice(SN * d, SN * d + SN)
                    src = side(n)[part, :].rearrange("p (r d q) -> p r d q", d=2, q=SP_)[:, :, d, :]
                    if cc:
                        st.do(act.activation(cT[part, 2], src, ACT.Copy, scale=-1.0))
                    if d:
                        copy(cT[part, cc], src, side_out[n % 3])
                    else:
                        st.do(act.activation(cT[part, cc], src, ACT.Copy))
            act.wait_ge(s5_ang, 1)
            act.activation(sc[:, 4, :], sc[:, 2, :], ACT.Exp).then_inc(s5_trig, 1)
            act.wait_ge(s5_ang, 2)
            act.activation(sc[:, 6, :], sc[:, 7, :], ACT.Sin).then_inc(s5_trig, 1)
            act.activation(sc[:, 5, :], sc[:, 3, :], ACT.Sin).then_inc(s5_trig, 1)
            for a in range(2):
                acc_copy(ACC["iq"] + a, iqT[:, a])
            acc_copy(ACC["ik"], ikT)
            acc_copy(ACC["lr"], lrT, acc(ACC["lr"])[0:RANK, :])
            acc_copy(ACC["iw"], iw.rearrange("p t h -> p (t h)"), acc(ACC["iw"])[:, 0:NT * HI], (HI * DI) ** -0.5)
            for a in range(3 * NB):
                name, i = ("u", "q", "k")[a // NB], a % NB
                n = ACC[name] + i
                if name == "u":
                    acc_copy(n, uP[:, i], acc(n)[:, :].rearrange("p (m j) -> p j m", j=L))
                else:
                    acc_copy(n, (q_sb if name == "q" else k_sb)[:, i])
                for d in (2 * a, 2 * a + 1):
                    side_read(act, SIDE["dots"] + d)
                    if d >= 2:
                        act.wait_ge(score_mul, d - 1)
                    w = P * (2 + d // HI)
                    act.activation(relu[:, d % 2, 0:w], side(SIDE["dots"] + d)[:, 0:w], ACT.Relu
                                   ).then_inc(side_out[(SIDE["dots"] + d) % 3], 1)
            act.wait_ge(w2_ready, 1)
            for a in range(NT):
                acc_copy(ACC["v"] + a, v_sb[:, a])
            act.wait_ge(x_kept, 16)
            for b in range(8):
                cc, g = b // 4, 4 * (b % 4)
                side_copy(SIDE["w1"] + b, w1[:, cc, g:g + 4, :].rearrange("p g n -> p (g n)"))
            for d in range(2):
                n = SIDE["lag"] + d
                side_copy(n, lag[:, 256 * d:256 * d + 256], side(n)[:, 0:256])
            for j in range(L):
                n = SIDE["shift"] + j
                side_copy(n, toep[:, :, j, :].rearrange("p (g d) q -> p d g q", d=2),
                          side(n)[:, :].rearrange("p (d g q) -> p d g q", d=2, g=GP))
            act.wait_ge(state_ready, 1)
            for b in range(4):
                side_copy(SIDE["y"] + b, yblk.rearrange("p (g d) m -> p d g m", d=2)[:, b % 2, 8 * (b // 2):8 * (b // 2) + 8],
                          side(SIDE["y"] + b)[:, :].rearrange("p (g m) -> p g m", g=8))
            for name, dst, n in (("gq", gq, 2), ("gk", gk, 2), ("gv", gv, 4)):
                for a in range(n):
                    acc_copy(ACC[name] + a, dst[:, a])
            for a in range(NB):
                act.wait_ge(yd_ready, a + 1)
                act.activation(yback[:, a], yback[:, a], ACT.Gelu_apprx_tanh).then_inc(g_ready, 1)
            for a in range(GH):
                acc_read(act, ACC["gr"] + a)
                act.activation(sr[:, a], acc(ACC["gr"] + a)[:, :], ACT.Sigmoid).then_inc(r_sig, 1)
            for a in range(2):
                n = SIDE["z"] + a
                side_read(act, n)
                act.activation(e1[:, a], side(n)[:, :], ACT.Abs, bias=vT[:, V_GB + a:V_GB + a + 1]).then_inc(f_abs, 1)
            act.wait_ge(f_abs, 2)
            act.activation(e1, e1, ACT.Exp, scale=-1.0).then_inc(f_exp, 1)
            act.wait_ge(f_exp, 1)
            act.activation(e1, e1, ACT.Ln, bias=1.0).then_inc(f_exp, 1)
            for a in range(NB):
                n = ACC["glu"] + 2 * a + 1
                acc_read(act, n)
                if a >= 2:
                    acc_copied(act, n - 5)
                act.activation(msig[:, a % 2], acc(n)[:, :], ACT.Sigmoid).then_inc(acc_out[n % 4], 1)
            acc_copied(act, ACC["glu"] + 6)
            def gla(part, b):
                if part == "decay":
                    act.wait_ge(f_cum, 2)
                    act.activation(e1, cum, ACT.Exp, scale=1.0 / TAU).then_inc(g_dec, 1)
                    act.activation(e2, cum, ACT.Exp, scale=-1.0 / TAU).then_inc(g_dec, 1)
                    act.wait_ge(f_tail, 1)
                    act.activation(e3, tail, ACT.Exp, scale=1.0 / TAU).then_inc(g_dec, 1)
                elif part == "kt":
                    n = ACC["kt"] + b
                    acc_copy(n, ktok[:, :, P * b:P * b + P], acc(n)[:, :].rearrange("p (t d) -> p t d", t=NT))
                elif part == "o":
                    n = ACC["o"] + b
                    acc_read(act, n)
                    st.do(act.activation(o_part(b), acc(n)[:, :].rearrange("p (t h e) -> p t h e", t=2, h=2), ACT.Copy))
                    if b:
                        act.wait_ge(o_sum, b)
                    act.activation(osq, acc(n)[:, :], ACT.Square).then_inc(acc_out[n % 4], 1)
                else:
                    act.wait_ge(o_sum, NT + 1)
                    act.activation(stat[:, 16:32], stat[:, 16:32], ACT.Sqrt).then_inc(o_root, 1)

            for i in range(NT * HA + 1):
                if i < NT * HA:
                    tt, h = i // HA, i % HA
                    w = P * (tt + 1)
                    side_copied(act, s_use(i))
                    if i >= 2:
                        side_read(act, pt_use(i - 2))
                    act.activation(prob[:, i % 2, 0:w], logit[:, i % 2, 0:w], ACT.Exp, scale=-1.0,
                                   bias=amax[:, tt, h:h + 1], accum_out=asum[:, tt, h:h + 1]).then_inc(p_ready, 1)
                if i >= 1:
                    n, w = pt_use(i - 1), P * ((i - 1) // HA + 1)
                    side_copy(n, probT[:, (i - 1) % 2, 0:w], side(n)[:, 0:w])
                if i in ACT_GLA:
                    gla(*ACT_GLA[i])
            for tt in range(NT):
                n = SIDE["ya"] + tt
                side_copy(n, ys[:, 0, :, P * tt:P * tt + P], side(n)[:, :].rearrange("p (a q) -> p a q", a=NB))
            def top(s, per=0, it=0, kt=NK):
                act.wait_ge(slab_in[s % RING], it * (16 * per // RING) + 16 * (s // RING + 1))
                if split_no(s) >= 2:
                    act.wait_ge(slab_used, it * per + (s - 1))
                act.activation(w_hi[:, split_no(s) % 2, 0:kt * SW], ring[:, s % RING, 0:kt * SW], ACT.Copy
                               ).then_inc(w_top, 1)

            side_copied(act, s_use(NT * HA - 1))
            top(SLAB["merge"])
            for k in range(NK):
                copy(h_hi[:, k], hT[:, k], h_top)
            top(SLAB["merge"] + 1, kt=NB)
            with act.Fori(0, 2) as it:
                for step in range(6):
                    for q in range(2):
                        n = ACC["merge"] + 4 * step + q
                        act.wait_ge(acc_done, it * 24 + (n + 1))
                        act.wait_ge(acc_out[(n - 2) % 4], it * 6 + ((n - 2) // 4 + 1))
                        act.activation(msig[:, q], acc(n)[:, :], ACT.Sigmoid).then_inc(acc_out[n % 4], 1)
                    s = SLAB["merge"] + 2 * step + 2
                    top(s, 12, it)
                    top(s + 1, 12, it, NB)
            act.wait_ge(slab_in[(s + 1) % RING], 16 * ((SLAB["out"] + 1) // RING + 1))
            act.activation(w_hi[:, 1, NB * SW:], ring[:, (s + 1) % RING, NB * SW:], ACT.Copy).then_inc(half_top, 1)
            for k in range(NK):
                n = ACC["out"] + k
                acc_read(act, n)
                if k < 2:
                    acc_copied(act, ACC["merge"] + 46 + k)
                squares(k, acc(n)[:, :], 1, acc_out[n % 4])
                copy(yT[:, k], acc(n)[:, :], y_copied)
                if k % 2 and k < NK - 1:
                    top(SLAB["out"] + 2 + k // 2)
            root("rms1")
            for k in range(NK):
                act.wait_ge(x1_ready, k + 1)
                if k < 2:
                    slow_read(act, SLOW["rms1"])
                squares(k, x1[:, k], 2, sq_ready)
            root("rms2")
            act.wait_ge(fmod_ready, 1)
            for k in range(NK):
                act.wait_ge(hx, NK + k + 1)
                for dst in (h_hi, hT):
                    act.activation(dst[:, k], hT[:, k], ACT.Identity, scale=fpre[:, k:k + 1],
                                   bias=fmod[:, k:k + 1]).then_inc(h2_top, 1)

            top(SLAB["up"] + 1)
            act.sem_inc(gelu_out, 2)

            def up_pair(it, pair, s):
                act.wait_ge(taps, it * 3 + (pair + 1))
                slab = SLAB["up"] + 2 * pair + 2
                for r in range(4):
                    n = ACC["up"] + 4 * pair + r
                    act.wait_ge(acc_done, it * 12 + (n + 1))
                    act.wait_ge(gelu_out if r < 2 else ff_ready, it * 6 + (2 * pair + r % 2 + 1))
                    act.activation(cb[:, r], acc(n)[:, :], ACT.Identity, scale=cs[:, s, 2, r:r + 1],
                                   bias=cs[:, s, 3, r:r + 1]).then_inc(conv_0, 1)
                    if r == 1:
                        top(slab, 6, it)
                        for q in range(2):
                            n = ACC["up"] + 4 * pair + q
                            act.wait_ge(acc_out[n % 4], it * 3 + (n // 4 + 1))
                            act.wait_ge(ff_ready, it * 6 + (2 * pair + q + 1))
                            act.activation(gl[:, q], cb[:, q], ACT.Gelu_apprx_tanh).then_inc(gelu_out, 1)
                top(slab + 1, 6, it)

            def ff_top_part(j):
                act.wait_ge(ff_ready, 2 + 2 * j + 2)
                act.activation(ff_hi[:, j % 2], arena[:, 2 * T * j:2 * T * j + 2 * T], ACT.Copy).then_inc(ff_top, 1)

            with act.Fori(0, 3) as it:
                for s in range(3):
                    up_pair(it, s, s)
            up_pair(0, 9, 0)
            for j in range(2):
                ff_top_part(j)
            up_pair(0, 10, 1)
            for j in range(2, NF // 2):
                top(SLAB["down"] + j)
                ff_top_part(j)
            for i, m in enumerate(DOWN_ORDER):
                if m < 4:
                    acc_read(act, ACC["down"] + m)
                    signal = acc_out[(ACC["down"] + m) % 4]
                elif m < 7:
                    side_read(act, SIDE["down"] + m - 4)
                    signal = side_out[(SIDE["down"] + m - 4) % 3]
                else:
                    slow_read(act, SLOW["down"])
                    signal = slow_out
                if i < 2:
                    slow_read(act, SLOW["rms2"])
                squares(i, down_bank(m)[:, :], 3, signal)
            root("rms3")
            for n in (0, 1, 2, 3, 5, 7):
                acc_copy(ACC["xo"] + n, xo[:, n % NT, BW * (n // NT):BW * (n // NT) + BW])

        @block.vector
        def _(dve):
            st = Steps(dve, vstep)
            tt_, ts, stt = dve.tensor_tensor, dve.tensor_scalar, dve.scalar_tensor_tensor

            def cmul(out_r, out_i, ar, ai, br, bi, t):
                st.do(tt_(t[0], ar, br, ALU.mult))
                st.do(tt_(t[1], ai, bi, ALU.mult))
                st.do(tt_(t[2], ar, bi, ALU.mult))
                st.do(tt_(t[3], ai, br, ALU.mult))
                st.settle()
                st.do(tt_(out_r, t[0], t[1], ALU.subtract))
                st.do(tt_(out_i, t[2], t[3], ALU.add))

            def inverse_rms(norm, n):
                slow_read(dve, n)
                ts(rb, slow[:, :], EPS, None, ALU.add).then_inc(slow_out, 1)
                dve.wait_ge(rms_root, norm + 1)
                dve.reciprocal(rb, rb).then_inc(rinv, 1)
                dve.wait_ge(rinv, norm + 1)

            def modulate(part, slab, count, signal, it=0, per=0):
                for k in range(NK):
                    if k == 0:
                        ts(part, slab[:, 0, :], csil[:, 0:1], None, ALU.mult).then_inc(signal, 1)
                    else:
                        dve.wait_ge(signal, it * per + (count + k))
                        stt(part, slab[:, k, :], csil[:, k:k + 1], part, ALU.mult, ALU.add).then_inc(signal, 1)

            side_copied(dve, SIDE["vec"])
            dve.wait_ge(c_sig, 1)
            tt_(csil[:, :], csil[:, :], vT[:, V_C:V_C + NK], ALU.mult).then_inc(c_silu, 1)
            dve.wait_ge(c_silu, 1)
            for j in range(8):
                s = SLAB["mod"] + j
                dve.wait_ge(slab_in[s % RING], 16 * (s // RING + 1))
                if j >= 2:
                    dve.wait_ge(slab_used, s - 1)
                modulate(gemv[:, j % 2], slab_k(s), NK * j, mod_k)
            inverse_rms(0, SLOW["rms0"])
            for k in range(NK):
                tt_(hT[:, k], xT[:, k], rb, ALU.mult).then_inc(hx, 1)
            side_read(dve, SIDE["mod"])
            stt(mod[:, 0:16], side(SIDE["mod"])[:, 0:16], float(D), vT[:, V_MB:V_MB + 16], ALU.mult, ALU.add
                ).then_inc(side_out[SIDE["mod"] % 3], 1)
            side_copied(dve, SIDE["mod"])
            stt(pre[:, :], mod[:, 8:16], 1.0, vT[:, V_PRE:V_PRE + NK], ALU.add, ALU.mult).then_inc(mod_ready, 1)
            S = [sc[:, i, :] for i in range(28)]
            lr, li = vT[:, V_LR:V_LR + GP], vT[:, V_LI:V_LI + GP]
            dve.wait_ge(dt_exp, 2)
            tt_(S[2], lr, S[1], ALU.mult).then_inc(s5_ang, 1)
            st.do(tt_(S[8], li, S[1], ALU.mult))
            st.do(tt_(S[10], lr, lr, ALU.mult))
            st.do(tt_(S[11], li, li, ALU.mult))
            st.settle()
            ROUND = 1.5 * 2.0 ** 23
            st.do(ts(S[9], S[8], 1.0 / (2.0 * math.pi), None, ALU.mult))
            st.do(tt_(S[10], S[10], S[11], ALU.add))
            st.settle()
            st.do(ts(S[9], S[9], ROUND, None, ALU.add))
            st.do(dve.reciprocal(S[11], S[10]))
            st.settle()
            st.do(ts(S[9], S[9], -ROUND, None, ALU.add))
            st.settle()
            for part in (6.28125, 0.001934051513671875, 1.2556659314782e-06):
                st.do(stt(S[8], S[9], -part, S[8], ALU.mult, ALU.add))
                st.settle()
            st.do(ts(S[3], S[8], 3.1415925, -3.1415925, ALU.min, ALU.max))
            st.settle()
            st.do(ts(S[7], S[3], -1.0, None, ALU.mult))
            st.settle()
            st.do(tt_(S[7], S[7], S[3], ALU.max))
            st.settle()
            ts(S[7], S[7], -1.0, math.pi / 2, ALU.mult, ALU.add).then_inc(s5_ang, 1)
            dve.wait_ge(s5_trig, 3)
            apr, api = (apw[:, cc] for cc in range(2))
            st.do(dve.memset(apr[:, :, 0:1], 1.0))
            st.do(dve.memset(api[:, :, 0:1], 0.0))
            col = [s.unsqueeze(2) for s in S]
            st.do(tt_(apr[:, :, 1:2], col[4], col[6], ALU.mult))
            st.do(tt_(api[:, :, 1:2], col[4], col[5], ALU.mult))
            st.do(dve.memset(ph[:, 0, :, 0:1], 1.0))
            st.do(dve.memset(ph[:, 1, :, 0:1], 0.0))
            st.settle()
            for m in (1, 2, 4):
                t = [a_tmp[:, 64 * i:64 * i + GP * m].rearrange("p (g m) -> p g m", g=GP) for i in range(4)]
                a = [p[:, :, 1:m + 1] for p in (apr, api)]
                b = [p[:, :, m:m + 1].broadcast_to([P, GP, m]) for p in (apr, api)]
                cmul(apr[:, :, m + 1:2 * m + 1], api[:, :, m + 1:2 * m + 1], *a, *b, t)
                st.settle()
            st.do(ts(S[12], apr[:, :, 1], -1.0, None, ALU.add))
            st.settle()
            st.do(tt_(S[13], S[12], lr, ALU.mult))
            st.do(tt_(S[14], api[:, :, 1], li, ALU.mult))
            st.do(tt_(S[15], api[:, :, 1], lr, ALU.mult))
            st.do(tt_(S[16], S[12], li, ALU.mult))
            st.settle()
            st.do(tt_(S[13], S[13], S[14], ALU.add))
            st.do(tt_(S[15], S[15], S[16], ALU.subtract))
            st.settle()
            st.do(tt_(S[13], S[13], S[11], ALU.mult))
            tt_(S[15], S[15], S[11], ALU.mult).then_inc(s5_pow, 1)
            st.settle()
            dve.wait_ge(s5_pow, 1)
            dve.wait_ge(b_in, 32)
            f = [col[13].broadcast_to([P, GP, SP_]), col[15].broadcast_to([P, GP, SP_])]
            t = [a_tmp[:, 256 * i:256 * i + 256].rearrange("p (g q) -> p g q", g=GP) for i in range(4)]
            cmul(bb[:, 0], bb[:, 1], *f, brow[:, 0], brow[:, 1], t)
            st.settle()
            dve.wait_ge(x_in, 16)
            acc_copied(dve, ACC["x"] + NK - 1)
            for i in range(L):
                t = [a_tmp[:, 1024 * (i % 2) + 256 * n:1024 * (i % 2) + 256 * n + 256].rearrange(
                    "p (g q) -> p g q", g=GP) for n in range(4)]
                a = [p[:, :, L - 1 - i:L - i].broadcast_to([P, GP, SP_]) for p in (apr, api)]
                cmul(w1T[:, 0, :, i, :], w1T[:, 1, :, i, :], *a, bb[:, 0], bb[:, 1], t)
            mag, pc, ps = S[17], S[18], S[19]
            st.do(tt_(mag, S[4], S[4], ALU.mult))
            src = (S[6], S[5])
            for n in range(3):
                st.do(tt_(S[20], src[0], src[0], ALU.mult))
                st.do(tt_(S[21], src[1], src[1], ALU.mult))
                st.do(tt_(S[22], src[0], src[1], ALU.mult))
                st.settle()
                st.do(tt_(pc, S[20], S[21], ALU.subtract))
                st.do(ts(ps, S[22], 2.0, None, ALU.mult))
                if n < 2:
                    st.do(tt_(mag, mag, mag, ALU.mult))
                st.settle()
                src = (pc, ps)
            st.do(dve.tensor_copy(rho, mag.unsqueeze(2).broadcast_to([P, GP, NM])))
            for m in (1, 2, 4, 8, 16, 32):
                t = [a_tmp[:, 512 * i:512 * i + GP * m].rearrange("p (g m) -> p g m", g=GP) for i in range(4)]
                a = [ph[:, cc, :, 0:m] for cc in range(2)]
                b = [s.unsqueeze(2).broadcast_to([P, GP, m]) for s in (pc, ps)]
                cmul(ph[:, 0, :, m:2 * m], ph[:, 1, :, m:2 * m], *a, *b, t)
                if m < 32:
                    st.do(tt_(S[20], pc, pc, ALU.mult))
                    st.do(tt_(S[21], ps, ps, ALU.mult))
                    st.do(tt_(S[22], pc, ps, ALU.mult))
                    st.settle()
                    st.do(tt_(pc, S[20], S[21], ALU.subtract))
                    st.do(ts(ps, S[22], 2.0, None, ALU.mult))
                st.settle()
            dve.memset(rho[:, :, 0:1], 0.0).then_inc(s5_tables, 1)
            acc_copied(dve, ACC["iw"])
            for d in range(HI * (NT - 1)):
                tt, h = 1 + d // HI, d % HI
                w = P * (tt + 1)
                side_copied(dve, SIDE["dots"] + d)
                if h == 0:
                    ts(mb[:, tt, 0:w], relu[:, d % 2, 0:w], iw[:, tt, h:h + 1], None, ALU.mult).then_inc(score_mul, 1)
                else:
                    dve.wait_ge(score_mul, d)
                    stt(mb[:, tt, 0:w], relu[:, d % 2, 0:w], iw[:, tt, h:h + 1], mb[:, tt, 0:w],
                        ALU.mult, ALU.add).then_inc(score_mul, 1)
            for tt in range(1, NT):
                w = P * (tt + 1)
                dve.wait_ge(score_masked, tt)
                src = mb[:, tt, 0:w]
                for r in range(TOPK // 8):
                    st.do(dve.max(out=stat[:, 0:8], in_=src))
                    st.settle()
                    st.do(dve.match_replace(out=work[:, 0:w], in_to_replace=stat[:, 0:8], in_values=src,
                                            imm_value=TAKEN))
                    st.settle()
                    src = work[:, 0:w]
                st.do(tt_(work[:, 0:w], work[:, 0:w], mb[:, tt, 0:w], ALU.not_equal))
                st.settle()
                ts(mb[:, tt, 0:w], work[:, 0:w], -1.0, BIG, ALU.add, ALU.mult).then_inc(mask_ready, 1)
            side_read(dve, SIDE["lag"] + 1)
            for hf in range(2):
                nr, ni = SIDE["state"] + 2 * hf, SIDE["state"] + 2 * hf + 1
                g = slice(8 * hf, 8 * hf + 8)
                vr, vi = (side(n)[:, :].rearrange("p (g m) -> p g m", g=8) for n in (nr, ni))
                t = [a_tmp[:, 512 * i:512 * i + 512].rearrange("p (g m) -> p g m", g=8) for i in range(4)]
                side_read(dve, ni)
                st.do(tt_(t[0], vr, ph[:, 0, g], ALU.mult))
                st.do(tt_(t[1], vi, ph[:, 1, g], ALU.mult))
                tt_(t[2], vr, ph[:, 1, g], ALU.mult).then_inc(side_out[nr % 3], 1)
                tt_(t[3], vi, ph[:, 0, g], ALU.mult).then_inc(side_out[ni % 3], 1)
                st.settle()
                side_copied(dve, nr)
                side_copied(dve, ni)
                st.do(tt_(zst[:, 0, g], t[0], t[1], ALU.add))
                st.do(tt_(zst[:, 1, g], t[3], t[2], ALU.subtract))
                st.settle()
            for cc in range(2):
                z = zst[:, cc].rearrange("p g m -> p (g m)")
                st.do(dve.tensor_tensor_scan(z, rho.rearrange("p g m -> p (g m)"), z, 0.0, ALU.mult, ALU.add))
            st.settle()
            for hf in range(2):
                g = slice(8 * hf, 8 * hf + 8)
                t = [a_tmp[:, 512 * i:512 * i + 512].rearrange("p (g m) -> p g m", g=8) for i in range(4)]
                cmul(xst[:, 0, g, 1:], xst[:, 1, g, 1:], zst[:, 0, g], zst[:, 1, g], ph[:, 0, g], ph[:, 1, g], t)
                st.settle()
            dve.memset(xst[:, :, :, 0:1], 0.0).then_inc(state_ready, 1)
            dve.wait_ge(y_in, 16)
            for a in range(NB):
                stt(yback[:, a], tiles(a_u, NB)[:, a], vT[:, V_SD + a:V_SD + a + 1], yback[:, a],
                    ALU.mult, ALU.add).then_inc(yd_ready, 1)
            for a in range(GH):
                n = ACC["gr"] + a
                dve.wait_ge(r_sig, a + 1)
                tt_(sr[:, a], sr[:, a], acc(n)[:, :], ALU.mult).then_inc(acc_out[n % 4], 1)
            for a in range(2):
                n = SIDE["z"] + a
                side_read(dve, n)
                dve.wait_ge(f_abs, a + 1)
                ts(cum[:, a], side(n)[:, :], vT[:, V_GB + a:V_GB + a + 1], 0.0, ALU.add, ALU.min
                   ).then_inc(side_out[n % 3], 1)
            side_copied(dve, SIDE["z"])
            side_copied(dve, SIDE["z"] + 1)
            dve.wait_ge(f_exp, 2)
            st.do(tt_(cum, cum, e1, ALU.subtract))
            st.settle()
            dve.wait_ge(g_zero, 3)
            for a in range(2):
                dve.tensor_tensor_scan(cum[:, a], keep, cum[:, a], 0.0, ALU.mult, ALU.add).then_inc(f_cum, 1)
            dve.wait_ge(f_cum, 2)
            cc = cum.rearrange("p a t -> p (a t)").rearrange("p (c t) -> p c t", t=GC)
            tt_(tail.rearrange("p a t -> p (a t)").rearrange("p (c t) -> p c t", t=GC),
                cc[:, :, GC - 1:GC].broadcast_to([P, 2 * NC, GC]), cc, ALU.subtract).then_inc(f_tail, 1)
            for a in range(NB):
                n = ACC["glu"] + 2 * a
                acc_copied(dve, n + 1)
                tt_(ys[:, 1, a].rearrange("p (m j) -> p j m", j=L),
                    acc(n)[:, :].rearrange("p (j m) -> p j m", j=L),
                    msig[:, a % 2].rearrange("p (j m) -> p j m", j=L), ALU.mult).then_inc(acc_out[n % 4], 1)
            def gla(part, b):
                if part == "decay":
                    dve.wait_ge(g_dec, 3)
                    for a in range(2):
                        acc_copied(dve, ACC["gq"] + a)
                        acc_copied(dve, ACC["gk"] + a)
                    stt(gq, gq, GDK ** -0.5, e1, ALU.mult, ALU.mult).then_inc(g_k, 1)
                    tt_(e2, gk, e2, ALU.mult).then_inc(g_k, 1)
                    tt_(e3, gk, e3, ALU.mult).then_inc(g_k, 1)
                elif part == "gatt":
                    n = ACC["gatt"] + b
                    acc_read(dve, n)
                    dve.copy_predicated(gatt[:, b], chunkmask[:, :].bitcast(U32).unsqueeze(1).broadcast_to([P, NT, P]),
                                        acc(n)[:, :].rearrange("p (t q) -> p t q", t=NT)).then_inc(acc_out[n % 4], 1)
                elif part == "kv":
                    for pr in range(2):
                        n, cl = ACC["kv"] + 2 * pr + b % 2, b // 2
                        acc_read(dve, n)
                        if b == NC - 2:
                            acc_copied(dve, ACC["kv"] + 2 * pr + (b - 1) % 2)
                        elif b:
                            dve.wait_ge(carried, 2 * (b - 1) + pr + 1)
                        ins = stt(sprev[:, pr, b + 1, :], sprev[:, pr, b, :], e1[:, pr, GC * b + GC - 1:GC * b + GC],
                                  acc(n)[:, GDV * cl:GDV * cl + GDV], ALU.mult, ALU.add)
                        ins.then_inc(acc_out[n % 4] if b >= NC - 3 else carried, 1)
                elif part == "sum":
                    acc_copied(dve, ACC["o"] + b)
                    dve.tensor_reduce(stat[:, 16 + 4 * b:20 + 4 * b], osq.rearrange("p (h e) -> p h e", h=GH),
                                      AX.X, ALU.add).then_inc(o_sum, 1)
                    if b == 3:
                        dve.wait_ge(o_sum, NT)
                        ts(stat[:, 16:32], stat[:, 16:32], 1.0 / GDV, EPS, ALU.mult, ALU.add).then_inc(o_sum, 1)
                elif part == "inverse":
                    dve.wait_ge(o_root, 1)
                    dve.reciprocal(stat[:, 16:32], stat[:, 16:32]).then_inc(o_inv, 1)
                elif part == "norm":
                    dve.wait_ge(o_inv, 1)
                    for c in range(2 * b, 2 * b + 2):
                        for i in range(2):
                            v, col = o_part(c)[:, i], 16 + 4 * c + 2 * i
                            tt_(v, v, stat[:, col:col + 2].unsqueeze(2).broadcast_to([P, 2, GDV]), ALU.mult
                                ).then_inc(o_norm, 1)
                else:
                    n = ACC["ot"] + b
                    acc_read(dve, n)
                    stt(ys[:, 2, b], acc(n)[:, :], vT[:, V_GN + b:V_GN + b + 1], sr[:, b], ALU.mult, ALU.mult
                        ).then_inc(acc_out[n % 4], 1)

            dve.wait_ge(mask0_ready, 1)
            dve.wait_ge(mask_ready, NT - 1)
            for i in range(NT * HA + 2):
                if i >= 2 and (i - 2) % HA == HA - 1:
                    tt = (i - 2) // HA
                    dve.wait_ge(p_ready, HA * (tt + 1))
                    st.do(dve.reciprocal(asum[:, tt], asum[:, tt]))
                    st.settle()
                    slow_read(dve, SLOW["pv"] + tt)
                    tt_(ytok[:, tt].rearrange("p (h d) -> p h d", h=HA), slow[:, :].rearrange("p (h d) -> p h d", h=HA),
                        asum[:, tt].unsqueeze(2).broadcast_to([P, HA, DH]), ALU.mult).then_inc(slow_out, 1)
                if i < NT * HA:
                    tt, h = i // HA, i % HA
                    w, n = P * (tt + 1), s_use(i)
                    side_read(dve, n)
                    if i >= 2:
                        dve.wait_ge(p_ready, i - 1)
                    dve.tensor_tensor_reduce(logit[:, i % 2, 0:w], side(n)[:, 0:w], mb[:, tt, 0:w], -(DH ** -0.5),
                                             3.0e38, ALU.add, ALU.min, amax[:, tt, h:h + 1]).then_inc(side_out[n % 3], 1)
                if i in DVE_GLA:
                    gla(*DVE_GLA[i])
            def rest(s, per=0, it=0, kt=NK):
                dve.wait_ge(w_top, it * per + (split_no(s) + 1))
                tt_(w_lo[:, s % RING, 0:kt * SW], ring[:, s % RING, 0:kt * SW],
                    w_hi[:, split_no(s) % 2, 0:kt * SW].bitcast(F32), ALU.subtract).then_inc(w_ready, 1)

            rest(SLAB["merge"])
            for k in range(NK):
                dve.wait_ge(h_top, k + 1)
                tt_(h_lo[:, k], hT[:, k], h_hi[:, k].bitcast(F32), ALU.subtract).then_inc(h_split, 1)
            rest(SLAB["merge"] + 1, kt=NB)

            with dve.Fori(0, 2) as it:
                for step in range(6):
                    jj, i = step // NBR, step % NBR
                    dve.wait_ge(fmod_in, it * 96 + 16 * (step + 1))
                    n = SIDE["fmod"] + step
                    dve.wait_ge(side_out[(n - 2) % 3], it * 2 + ((n - 2) // 3 + 1))
                    modulate(gemv[:, step % 2], fmod_slab, NK * step, gemv_k, it, 6 * NK)
                    for q in range(2):
                        n = ACC["merge"] + 4 * step + q
                        m = merged[:, bass.ds(it * 4 + (2 * jj + q), 1), :].squeeze(1)
                        dve.wait_ge(acc_done, it * 24 + (n + 3))
                        dve.wait_ge(acc_out[n % 4], it * 6 + (n // 4 + 1))
                        dst = m if i == 0 else mtmp
                        tt_(dst, acc(n + 2)[:, :], msig[:, q], ALU.mult).then_inc(acc_out[(n + 2) % 4], 1)
                        dve.wait_ge(acc_out[(n + 2) % 4], it * 6 + ((n + 2) // 4 + 1))
                        if i:
                            tt_(m, m, mtmp, ALU.add).then_inc(merge_sum, 1)
                            dve.wait_ge(merge_sum, it * 8 + (4 * jj + 2 * (i - 1) + q + 1))
                        if i == 2:
                            hi, lo = (x[:, bass.ds(it * 4 + (2 * jj + q), 1), :].squeeze(1) for x in (m_hi, m_lo))
                            dve.tensor_copy(hi, m).then_inc(m_split, 1)
                            dve.wait_ge(m_split, it * 8 + (4 * jj + 2 * q + 1))
                            tt_(lo, m, hi.bitcast(F32), ALU.subtract).then_inc(m_split, 1)
                        s = SLAB["merge"] + 2 * step + 2 + q
                        rest(s, 12, it, NB if q else NK)
                    n = SIDE["fmod"] + step
                    dve.wait_ge(side_done, it * 6 + (n + 1))
                    stt(fmod[:, bass.ds(it * 12 + 2 * step, 2)], side(n)[:, 0:2], float(D),
                        vT[:, bass.ds(it * 12 + (V_FMB + 2 * step), 2)], ALU.mult, ALU.add).then_inc(side_out[n % 3], 1)
            dve.wait_ge(half_top, 1)
            s = SLAB["out"] + 1
            tt_(w_lo[:, s % RING, NB * SW:], ring[:, s % RING, NB * SW:], w_hi[:, 1, NB * SW:].bitcast(F32), ALU.subtract
                ).then_inc(half_ready, 1)
            rest(SLAB["out"] + 2)
            for j in range(4):
                dve.wait_ge(modg_in[j % 2], 16 * (j // 2 + 1))
                if j < 2:
                    side_copied(dve, SIDE["fmod"] + 10 + j)
                else:
                    dve.wait_ge(fmod_used, 12 + j)
                modulate(gemv[:, j % 2], (fmod_slab, modg_slab)[j % 2], NK * (12 + j), gemv_k)
                if j == 1:
                    rest(SLAB["out"] + 3)
            for step in range(9, 12):
                side_copied(dve, SIDE["fmod"] + step)
            st.do(tt_(fpost[:, :], fmod[:, 16:24], vT[:, V_FPOST:V_FPOST + NK], ALU.mult))
            stt(fpre[:, :], fmod[:, 8:16], 1.0, vT[:, V_FPRE:V_FPRE + NK], ALU.add, ALU.mult).then_inc(fmod_ready, 1)
            def residual(factor, signal):
                base = st.n
                for k in range(NK + 2):
                    if k < NK:
                        st.do(tt_(yT[:, k], yT[:, k], rb, ALU.mult))
                    if k >= 2:
                        dve.wait_ge(vstep, base + k - 1)
                        stt(x1[:, k - 2], yT[:, k - 2], factor[:, k - 2:k - 1], x1[:, k - 2], ALU.mult, ALU.add
                            ).then_inc(signal, 1)

            side_read(dve, SIDE["modg"])
            st.do(stt(mod[:, 16:24], side(SIDE["modg"])[:, 0:8], float(D), vT[:, V_MB + 16:V_MB + 24], ALU.mult, ALU.add))
            st.settle()
            tt_(post[:, :], mod[:, 16:24], vT[:, V_POST:V_POST + NK], ALU.mult).then_inc(side_out[SIDE["modg"] % 3], 1)
            side_copied(dve, SIDE["modg"])
            inverse_rms(1, SLOW["rms1"])
            dve.wait_ge(x_back, 16)
            dve.wait_ge(y_copied, NK)
            residual(post, x1_ready)
            rest(SLAB["up"])
            dve.wait_ge(x1_ready, NK)
            inverse_rms(2, SLOW["rms2"])
            for k in range(NK):
                tt_(hT[:, k], x1[:, k], rb, ALU.mult).then_inc(hx, 1)
            for k in range(NK):
                dve.wait_ge(h2_top, 2 * k + 2)
                tt_(h_lo[:, k], hT[:, k], h_hi[:, k].bitcast(F32), ALU.subtract).then_inc(h2_ready, 1)
            rest(SLAB["up"] + 1)

            dve.sem_inc(ff_ready, 2)

            def up_pair(it, pair, s):
                for r in range(4):
                    n, j = ACC["up"] + 4 * pair + r, 4 * pair + r
                    dve.wait_ge(conv_0, it * 12 + (j + 1))
                    stt(cb[:, r, 1:], acc(n)[:, 0:T - 1], cs[:, s, 1, r:r + 1], cb[:, r, 1:], ALU.mult, ALU.add
                        ).then_inc(conv_1, 1)
                    dve.wait_ge(conv_1, it * 12 + (j + 1))
                    stt(cb[:, r, 2:], acc(n)[:, 0:T - 2], cs[:, s, 0, r:r + 1], cb[:, r, 2:], ALU.mult, ALU.add
                        ).then_inc(acc_out[n % 4], 1)
                    if r == 1:
                        rest(SLAB["up"] + 2 * pair + 2, 6, it)
                for q in range(2):
                    n = ACC["up"] + 4 * pair + 2 + q
                    dve.wait_ge(acc_out[n % 4], it * 3 + (n // 4 + 1))
                    dve.wait_ge(gelu_out, it * 6 + (2 * pair + q + 3))
                    dst = ff[:, bass.ds(it * 6 + (2 * pair + q), 1), :].squeeze(1) if pair < 9 else ff[:, 2 * pair + q]
                    tt_(dst, gl[:, q], cb[:, 2 + q], ALU.mult).then_inc(ff_ready, 1)
                rest(SLAB["up"] + 2 * pair + 3, 6, it)

            def ff_rest(j):
                dve.wait_ge(ff_top, j + 1)
                tt_(ff_lo[:, j % 2], arena[:, 2 * T * j:2 * T * j + 2 * T], ff_hi[:, j % 2].bitcast(F32), ALU.subtract
                    ).then_inc(ff_split, 1)

            with dve.Fori(0, 3) as it:
                for s in range(3):
                    up_pair(it, s, s)
            up_pair(0, 9, 0)
            for j in range(2):
                ff_rest(j)
            up_pair(0, 10, 1)
            for j in range(2, NF // 2):
                rest(SLAB["down"] + j)
                ff_rest(j)
            for m in DOWN_ORDER:
                if m < 4:
                    acc_copied(dve, ACC["down"] + m)
                elif m < 7:
                    side_copied(dve, SIDE["down"] + m - 4)
                else:
                    slow_copied(dve, SLOW["down"])
                dve.tensor_copy(yT[:, m], down_bank(m)[:, :]).then_inc(y_copied, 1)
            dve.wait_ge(y_copied, 2 * NK)
            inverse_rms(3, SLOW["rms3"])
            residual(fpost, x2_ready)
            for n in (4, 6):
                acc_read(dve, ACC["xo"] + n)
                dve.tensor_copy(xo[:, n - 4, BW:D], acc(ACC["xo"] + n)[:, :]).then_inc(acc_out[(ACC["xo"] + n) % 4], 1)

        @block.tensor
        def _(pe):
            def mm(dst, w, moving, start, stop, signal=None, **kw):
                ins = pe.matmul(dst, w, moving, start=start, stop=stop, **kw)
                if signal is not None:
                    ins.then_inc(signal, 1)

            def take(s):
                pe.wait_ge(slab_in[s % RING], 16 * (s // RING + 1))

            def acc_free(n):
                if n >= 4:
                    acc_copied(pe, n - 4)

            def side_free(n):
                if n >= 3:
                    side_copied(pe, n - 3)

            def channel_tile(n, s, q, moving, kt=NK, cols=SW):
                acc_free(n)
                for k in range(kt):
                    mm(acc(n)[:, :], slab_k(s, cols)[:, k, P * q:P * q + P], moving[:, k], k == 0, k == kt - 1,
                       slab_used if k == 0 and q == 0 and s != SLAB["iq"] else acc_done if k == kt - 1 else None)

            def split_tile(n, s, q, moving, kt=NK, ready=None):
                for k in range(kt):
                    if ready is not None:
                        pe.wait_ge(ready, k + 1)
                    for i, (wp, mp) in enumerate(PARTS):
                        w = (w_hi[:, split_no(s) % 2], w_lo[:, s % RING])[wp].rearrange("p (k n) -> p k n", n=SW)
                        first, last = k == i == 0, k == kt - 1 and i == 2
                        mm(acc(n)[:, :], w[:, k, P * q:P * q + P], moving[mp][:, k], first, last,
                           acc_done if last else slab_used if first and q == 0 else None)

            def project(name, a):
                s = SLAB[name] + a // 2
                if a % 2 == 0:
                    take(s)
                channel_tile(ACC[name] + a, s, a % 2, hT)

            def token_tiles(name):
                for half in range(2):
                    s = SLAB[name] + half
                    take(s)
                    for tt in range(NT):
                        n = ACC[name] + tt
                        if half == 0:
                            acc_free(n)
                        for k in range(4):
                            mm(acc(n)[:, :], hT[:, 4 * half + k, P * tt:P * tt + P], slab_k(s, BW)[:, k, :],
                               half == k == 0, half == 1 and k == 3,
                               slab_used if tt == k == 0 else acc_done if half == 1 and k == 3 else None)

            def modulate(use, j, part, signal, last):
                for q in range(2):
                    mm(side(use)[:, 2 * j + q:2 * j + q + 1], part[:, P * q:P * q + P], mean[:, 0:1], True, True,
                       side_done if last and q else signal if last or q else None)

            def sum_squares(k, name):
                mm(slow[:, :], mean[:, :], sq[:, k % 2], k == 0, k == NK - 1,
                   slow_done if k == NK - 1 else sq_used)

            def dots(d):
                n, tt, h = SIDE["dots"] + d, 1 + d // HI, d % HI
                part, w = slice(DI * (h % 4), DI * (h % 4) + DI), P * (tt + 1)
                side_free(n)
                mm(side(n)[:, 0:w], iqT[part, h // 4, P * tt:P * tt + P], ikT[part, 0:w], True, True, side_done)

            pe.wait_ge(consts, 4)
            pe.wait_ge(vec_in, 16 * 15)
            n = SIDE["vec"]
            pe.transpose(side(n)[:, 0:V_CW], vrow[0:V_CW, 0, :], ident[0:V_CW, 0:V_CW])
            pe.transpose(side(n)[:, V_CW:V_CW + P], vrow[:, 1, :], ident[:, :])
            pe.transpose(side(n)[:, V_CW + P:V_N], vrow[0:V_N - V_CW - P, 2, :],
                         ident[0:V_N - V_CW - P, 0:V_N - V_CW - P]).then_inc(side_done, 1)
            side_free(SIDE["mod"])
            pe.wait_ge(x_in, 16)
            for k in range(NK + 1):
                if k < NK:
                    n = ACC["x"] + k
                    acc_free(n)
                    for tt in range(NT):
                        ins = pe.transpose(acc(n)[:, P * tt:P * tt + P], xtok[:, tt, P * k:P * k + P], ident[:, :])
                    ins.then_inc(acc_done, 1)
                if k:
                    acc_copied(pe, ACC["x"] + k - 1)
                    sum_squares(k - 1, "rms0")
                j = k - 1
                if j >= 0:
                    pe.wait_ge(mod_k, NK * (j + 1))
                    modulate(SIDE["mod"], j, gemv[:, j % 2], slab_used, j == 7)
            pe.wait_ge(c_in, 64)
            for cc in range(2):
                n = SIDE["ctr"] + cc
                for r in range(4):
                    ins = pe.transpose(side(n)[:, P * r:P * r + P],
                                       crow[:, cc, r].rearrange("p d n -> p (d n)"), ident[:, :])
                ins.then_inc(side_done, 1)
            pe.wait_ge(h_ready, NK)
            project("iq", 0)
            project("iq", 1)
            pe.wait_ge(small_in, 16 * 7)
            for name, c0, w in (("ik", 0, P), ("lr", 4 * DI + HI, RANK)):
                n = ACC[name]
                acc_free(n)
                for k in range(NK):
                    mm(acc(n)[0:w, :], wsmall[:, k, c0:c0 + w], hT[:, k], k == 0, k == NK - 1,
                       acc_done if k == NK - 1 else None)
            n = ACC["iw"]
            acc_free(n)
            for tt in range(NT):
                for k in range(NK):
                    mm(acc(n)[:, HI * tt:HI * tt + HI], hT[:, k, P * tt:P * tt + P],
                       wsmall[:, k, 4 * DI:4 * DI + HI], k == 0, k == NK - 1,
                       acc_done if tt == NT - 1 and k == NK - 1 else None)
            for a in range(3 * NB):
                project(("u", "q", "k")[a // NB], a % NB)
                if a == 0:
                    acc_copied(pe, ACC["iq"] + 1)
                    acc_copied(pe, ACC["ik"])
                dots(2 * a)
                dots(2 * a + 1)
            token_tiles("v")
            pe.wait_ge(s5_tables, 1)
            for b in range(8):
                n, cc = SIDE["w1"] + b, b // 4
                side_free(n)
                for i in range(4):
                    ins = pe.transpose(side(n)[:, P * i:P * i + P],
                                       w1T[:, cc, 4 * (b % 4) + i].rearrange("p i q -> p (i q)"), ident[:, :])
                ins.then_inc(side_done, 1)
            for d in range(2):
                n, part = SIDE["lag"] + d, slice(SN * d, SN * d + SN)
                side_free(n)
                for g in range(GP):
                    for cc in range(2):
                        mm(side(n)[:, SP_ * g:SP_ * g + SP_], w1T[part, cc, g].rearrange("p i q -> p (i q)"),
                           cT[part, 2 * cc, g], cc == 0, cc == 1, side_done if g == GP - 1 and cc else None)
            for d in range(2):
                side_copied(pe, SIDE["lag"] + d)
            for j in range(L):
                n, c0 = SIDE["shift"] + j, SP_ * (L - 1 - j)
                side_free(n)
                mm(side(n)[:, :], wide[:, c0:c0 + P], lag, True, True, side_done)
            pe.wait_ge(ub_in, 16 * L)
            for hf in range(2):
                for cc in range(2):
                    n = SIDE["state"] + 2 * hf + cc
                    side_free(n)
                    for g in range(16 * hf, 16 * hf + 16):
                        part = slice(SN * (g % 2), SN * (g % 2) + SN)
                        col = NM * (g // 2 % 8)
                        mm(side(n)[part, col:col + NM], w1[:, cc, g // 2, part], ub[:, g], True, True,
                           side_done if g == 16 * hf + 15 else None)
            project("gq", 0)
            project("gq", 1)
            project("gk", 0)
            project("gk", 1)
            pe.wait_ge(state_ready, 1)
            for b in range(4):
                n = SIDE["y"] + b
                side_free(n)
                part = slice(SN * (b % 2), SN * (b % 2) + SN)
                for i in range(8):
                    g = 2 * (8 * (b // 2) + i) + b % 2
                    dst = side(n)[:, NM * i:NM * i + NM]
                    mm(dst, toep[:, g].rearrange("p j q -> p (j q)"), ub[:, g], True, False)
                    for cc in range(2):
                        mm(dst, w2[cc][part, g // 2].rearrange("p j q -> p (j q)"), xst[part, cc, g // 2, 0:NM],
                           False, cc == 1, side_done if cc and i == 7 else None)
            token_tiles("gv")
            for a in range(GH):
                project("gr", a)
            for a in range(2):
                n = SIDE["z"] + a
                side_free(n)
                mm(side(n)[:, :], wgate[:, P * a:P * a + P], lrT, True, True, side_done)
            for half in range(2):
                take(SLAB["glu"] + half)
            pe.wait_ge(g_ready, NB)
            for a in range(NB):
                for half in range(2):
                    n, s = ACC["glu"] + 2 * a + half, SLAB["glu"] + half
                    acc_free(n)
                    for k in range(NB):
                        mm(acc(n)[:, :], slab_k(s, BW)[:, k, P * a:P * a + P], yback[:, k], k == 0, k == NB - 1,
                           acc_done if k == NB - 1 else slab_used if k == 0 and a == 0 and half == 0
                           else slab_used if k == 0 and a == NB - 1 and half == 1 else None)
            def gla(part, b):
                if part == "kt":
                    n = ACC["kt"] + b
                    acc_free(n)
                    pe.wait_ge(g_k, 3)
                    for tt in range(NT):
                        ins = pe.transpose(acc(n)[:, P * tt:P * tt + P], e3[:, b, P * tt:P * tt + P], ident[:, :])
                    ins.then_inc(acc_done, 1)
                elif part == "gatt":
                    n, half = ACC["gatt"] + b, slice(GDK * (b % 2), GDK * (b % 2) + GDK)
                    acc_free(n)
                    for tt in range(NT):
                        tok = slice(P * tt, P * tt + P)
                        mm(acc(n)[:, tok], e2[half, b // 2, tok], gq[half, b // 2, tok], True, True,
                           acc_done if tt == NT - 1 else None)
                elif part == "kv":
                    acc_copied(pe, ACC["kt"] + b)
                    for hf in range(2):
                        n, rws = ACC["kv"] + 2 * b + hf, slice(GC * hf, GC * hf + GC)
                        acc_free(n)
                        for cl in range(4 - hf):
                            ch = 2 * cl + hf
                            for d in range(2):
                                half = slice(GDK * d, GDK * d + GDK)
                                mm(acc(n)[half, GDV * cl:GDV * cl + GDV],
                                   ktok[rws, ch // 2, P * b + GDK * d:P * b + GDK * d + GDK],
                                   gv[rws, ch // 2, GDV * (2 * b + d):GDV * (2 * b + d) + GDV], True, True,
                                   acc_done if cl == 3 - hf and d else None)
                elif part == "o":
                    n, half = ACC["o"] + b, slice(GDK * (b % 2), GDK * (b % 2) + GDK)
                    if b == 0:
                        for h in range(GH):
                            acc_copied(pe, ACC["gatt"] + h)
                        for kv in range(4):
                            acc_copied(pe, ACC["kv"] + kv)
                    acc_free(n)
                    for i in range(4):
                        tt, h = 2 * (b // 2) + i // 2, b % 2 + 2 * (i % 2)
                        col = slice(GDV * i, GDV * i + GDV)
                        mm(acc(n)[:, col], gatt[:, h, tt, :], gv[:, tt, GDV * h:GDV * h + GDV], True, False,
                           skip_group_check=True)
                        for hf in range(2):
                            ch = 2 * tt + hf
                            if ch:
                                mm(acc(n)[GC * hf:GC * hf + GC, col], gq[half, h // 2, GC * ch:GC * ch + GC],
                                   sprev[half, h // 2, ch, :], False, True,
                                   acc_done if i == 3 and hf else None, skip_group_check=True)
                else:
                    n = ACC["ot"] + b
                    acc_free(n)
                    pe.wait_ge(o_norm, 8)
                    for tt in range(NT):
                        ins = pe.transpose(acc(n)[:, P * tt:P * tt + P], og[:, tt, GDV * b:GDV * b + GDV], ident[:, :])
                    ins.then_inc(acc_done, 1)

            for i in range(NT * HA + 2):
                if i < NT * HA:
                    n, tt, h = s_use(i), i // HA, i % HA
                    part, w = slice(DH * (h % 2), DH * (h % 2) + DH), P * (tt + 1)
                    side_free(n)
                    mm(side(n)[:, 0:w], q_sb[part, h // 2, P * tt:P * tt + P], k_sb[part, h // 2, 0:w], True, True,
                       side_done)
                if 1 <= i <= NT * HA:
                    n = pt_use(i - 1)
                    side_free(n)
                    pe.wait_ge(p_ready, i)
                    for j in range((i - 1) // HA + 1):
                        ins = pe.transpose(side(n)[:, P * j:P * j + P], prob[:, (i - 1) % 2, P * j:P * j + P],
                                           ident[:, :])
                    ins.then_inc(side_done, 1)
                if i >= 2:
                    tt, h = (i - 2) // HA, (i - 2) % HA
                    if h == 0:
                        slow_copied(pe, SLOW["pv"] + tt - 1)
                    side_copied(pe, pt_use(i - 2))
                    for j in range(tt + 1):
                        mm(slow[:, DH * h:DH * h + DH], probT[:, i % 2, P * j:P * j + P],
                           v_sb[:, j, DH * h:DH * h + DH], j == 0, j == tt,
                           slow_done if h == HA - 1 and j == tt else None)
                if i in PE_GLA:
                    gla(*PE_GLA[i])
            for tt in range(NT):
                n = SIDE["ya"] + tt
                side_free(n)
                slow_copied(pe, SLOW["pv"] + tt)
                for a in range(NB):
                    ins = pe.transpose(side(n)[:, P * a:P * a + P], ytok[:, tt, P * a:P * a + P], ident[:, :])
                ins.then_inc(side_done, 1)
            with pe.Fori(0, 2) as it:
                for step in range(6):
                    i, s = step % NBR, SLAB["merge"] + 2 * step
                    for m, moving, kt in ((0, (h_hi, h_lo), NK), (1, (ys_hi[i], ys_lo[:, i]), NB)):
                        pe.wait_ge(w_ready, it * 12 + (split_no(s) + m + 1))
                        if m:
                            pe.wait_ge(y_split, i + 1)
                        for q in range(2):
                            n = ACC["merge"] + 4 * step + 2 * m + q
                            pe.wait_ge(acc_out[n % 4], it * 6 + n // 4)
                            split_tile(n, s + m, q, moving, kt, h_split if step == m == q == 0 else None)
                    n = SIDE["fmod"] + step
                    pe.wait_ge(gemv_k, it * (6 * NK) + NK * (step + 1))
                    pe.wait_ge(side_out[n % 3], it * 2 + n // 3)
                    for q in range(2):
                        mm(side(n)[:, q:q + 1], gemv[:, step % 2, P * q:P * q + P], mean[:, 0:1], True, True,
                           side_done if q else fmod_used)
            pe.wait_ge(m_split, 2 * NK)
            for k in range(NK + 1):
                if k < NK:
                    s = SLAB["out"] + k // 2
                    if k % 2 == 0:
                        pe.wait_ge(w_ready, split_no(s) + 1)
                    if k == 2:
                        pe.wait_ge(half_ready, 1)
                    acc_free(ACC["out"] + k)
                    if k >= 4:
                        pe.wait_ge(y_copied, k - 3)
                    split_tile(ACC["out"] + k, s, k % 2, (m_hi, m_lo))
                if k:
                    acc_copied(pe, ACC["out"] + k - 1)
                    sum_squares(k - 1, "rms1")
                if k in (3, 5, 7, 8):
                    j = (3, 5, 7, 8).index(k)
                    if j == 0:
                        side_free(SIDE["modg"])
                    pe.wait_ge(gemv_k, NK * (12 + j + 1))
                    modulate(SIDE["modg"], j, gemv[:, j % 2], fmod_used, j == 3)
            for k in range(NK):
                pe.wait_ge(sq_ready, k + 1)
                if k == 0:
                    slow_copied(pe, SLOW["rms1"])
                sum_squares(k, "rms2")

            def up_pair(it, pair):
                for r in range(4):
                    n, s = ACC["up"] + 4 * pair + r, SLAB["up"] + 2 * pair + r // 2
                    if r % 2 == 0:
                        pe.wait_ge(w_ready, it * 6 + (split_no(s) + 1))
                    pe.wait_ge(acc_out[n % 4], it * 3 + n // 4)
                    split_tile(n, s, r % 2, (h_hi, h_lo), ready=h2_ready if pair == r == 0 else None)

            with pe.Fori(0, 3) as it:
                for pair in range(3):
                    up_pair(it, pair)
            for pair in range(9, 11):
                up_pair(0, pair)
            for m in range(4):
                acc_free(ACC["down"] + m)
            for m in range(3):
                side_free(SIDE["down"] + m)
            slow_copied(pe, SLOW["rms2"])
            for j in range(NF // 2):
                s = SLAB["down"] + j
                pe.wait_ge(w_ready, split_no(s) + 1)
                pe.wait_ge(ff_split, j + 1)
                for kk in range(2):
                    tok = slice(T * kk, T * kk + T)
                    for m in range(NK):
                        col = slice(D * kk + P * m, D * kk + P * m + P)
                        done = acc_done if m < 4 else side_done if m < 7 else slow_done
                        for i, (wp, mp) in enumerate(PARTS):
                            w, f = (w_hi[:, split_no(s) % 2], w_lo[:, s % RING])[wp], (ff_hi, ff_lo)[mp][:, j % 2]
                            last = j == NF // 2 - 1 and kk == 1 and i == 2
                            mm(down_bank(m)[:, :], w[:, col], f[:, tok], j == kk == i == 0, last,
                               done if last else slab_used if kk == m == i == 0 else None)
            for i, m in enumerate(DOWN_ORDER):
                if m < 4:
                    acc_copied(pe, ACC["down"] + m)
                elif m < 7:
                    side_copied(pe, SIDE["down"] + m - 4)
                else:
                    slow_copied(pe, SLOW["down"])
                    pe.wait_ge(y_copied, NK + 1)
                sum_squares(i, "rms3")
            for n in range(8):
                half, tt = n // NT, n % NT
                pe.wait_ge(x2_ready, 4 * half + 4)
                acc_free(ACC["xo"] + n)
                for i in range(4):
                    ins = pe.transpose(acc(ACC["xo"] + n)[:, P * i:P * i + P],
                                       x1[:, 4 * half + i, P * tt:P * tt + P], ident[:, :])
                ins.then_inc(acc_done, 1)


_INS = ['x', 'c', 'mix_mod_w', 'mix_mod_b', 'mix_pre_g', 'mix_post_g', 'w_in', 's5_lam_re', 's5_lam_im', 's5_log_dt', 's5_b_re', 's5_b_im', 's5_c_re', 's5_c_im', 's5_d', 's5_w_glu', 'gla_w_gate', 'gla_b_gate', 'gla_norm_g', 'w_branch', 'w_out', 'ffn_mod_w', 'ffn_mod_b', 'ffn_pre_g', 'ffn_post_g', 'ffn_w_up', 'ffn_conv_w', 'ffn_conv_b', 'ffn_w_down']
_OUTS = [((1, T, D), 'float32')]


def kernel(**inputs):
    import numpy as _np
    import concourse.bacc as _bacc
    from concourse import mybir as _mybir
    from concourse.bass_utils import run_bass_kernel_spmd as _run

    nc = _bacc.Bacc("TRN2", target_bir_lowering=False, num_devices=1)
    arrays, args = {}, []
    for name in _INS:
        a = _np.ascontiguousarray(inputs[name])
        arrays[f"in_{name}_dram"] = a
        args.append(nc.dram_tensor(f"in_{name}_dram", a.shape, _mybir.dt.from_np(a.dtype), kind="ExternalInput").ap())
    for i, (shape, dtype) in enumerate(_OUTS):
        dt = _mybir.dt.from_np(_np.dtype(dtype))
        args.append(nc.dram_tensor(f"out_{i}_dram", shape, dt, kind="ExternalOutput").ap())
    trunk_kernel(nc, *args)
    r = _run(nc, [arrays], core_ids=[0])
    return r.results[0]["out_0_dram"]
```

```python
from contextlib import ExitStack
import math

import concourse.bass as bass
from concourse import mybir

F32 = mybir.dt.float32
F32R = mybir.dt.float32r
U32 = mybir.dt.uint32
ALU = mybir.AluOpType
ACT = mybir.ActivationFunctionType
AX = mybir.AxisListType

P = 128
T = 512
D = 1024
NT = T // P
NK = D // P
HA, DH = 8, 64
HI, DI = 8, 32
TOPK = min(256, T // 4)
BW = 512
NB = BW // P
NBR = 3
SG, SP_, SN = 32, 16, 64
GP = SG // 2
L = P // SP_
NM = T // L
GH, GDK, GDV, GC = 4, 64, 128, 64
NC = T // GC
RANK = 16
TAU = 16.0
FF = 2816
NF = FF // P
EPS = 1e-6
BIG = 1.0e30
TAKEN = -3.4e38
NEVER = -3.3e38

C_AQ, C_AK, C_AV, C_IQ, C_IK, C_IW = 0, 512, 1024, 1536, 1792, 1824
C_U, C_GQ, C_GK, C_GV, C_GR, C_LR, C_GL = 1832, 2344, 2600, 2856, 3368, 3880, 3896

V_MB, V_PRE, V_POST, V_SD, V_GB, V_GN, V_FMB, V_FPRE, V_FPOST = 0, 24, 32, 40, 44, 46, 50, 74, 82
V_CW, V_CB, V_LR, V_LI, V_N = 90, 222, 266, 282, 298

RING = 3
SW = 256


def count_up(parts):
    at, n = {}, 0
    for name, uses in parts:
        at[name] = n
        n += uses
    return at


SLAB = count_up([("mod", 8), ("iq", 1), ("u", 2), ("q", 2), ("k", 2), ("v", 2), ("gq", 1), ("gk", 1),
                 ("gv", 2), ("gr", 2), ("glu", 2), ("merge", 24), ("out", 4), ("up", 22), ("down", 11), ("end", 0)])
PARTS = ((0, 0), (0, 1), (1, 0))
ACC = count_up([("x", NK), ("lr", 1), ("ik", 1), ("iq", 2), ("u", 4), ("q", 4), ("k", 4), ("v", 4),
                ("gq", 2), ("gk", 2), ("gv", 4), ("gr", 4), ("glu", 8), ("kt", 2), ("gatt", 4), ("kv", 4), ("o", 4), ("ot", 4), ("merge", 48), ("out", 8), ("up", 44),
                ("down", 4), ("xo", 8)])
SIDE = count_up([("c", 1), ("vec", 1), ("mod", 1), ("ctr", 2), ("iw", 1), ("dots", 24), ("lag", 1), ("w1", 8), ("shift", 8), ("state", 4),
                 ("y", 4), ("z", 2), ("att", 64), ("ya", 4), ("fmod", 12), ("modg", 1), ("down", 3)])
SLOW = count_up([("rms0", 1), ("pv", 4), ("rms1", 1), ("rms2", 1), ("down", 1), ("rms3", 1)])


def s_use(i):
    return SIDE["att"] + max(2 * i - 1, 0)


def pt_use(i):
    return SIDE["att"] + min(2 * i + 2, 2 * NT * HA - 1)


PE_GLA = {3: ("kt", 0), 4: ("kt", 1), 6: ("gatt", 0), 7: ("gatt", 1), 8: ("gatt", 2), 9: ("gatt", 3), 11: ("kv", 0),
          12: ("kv", 1), 20: ("o", 0), 21: ("o", 1), 22: ("o", 2), 23: ("o", 3), 28: ("ot", 0), 29: ("ot", 1),
          30: ("ot", 2), 31: ("ot", 3)}
ACT_GLA = {0: ("decay", 0), 4: ("kt", 0), 5: ("kt", 1), 21: ("o", 0), 22: ("o", 1), 23: ("o", 2), 24: ("o", 3),
           25: ("root", 0)}
DVE_GLA = {1: ("decay", 0), 8: ("gatt", 0), 9: ("gatt", 1), 10: ("gatt", 2), 11: ("gatt", 3), 12: ("kv", 0),
           13: ("kv", 1), 14: ("kv", 2), 15: ("kv", 3), 16: ("kv", 4), 17: ("kv", 5), 18: ("kv", 6), 21: ("sum", 0),
           22: ("sum", 1), 23: ("sum", 2), 24: ("sum", 3), 25: ("inverse", 0), 26: ("norm", 0), 27: ("norm", 1),
           29: ("out", 0), 30: ("out", 1), 31: ("out", 2), 32: ("out", 3)}


MOD_DVE = (0, 1, 2, 4, 5, 6, 7)


def dots_after(a):
    return range(3 * (a - 4), 3 * (a - 3)) if a >= 4 else range(0)


DOWN_ORDER = (7, 4, 5, 6, 0, 1, 2, 3)


class Steps:

    def __init__(self, eng, sem):
        self.eng, self.sem, self.n = eng, sem, 0

    def do(self, ins):
        ins.then_inc(self.sem, 1)
        self.n += 1

    def settle(self):
        self.eng.wait_ge(self.sem, self.n)


def trunk_kernel(nc, x, c, mix_mod_w, mix_mod_b, mix_pre_g, mix_post_g, w_in, s5_lam_re, s5_lam_im, s5_log_dt,
                 s5_b_re, s5_b_im, s5_c_re, s5_c_im, s5_d, s5_w_glu, gla_w_gate, gla_b_gate, gla_norm_g, w_branch,
                 w_out, ffn_mod_w, ffn_mod_b, ffn_pre_g, ffn_post_g, ffn_w_up, ffn_conv_w, ffn_conv_b, ffn_w_down,
                 out):
    ctx = ExitStack()
    with ctx:
        def sb(name, shape, dt=F32):
            return ctx.enter_context(nc.sbuf_tensor(name, shape, dt))

        def sem(name):
            return ctx.enter_context(nc.semaphore(name))

        def sems(name, n):
            return [sem(f"{name}{i}") for i in range(n)]

        with ExitStack() as early:
            def region(stack, name, shape, dt=F32):
                return stack.enter_context(nc.sbuf_tensor(name, shape, dt))

            ring = region(early, "ring", [P, RING, NK * SW])
            ys = region(early, "ys", [P, NBR, NB, T])
            hT = region(early, "hT", [P, NK, T])
            arena = region(early, "arena", [P, 12288])
            a_w1t = region(early, "a_w1t", [P, 4352])[:, :]
            a_ph = region(early, "a_ph", [P, 2048])[:, :]
            a_tmp = region(early, "a_tmp", [P, 2048])[:, :]
            a_s5 = region(early, "a_s5", [P, 2560])[:, :]
            a_k = region(early, "a_k", [P, 2048])[:, :]
            a_v = region(early, "a_v", [P, 2048])[:, :]
            mb = region(early, "mb", [P, NT, T])
            a_idx = region(early, "a_idx", [P, 2048])[:, :]
        w_lo = sb("w_lo", [P, RING, NK * SW], F32R)
        ys_lo = sb("ys_lo", [P, NBR, NB, T], F32R)
        h_lo = sb("h_lo", [P, NK, T], F32R)
        m_lo = sb("m_lo", [P, NK, T], F32R)
        m_hi = sb("m_hi", [P, NK, T], F32R)
        fmod_slab = sb("fmod_slab", [P, NK, SW])
        ys_hi0 = sb("ys_hi0", [P, NB, T], F32R)
        sb("x_again", [P, 4352])
        w_hi = sb("w_hi", [P, 2, NK * SW], F32R)
        ff_hi = sb("ff_hi", [P, 2, 2 * T], F32R)
        sb("a_s5_rest", [P, 512])
        ys_hi1 = sb("ys_hi1", [P, NB, T], F32R)
        ys_hi2 = sb("ys_hi2", [P, NB, T], F32R)
        h_hi = sb("h_hi", [P, NK, T], F32R)
        ys_hi = (ys_hi0, ys_hi1, ys_hi2)
        h1_hi = m_lo
        w1_hi = ys_lo[:, 0:2].rearrange("p s a t -> p s (a t)")
        ff_lo = ys_lo[:, 2].rearrange("p (s a) t -> p s (a t)", s=2)
        a_w1, a_w2, a_u, a_ub, a_q = (arena[:, 0:4096], arena[:, 4096:6144], arena[:, 6144:8192],
                                      arena[:, 8192:10240], arena[:, 10240:12288])
        vT = sb("vT", [P, V_N])
        ident = sb("ident", [P, P])
        wide = sb("wide", [P, (L - 1) * SP_ + P])
        mean = sb("mean", [P, P])
        chunkmask = sb("chunkmask", [P, P])
        csil = sb("csil", [P, NK])
        c_col = sb("c_col", [P, NK])
        csil_d = sb("csil_d", [P, NK])
        eps = sb("eps", [P, 2])
        mod = sb("mod", [P, 24])
        fmod = sb("fmod", [P, 24])
        pre = sb("pre", [P, NK])
        post = sb("post", [P, NK])
        fpre = sb("fpre", [P, NK])
        fpost = sb("fpost", [P, NK])
        a_wk = sb("a_wk", [P, 1536])[:, :]
        stat = sb("stat", [P, 64])
        amax = sb("amax", [P, NT, HA])
        asum = sb("asum", [P, NT, HA])
        cs = sb("cs", [P, 3, 4, 4])
        iw = sb("iw", [P, NT, HI])
        wgate = sb("wgate", [RANK, GH * GDK])
        cT = sb("cT", [P, 3, GP, SP_])
        apw = sb("apw", [P, 2, GP, L + 1])
        sc = sb("sc", [P, 28, GP])
        gemv = sb("gemv", [P, 2, SW])

        bank = [ctx.enter_context(nc.psum_tensor(f"bank{i}", [P, 512], F32)) for i in range(8)]
        x_keep = nc.dram_tensor("x_keep", (P, NK, T), F32).ap()
        u_dram = nc.dram_tensor("u_dram", (SG, SP_, L, NM), F32).ap()
        y_dram = nc.dram_tensor("y_dram", (SG, SP_, L, NM), F32).ap()

        def tiles(region, n):
            return region.rearrange("p (a t) -> p a t", a=n)

        q_sb, k_sb, v_sb = tiles(a_q, NB), tiles(a_k, NB), tiles(a_v, NT)
        q_odd = ys[:, 0]
        vrow = a_k[:, 0:3 * P].rearrange("p (a b) -> p a b", a=3)
        wsmall = a_k[:, 512:512 + NK * 152].rearrange("p (k n) -> p k n", k=NK)
        c_row = a_k[0:NK, 1792:1792 + P]
        xtok = a_w1t[:, 0:4096].rearrange("p (a d) -> p a d", a=NT)
        xT = tiles(a_w1, NK)
        sq = tiles(a_wk[:, 0:1024], 2)
        rb = a_wk[:, 1024:1536]
        iqT, ikT, lrT = tiles(a_idx[:, 0:1024], 2), a_idx[:, 1024:1536], a_idx[0:RANK + HI, 1536:2048]
        relu, work = tiles(a_wk[:, 0:1024], 2), a_wk[:, 1024:1536]
        uP = a_u.rearrange("p (a j m) -> p a j m", a=NB, j=L)
        ub = a_ub.rearrange("p (g m) -> p g m", g=SG)
        w1T = a_w1t[:, 0:4096].rearrange("p (c g i q) -> p c g i q", c=2, g=GP, i=L)
        zst = a_w1t[:, 0:2048].rearrange("p (c g m) -> p c g m", c=2, g=GP)
        xst = a_w1t[:, 2048:2048 + 2 * GP * (NM + 1)].rearrange("p (c g m) -> p c g m", c=2, g=GP)
        w1 = a_w1.rearrange("p (c g n) -> p c g n", c=2, g=GP)
        w2 = [ys[:, 2].rearrange("p a t -> p (a t)").rearrange("p (g j q) -> p g j q", g=GP, j=L),
              a_w2.rearrange("p (g j q) -> p g j q", g=GP, j=L)]
        toep = ys[:, 0:2].rearrange("p b a t -> p (b a t)").rearrange("p (g j q) -> p g j q", g=SG, j=L)
        cpair = a_idx[:, 0:1024].rearrange("p (c g d q) -> p c g d q", c=2, g=GP, d=2)
        ph = a_ph.rearrange("p (c g m) -> p c g m", c=2, g=GP)
        yblk = a_tmp.rearrange("p (g m) -> p g m", g=SG)
        yback = tiles(a_ph, NB)
        rho = a_s5[:, 0:1024].rearrange("p (g m) -> p g m", g=GP)
        brow = a_s5[:, 1024:1536].rearrange("p (c g q) -> p c g q", c=2, g=GP)
        bb = a_s5[:, 1536:2048].rearrange("p (c g q) -> p c g q", c=2, g=GP)
        lag = a_s5[:, 2048:2560]
        crow = a_q[:, 0:1024].rearrange("p (c r d n) -> p c r d n", c=2, r=4, d=2)
        gq, gk, cum, e1 = (tiles(a_w1[:, 1024 * i:1024 * i + 1024], 2) for i in range(4))
        e2, e3 = (tiles(a_w1t[:, 1024 * i:1024 * i + 1024], 2) for i in range(2))
        ktok = a_w1t[:, 2048:3072].rearrange("p (a d) -> p a d", a=NT)
        tail = tiles(a_w1t[:, 3072:4096], 2)
        gv, sr, og = tiles(a_ub, NT), tiles(a_w2, GH), tiles(a_u, NT)
        sprev = ys[:, 2].rearrange("p a t -> p (a t)").rearrange("p (a c e) -> p a c e", a=2, c=NC)
        gatt = a_tmp.rearrange("p (h t q) -> p h t q", h=GH, t=NT)
        keep, osq = a_s5[:, 0:512], a_s5[:, 512:1024]
        logit, prob = tiles(a_idx[:, 0:1024], 2), tiles(a_wk[:, 0:1024], 2)
        probT = tiles(a_s5[:, 1536:2560], 2)
        ytok = tiles(a_ph, NT)
        merged, x1 = tiles(a_w1, NK), a_w1t[:, 0:4096].rearrange("p (k t) -> p k t", k=NK)
        modg_slab = a_v.rearrange("p (k n) -> p k n", k=NK)
        msig, mtmp = tiles(a_wk[:, 0:1024], 2), a_wk[:, 1024:1536]
        yT = ys[:, 0:2].rearrange("p b a t -> p (b a) t")
        ff = tiles(arena[:, 0:NF * T], NF)
        cb, gl = tiles(a_k, 4), tiles(a_v[:, 0:1024], 2)
        xo = arena[:, 0:NT * D].rearrange("p (t d) -> p t d", t=NT)
        slab_in = sems("slab_in", RING)
        slab_used = sem("slab_used")
        w_top, w_ready = sem("w_top"), sem("w_ready")
        w1_top, w1_ready = sem("w1_top"), sem("w1_ready")
        h1_top, h1_split = sem("h1_top"), sem("h1_split")
        h_back = sem("h_back")
        cpair_ready = sem("cpair_ready")
        q_pad = sem("q_pad")
        half_top, half_ready = sem("half_top"), sem("half_ready")
        h_top, h_split = sem("h_top"), sem("h_split")
        y0_whole, y0_split = sem("y0_whole"), sem("y0_split")
        y_top, y_split = sem("y_top"), sem("y_split")
        m_split = sem("m_split")
        h2_top, h2_ready = sem("h2_top"), sem("h2_ready")
        ff_top, ff_split = sem("ff_top"), sem("ff_split")
        fmod_in, modg_in = sem("fmod_in"), sems("modg_in", 2)
        fmod_used = sem("fmod_used")
        mod_k, gemv_k = sem("mod_k"), sem("gemv_k")
        acc_done = sem("acc_done")
        acc_out = sems("acc_out", 4)
        side_done = sem("side_done")
        side_out = sems("side_out", 3)
        slow_done = sem("slow_done")
        slow_out = sem("slow_out")
        vstep, astep, gstep = sem("vstep"), sem("astep"), sem("gstep")
        c_row_in = sem("c_row_in")
        x_in, vec_in, c_in, b_in, dt_in, small_in = (sem(n) for n in (
            "x_in", "vec_in", "c_in", "b_in", "dt_in", "small_in"))
        x_kept, x_back, u_store, ub_in, y_store, y_in, out_st = (sem(n) for n in (
            "x_kept", "x_back", "u_store", "ub_in", "y_store", "y_in", "out_st"))
        consts = sem("consts")
        sq_used = sem("sq_used")
        rinv = sem("rinv")
        y_copied = sem("y_copied")
        sq_ready = sem("sq_ready")
        c_sig, c_silu = sem("c_sig"), sem("c_silu")
        mod_ready = sem("mod_ready")
        hx, h_ready = sem("hx"), sem("h_ready")
        dt_exp, s5_ang, s5_trig, s5_pow = sem("dt_exp"), sem("s5_ang"), sem("s5_trig"), sem("s5_pow")
        s5_tables, w2_ready = sem("s5_tables"), sem("w2_ready")
        score_mul = sem("score_mul")
        score_masked = sem("score_masked")
        mask0_ready, mask_ready = sem("mask0_ready"), sem("mask_ready")
        state_ready = sem("state_ready")
        yd_ready, g_ready = sem("yd_ready"), sem("g_ready")
        p_ready = sem("p_ready")
        r_sig = sem("r_sig")
        f_abs, f_exp, f_cum, f_tail = sem("f_abs"), sem("f_exp"), sem("f_cum"), sem("f_tail")
        g_zero, g_dec, g_k = sem("g_zero"), sem("g_dec"), sem("g_k")
        carried = sem("carried")
        o_sum, o_root, o_inv, o_norm = sem("o_sum"), sem("o_root"), sem("o_inv"), sem("o_norm")
        merge_sum = sem("merge_sum")
        fmod_ready = sem("fmod_ready")
        x1_ready, x2_ready = sem("x1_ready"), sem("x2_ready")
        taps = sem("taps")
        conv_0, conv_1, gelu_out, ff_ready = sem("conv_0"), sem("conv_1"), sem("gelu_out"), sem("ff_ready")

        def acc(n):
            return bank[n % 4]

        def side(n):
            return bank[4 + n % 3]

        slow = bank[7]

        def acc_read(eng, n):
            eng.wait_ge(acc_done, n + 1)

        def acc_copied(eng, n):
            eng.wait_ge(acc_out[n % 4], n // 4 + 1)

        def side_read(eng, n):
            eng.wait_ge(side_done, n + 1)

        def side_copied(eng, n):
            eng.wait_ge(side_out[n % 3], n // 3 + 1)

        def slow_read(eng, n):
            eng.wait_ge(slow_done, n + 1)

        def slow_copied(eng, n):
            eng.wait_ge(slow_out, n + 1)

        def down_bank(m):
            if m < 4:
                return acc(ACC["down"] + m)
            return side(SIDE["down"] + m - 4) if m < 7 else slow

        def slab_k(s, cols=SW):
            return ring[:, s % RING, :].rearrange("p (k n) -> p k n", n=cols)

        def rows(w):
            return w.rearrange("(k p) n -> p k n", p=P)

        def split_no(s):
            return s - SLAB["merge"]

        def slot(s):
            return (split_no(s) + 1) % 2

        def first_no(s):
            return s - SLAB["iq"]

        block = ctx.enter_context(nc.Block())

        def o_part(b):
            return og[:, 2 * (b // 2):2 * (b // 2) + 2, :].rearrange("p t (h d e) -> p t d h e", h=2, d=2)[:, :, b % 2]

        @block.sync
        def _(sp):
            def load(s, view, src):
                if s >= RING:
                    sp.wait_ge(slab_used, s - RING + 1)
                sp.dma_start(view, src).then_inc(slab_in[s % RING], 16)

            def slabs(name, w, col, n):
                for j in range(n):
                    load(SLAB[name] + j, slab_k(SLAB[name] + j), rows(w[:, col + SW * j:col + SW * j + SW]))

            def half_slabs(name, w, col):
                for j in range(2):
                    load(SLAB[name] + j, slab_k(SLAB[name] + j, BW), rows(w[BW * j:BW * j + BW, col:col + BW]))

            sp.dma_start(c_row, c[0].rearrange("(a b) -> a b", b=P)).then_inc(c_row_in, 16)
            win = w_in[0]
            slabs("mod", mix_mod_w[0], 0, 8)
            slabs("iq", win, C_IQ, 1)
            slabs("u", win, C_U, 2)
            slabs("q", win, C_AQ, 2)
            slabs("k", win, C_AK, 2)
            half_slabs("v", win, C_AV)
            slabs("gq", win, C_GQ, 1)
            slabs("gk", win, C_GK, 1)
            half_slabs("gv", win, C_GV)
            slabs("gr", win, C_GR, 2)
            for j in range(2):
                load(SLAB["glu"] + j, slab_k(SLAB["glu"] + j, BW), rows(s5_w_glu[0][:, BW * j:BW * j + BW]))
            acc_read(sp, ACC["o"] + 3)
            sp.sem_inc(fmod_used, 1)
            with sp.Fori(1, 3) as it:
                for step in range(6):
                    jj, i = step // NBR, step % NBR
                    for m, (w, kt, col) in enumerate(((win, NK, C_GL + D * i), (w_branch[0, i], NB, 0))):
                        s = SLAB["merge"] + 2 * step + m
                        sp.wait_ge(slab_used, it * 12 + (s - RING + 1 - 12))
                        sp.dma_start(slab_k(s)[:, 0:kt, :], rows(w[:, bass.ds(it * (2 * SW) + (col + SW * (jj - 2)), SW)])
                                     ).then_inc(slab_in[s % RING], 16)
                    sp.wait_ge(fmod_used, it * 6 + (step - 5))
                    sp.dma_start(fmod_slab[:, :, :], rows(ffn_mod_w[0][:, bass.ds(it * (6 * SW) + SW * (step - 6), SW)])
                                 ).then_inc(fmod_in, 16)
            slabs("out", w_out[0], 0, 4)
            up = ffn_w_up[0]
            with sp.Fori(0, 3) as it:
                for m in range(6):
                    s, half, pair = SLAB["up"] + m, m % 2, m // 2
                    at = sp.snap(it * (3 * SW) + (FF * half + SW * pair))
                    free = sp.snap(it * 6 + (s - RING + 1))
                    sp.wait_ge(slab_used, free)
                    sp.dma_start(slab_k(s), rows(up[:, bass.ds(at, SW)])).then_inc(slab_in[s % RING], 16)
            for m in range(18, 22):
                s, col = SLAB["up"] + m, FF * (m % 2) + SW * (m // 2)
                load(s, slab_k(s), rows(up[:, col:col + SW]))
            for j in range(NF // 2):
                s = SLAB["down"] + j
                load(s, slab_k(s, D), rows(ffn_w_down[0][2 * P * j:2 * P * j + 2 * P, :]))
            for n in range(8):
                acc_copied(sp, ACC["xo"] + n)
                tok, col = slice(P * (n % NT), P * (n % NT) + P), slice(BW * (n // NT), BW * (n // NT) + BW)
                sp.dma_start(out[0, tok, col], xo[:, n % NT, col]).then_inc(out_st, 16)
            sp.wait_ge(out_st, 16 * 8)

        @block.gpsimd
        def _(pool):
            st = Steps(pool, gstep)
            st.do(pool.memset(ident[:, :], 0.0))
            st.do(pool.memset(wide[:, :], 0.0))
            st.do(pool.memset(chunkmask[:, :], 1.0))
            st.do(pool.memset(eps[:, :], EPS))
            pool.memset(mean[:, :], 1.0 / D).then_inc(consts, 1)
            st.settle()
            for m, width in ((ident, P), (wide, (L - 1) * SP_ + P)):
                pool.affine_select(out=m[:, :], in_=m[:, :], compare_op=ALU.not_equal, fill=1.0, base=0,
                                   pattern=[[-1, width]], channel_multiplier=1).then_inc(consts, 1)
            st.do(pool.affine_select(out=chunkmask[:, :], in_=chunkmask[:, :], compare_op=ALU.is_ge, fill=0.0,
                                     base=0, pattern=[[1, P]], channel_multiplier=-1))
            st.settle()
            pool.memset(chunkmask[0:GC, GC:P], 0.0).then_inc(consts, 1)
            small = rows(w_in[0])
            for half in range(2):
                for cc, w in enumerate((s5_c_re, s5_c_im)):
                    pool.dma_start(crow[:, cc, :, half, :],
                                   w[0].rearrange("(r g) p n -> (g p) r n", r=4)).then_inc(c_in, 16)
            for cc, w in enumerate((s5_b_re, s5_b_im)):
                pool.dma_start(brow[:, cc, :, :], w[0].rearrange("(g d) n p -> (d n) g p", d=2)).then_inc(b_in, 16)
            for at, col, n in ((4 * DI, C_LR, RANK), (4 * DI + RANK, C_IW, HI), *((DI * r, C_IK, DI) for r in range(4))):
                pool.dma_start(wsmall[:, :, at:at + n], small[:, :, col:col + n]).then_inc(small_in, 16)
            pool.dma_start(wgate[:, :], gla_w_gate[0]).then_inc(small_in, 16)
            for k in range(NK - 4, NK):
                acc_copied(pool, ACC["x"] + k)
            pool.dma_start(x_keep, xT).then_inc(x_kept, 16)
            pool.wait_ge(s5_pow, 1)
            side_copied(pool, SIDE["ctr"])
            side_copied(pool, SIDE["ctr"] + 1)
            for j in range(L):
                ar, ai = (apw[:, cc, :, j + 1:j + 2].broadcast_to([P, GP, SP_]) for cc in range(2))
                t = [a_v[:, 1024 * (j % 2) + 256 * i:1024 * (j % 2) + 256 * i + 256].rearrange(
                    "p (g q) -> p g q", g=GP) for i in range(4)]
                st.do(pool.tensor_tensor(t[0], cT[:, 0], ar, ALU.mult))
                st.do(pool.tensor_tensor(t[1], cT[:, 1], ai, ALU.mult))
                st.do(pool.tensor_tensor(t[2], cT[:, 0], ai, ALU.mult))
                st.do(pool.tensor_tensor(t[3], cT[:, 2], ar, ALU.mult))
                st.settle()
                st.do(pool.tensor_tensor(w2[0][:, :, j, :], t[0], t[1], ALU.subtract))
                st.do(pool.tensor_tensor(w2[1][:, :, j, :], t[3], t[2], ALU.subtract))
            pool.memset(mb[:, 0, 0:P], 0.0).then_inc(w2_ready, 1)
            pool.wait_ge(w2_ready, 1)
            pool.affine_select(out=mb[:, 0, 0:P], in_=mb[:, 0, 0:P], compare_op=ALU.is_ge, fill=-BIG, base=0,
                               pattern=[[-1, P]], channel_multiplier=1).then_inc(mask0_ready, 1)
            for a in range(NB):
                acc_copied(pool, ACC["u"] + a)
            pool.dma_start(u_dram.rearrange("(a g) p j m -> (g p) a (j m)", a=NB),
                           a_u.rearrange("p (a t) -> p a t", a=NB)).then_inc(u_store, 16)
            pool.wait_ge(u_store, 16)
            pool.wait_ge(x_kept, 16)
            for j in range(L):
                pool.dma_start(ub[SP_ * j:SP_ * j + SP_, :, :],
                               u_dram[:, :, j, :].rearrange("g p m -> p g m")).then_inc(ub_in, 16)
            for tt in range(1, NT):
                pool.wait_ge(score_mul, HI * tt)
                d = mb[:, tt, P * tt:P * tt + P]
                pool.affine_select(out=d, in_=d, compare_op=ALU.is_ge, fill=NEVER, base=0,
                                   pattern=[[-1, P]], channel_multiplier=1).then_inc(score_masked, 1)
            st.do(pool.memset(cpair, 0.0))
            st.settle()
            for cc in range(2):
                for d in range(2):
                    part = slice(SN * d, SN * d + SN)
                    pool.tensor_copy(cpair[part, cc, :, d, :], cT[part, 2 * cc]).then_inc(cpair_ready, 1)
            pool.wait_ge(cpair_ready, 4)
            acc_read(pool, ACC["v"] + NT - 1)
            for k in range(NK):
                pool.tensor_tensor(hT[:, k], h1_hi[:, k].bitcast(F32), h_lo[:, k].bitcast(F32), ALU.add
                                   ).then_inc(h_back, 1)
            for b in range(4):
                side_copied(pool, SIDE["y"] + b)
            for j in range(L):
                pool.dma_start(y_dram[:, :, j, :].rearrange("g p m -> p g m"),
                               yblk[SP_ * j:SP_ * j + SP_, :, :]).then_inc(y_store, 16)
            pool.wait_ge(y_store, 16 * L)
            pool.dma_start(yback, y_dram.rearrange("(a g) p j m -> (g p) a (j m)", a=NB)).then_inc(y_in, 16)
            st.do(pool.tensor_copy(q_odd[SN:P], q_sb[SN:P]))
            st.settle()
            pool.memset(q_odd[0:SN], 0.0).then_inc(q_pad, 1)
            pool.wait_ge(q_pad, 1)
            pool.memset(q_sb[SN:P], 0.0).then_inc(q_pad, 1)
            pool.wait_ge(q_pad, 2)
            pool.memset(a_tmp, 0.0).then_inc(g_zero, 1)
            pool.memset(sprev[:, :, 0, :], 0.0).then_inc(g_zero, 1)
            st.do(pool.memset(keep, 1.0))
            st.settle()
            pool.memset(keep.rearrange("p (c t) -> p c t", c=NC)[:, :, 0:1], 0.0).then_inc(g_zero, 1)
            acc_copied(pool, ACC["ot"])
            pool.dma_start(x1, x_keep).then_inc(x_back, 16)
            side_copied(pool, s_use(NT * HA - 1))
            slow_read(pool, SLOW["pv"] + NT - 1)
            for i in range(1, NBR):
                if i == 1:
                    acc_copied(pool, ACC["glu"] + 6)
                else:
                    for h in range(GH):
                        acc_copied(pool, ACC["ot"] + h)
                pool.tensor_copy(ys_hi[i][:, :, :], ys[:, i]).then_inc(y_top, 1)
                pool.wait_ge(y_top, i)
                pool.tensor_tensor(ys_lo[:, i], ys[:, i], ys_hi[i][:, :, :].bitcast(F32), ALU.subtract
                                   ).then_inc(y_split, 1)
            for j in range(4):
                pool.wait_ge(fmod_used, max(13, 12 + j))
                pool.dma_start((fmod_slab[:, :, :], modg_slab)[j % 2], rows(mix_mod_w[0][:, 2 * D + SW * j:2 * D + SW * j + SW])
                               ).then_inc(modg_in[j % 2], 16)
            cols = vT[:, V_CW:V_CW + 8 * NF].rearrange("p (j h n) -> p j h n", j=4, h=2)
            dst = [cs[:, s].rearrange("p j (h n) -> p j h n", h=2) for s in range(3)]
            for s in range(3):
                pool.tensor_copy(dst[s], cols[:, :, :, 2 * s:2 * s + 2]).then_inc(taps, 1)
            with pool.Fori(1, 3) as it:
                for s in range(3):
                    n = ACC["up"] + 4 * s - 9
                    pool.wait_ge(acc_out[n % 4], it * 3 + (n // 4 + 1))
                    pool.tensor_copy(dst[s], cols[:, :, :, bass.ds(it * 6 + 2 * s, 2)]).then_inc(taps, 1)
            for s in range(2):
                acc_copied(pool, ACC["up"] + 4 * (6 + s) + 3)
                pool.tensor_copy(dst[s], cols[:, :, :, 18 + 2 * s:20 + 2 * s]).then_inc(taps, 1)

        @block.scalar
        def _(act):
            st = Steps(act, astep)

            def copy(dst, src, signal, scale=1.0):
                act.activation(dst, src, ACT.Copy, scale=scale).then_inc(signal, 1)

            def acc_copy(n, dst, src=None, scale=1.0):
                acc_read(act, n)
                copy(dst, acc(n)[:, :] if src is None else src, acc_out[n % 4], scale)

            def side_copy(n, dst, src=None, scale=1.0):
                side_read(act, n)
                copy(dst, side(n)[:, :] if src is None else src, side_out[n % 3], scale)

            def squares(k, src, norm, signal):
                if k >= 2:
                    act.wait_ge(sq_used, (NK - 1) * norm + k - 1)
                act.activation(sq[:, k % 2], src, ACT.Square).then_inc(signal, 1)

            def root(name):
                slow_read(act, SLOW[name])
                act.activation(rb, slow[:, :], ACT.Sqrt, bias=eps[:, 0:1]).then_inc(slow_out, 1)

            at = 0
            for v, n in ((mix_mod_b, 24), (mix_pre_g, 8), (mix_post_g, 8), (s5_d, 4), (gla_b_gate, 2),
                         (gla_norm_g, 4), (ffn_mod_b, 24), (ffn_pre_g, 8), (ffn_post_g, 8)):
                src = v[0] if n != 4 or v.shape[-1] != GDV else v[0].rearrange("a b -> (a b)")
                act.dma_start(vrow[at:at + n, 0, :], src.rearrange("(a b) -> a b", b=P)).then_inc(vec_in, 16)
                at += n
            taps_rows = ffn_conv_w[0].rearrange("j (n b) -> (j n) b", b=P)
            act.dma_start(vrow[:, 1, :], taps_rows[0:P, :]).then_inc(vec_in, 16)
            act.dma_start(vrow[0:4, 2, :], taps_rows[P:P + 4, :]).then_inc(vec_in, 16)
            act.dma_start(vrow[4:48, 2, :], ffn_conv_b[0].rearrange("(n b) -> n b", b=P)).then_inc(vec_in, 16)
            for i, v in enumerate((s5_lam_re, s5_lam_im)):
                act.dma_start(vrow[48 + 16 * i:64 + 16 * i, 2, :],
                              v[0].rearrange("(g d) n -> g (d n)", d=2)).then_inc(vec_in, 16)
            act.dma_start(xtok, x[0].rearrange("(a p) d -> p a d", p=P)).then_inc(x_in, 16)
            log_dt = sc[:, 24:26, :].rearrange("p a g -> p (a g)")
            act.dma_start(log_dt, s5_log_dt[0].partition_broadcast(P)).then_inc(dt_in, 16)

            side_copy(SIDE["c"], c_col[:, :], side(SIDE["c"])[:, 0:NK])
            side_copied(act, SIDE["c"])
            act.activation(csil[:, :], c_col[:, :], ACT.Sigmoid).then_inc(c_sig, 1)
            side_copy(SIDE["vec"], vT[:, :], side(SIDE["vec"])[:, 0:V_N])
            act.wait_ge(dt_in, 16)
            for d in range(2):
                part = slice(SN * d, SN * d + SN)
                act.activation(sc[part, 1, :], log_dt[part].rearrange("p (g d) -> p d g", d=2)[:, d, :], ACT.Exp
                               ).then_inc(dt_exp, 1)
            for k in range(NK):
                n = ACC["x"] + k
                acc_read(act, n)
                st.do(act.activation(xT[:, k], acc(n)[:, :], ACT.Copy))
                squares(k, acc(n)[:, :], 0, acc_out[n % 4])
            root("rms0")
            act.wait_ge(mod_ready, 1)
            for k in range(NK):
                act.wait_ge(hx, k + 1)
                act.activation(hT[:, k], hT[:, k], ACT.Identity, scale=pre[:, k:k + 1],
                               bias=mod[:, k:k + 1]).then_inc(h_ready, 1)

            def first_top(s):
                act.wait_ge(slab_in[s % RING], 16 * (s // RING + 1))
                if first_no(s) >= 2:
                    act.wait_ge(slab_used, s - 1)
                act.activation(w1_hi[:, first_no(s) % 2], ring[:, s % RING], ACT.Copy).then_inc(w1_top, 1)

            act.wait_ge(x_kept, 16)
            act.wait_ge(h_ready, NK)
            for k in range(NK):
                copy(h1_hi[:, k], hT[:, k], h1_top)
            first_top(SLAB["iq"])
            for cc in range(2):
                n = SIDE["ctr"] + cc
                side_read(act, n)
                for d in range(2):
                    part = slice(SN * d, SN * d + SN)
                    src = side(n)[part, :].rearrange("p (r d q) -> p r d q", d=2, q=SP_)[:, :, d, :]
                    if cc:
                        st.do(act.activation(cT[part, 2], src, ACT.Copy, scale=-1.0))
                    if d:
                        copy(cT[part, cc], src, side_out[n % 3])
                    else:
                        st.do(act.activation(cT[part, cc], src, ACT.Copy))
            act.wait_ge(s5_ang, 1)
            act.activation(sc[:, 4, :], sc[:, 2, :], ACT.Exp).then_inc(s5_trig, 1)
            act.wait_ge(s5_ang, 2)
            act.activation(sc[:, 6, :], sc[:, 7, :], ACT.Sin).then_inc(s5_trig, 1)
            act.activation(sc[:, 5, :], sc[:, 3, :], ACT.Sin).then_inc(s5_trig, 1)
            acc_copy(ACC["lr"], lrT, acc(ACC["lr"])[0:RANK + HI, :])
            acc_copy(ACC["ik"], ikT)
            first_top(SLAB["u"])
            for a in range(2):
                acc_copy(ACC["iq"] + a, iqT[:, a])
            side_copy(SIDE["iw"], iw[:, :, :], side(SIDE["iw"])[:, 0:NT * (RANK + HI)].rearrange(
                "p (t h) -> p t h", t=NT)[:, :, RANK:], (HI * DI) ** -0.5)
            for a in range(3 * NB):
                if a % 2:
                    first_top(SLAB["u"] + a // 2 + 1)
                name, i = ("u", "q", "k")[a // NB], a % NB
                n = ACC[name] + i
                if name == "u":
                    acc_copy(n, uP[:, i], acc(n)[:, :].rearrange("p (m j) -> p j m", j=L))
                else:
                    acc_copy(n, (q_sb if name == "q" else k_sb)[:, i])
                for d in dots_after(a):
                    side_read(act, SIDE["dots"] + d)
                    if d >= 2:
                        act.wait_ge(score_mul, d - 1)
                    w = P * (2 + d // HI)
                    act.activation(relu[:, d % 2, 0:w], side(SIDE["dots"] + d)[:, 0:w], ACT.Relu
                                   ).then_inc(side_out[(SIDE["dots"] + d) % 3], 1)
            first_top(SLAB["v"] + 1)
            act.wait_ge(w2_ready, 1)
            for a in range(NT):
                acc_copy(ACC["v"] + a, v_sb[:, a])
            side_copy(SIDE["lag"], lag)
            act.wait_ge(h_back, NK)
            for b in range(8):
                cc, g = b // 4, 4 * (b % 4)
                side_copy(SIDE["w1"] + b, w1[:, cc, g:g + 4, :].rearrange("p g n -> p (g n)"))
            for j in range(L):
                n = SIDE["shift"] + j
                side_copy(n, toep[:, :, j, :], side(n)[:, :].rearrange("p (g q) -> p g q", g=SG))
            act.wait_ge(state_ready, 1)
            for b in range(4):
                side_copy(SIDE["y"] + b, yblk.rearrange("p (g d) m -> p d g m", d=2)[:, b % 2, 8 * (b // 2):8 * (b // 2) + 8],
                          side(SIDE["y"] + b)[:, :].rearrange("p (g m) -> p g m", g=8))
            for name, dst, n in (("gq", gq, 2), ("gk", gk, 2), ("gv", gv, 4)):
                for a in range(n):
                    acc_copy(ACC[name] + a, dst[:, a])
            for a in range(NB):
                act.wait_ge(yd_ready, a + 1)
                act.activation(yback[:, a], yback[:, a], ACT.Gelu_apprx_tanh).then_inc(g_ready, 1)
            for a in range(GH):
                acc_read(act, ACC["gr"] + a)
                act.activation(sr[:, a], acc(ACC["gr"] + a)[:, :], ACT.Sigmoid).then_inc(r_sig, 1)
            for a in range(2):
                n = SIDE["z"] + a
                side_read(act, n)
                act.activation(e1[:, a], side(n)[:, :], ACT.Abs, bias=vT[:, V_GB + a:V_GB + a + 1]).then_inc(f_abs, 1)
            act.wait_ge(f_abs, 2)
            act.activation(e1, e1, ACT.Exp, scale=-1.0).then_inc(f_exp, 1)
            act.wait_ge(f_exp, 1)
            act.activation(e1, e1, ACT.Ln, bias=1.0).then_inc(f_exp, 1)
            for a in range(NB):
                n = ACC["glu"] + 2 * a + 1
                acc_read(act, n)
                if a >= 2:
                    acc_copied(act, n - 5)
                act.activation(msig[:, a % 2], acc(n)[:, :], ACT.Sigmoid).then_inc(acc_out[n % 4], 1)
            acc_copied(act, ACC["glu"] + 6)
            def gla(part, b):
                if part == "decay":
                    act.wait_ge(f_cum, 2)
                    act.activation(e1, cum, ACT.Exp, scale=1.0 / TAU).then_inc(g_dec, 1)
                    act.activation(e2, cum, ACT.Exp, scale=-1.0 / TAU).then_inc(g_dec, 1)
                    act.wait_ge(f_tail, 1)
                    act.activation(e3, tail, ACT.Exp, scale=1.0 / TAU).then_inc(g_dec, 1)
                elif part == "kt":
                    n = ACC["kt"] + b
                    acc_copy(n, ktok[:, :, P * b:P * b + P], acc(n)[:, :].rearrange("p (t d) -> p t d", t=NT))
                elif part == "o":
                    n = ACC["o"] + b
                    acc_read(act, n)
                    st.do(act.activation(o_part(b), acc(n)[:, :].rearrange("p (t h e) -> p t h e", t=2, h=2), ACT.Copy))
                    if b:
                        act.wait_ge(o_sum, b)
                    act.activation(osq, acc(n)[:, :], ACT.Square).then_inc(acc_out[n % 4], 1)
                else:
                    act.wait_ge(o_sum, NT + 1)
                    act.activation(stat[:, 16:32], stat[:, 16:32], ACT.Sqrt).then_inc(o_root, 1)

            def load_root():
                act.activation(eps[:, 1:2], eps[:, 0:1], ACT.Sqrt).then_inc(astep, 1)
                st.n += 1

            def top(s, per=0, it=0, kt=NK):
                act.wait_ge(slab_in[s % RING], it * (16 * per // RING) + 16 * (s // RING + 1))
                if split_no(s) >= 2:
                    act.wait_ge(slab_used, it * per + (s - 1))
                act.activation(w_hi[:, slot(s), 0:kt * SW], ring[:, s % RING, 0:kt * SW], ACT.Copy
                               ).then_inc(w_top, 1)

            for i in range(NT * HA + 1):
                if i < NT * HA:
                    tt, h = i // HA, i % HA
                    w = P * (tt + 1)
                    side_copied(act, s_use(i))
                    if i >= 2:
                        side_read(act, pt_use(i - 2))
                    act.activation(prob[:, i % 2, 0:w], logit[:, i % 2, 0:w], ACT.Exp, scale=-1.0,
                                   bias=amax[:, tt, h:h + 1], accum_out=asum[:, tt, h:h + 1]).then_inc(p_ready, 1)
                if i >= 1:
                    n, w = pt_use(i - 1), P * ((i - 1) // HA + 1)
                    side_copy(n, probT[:, (i - 1) % 2, 0:w], side(n)[:, 0:w])
                if i in ACT_GLA:
                    gla(*ACT_GLA[i])
            side_copied(act, s_use(NT * HA - 1))
            top(SLAB["merge"])
            for tt in range(NT):
                for k in (2 * tt, 2 * tt + 1):
                    copy(h_hi[:, k], hT[:, k], h_top)
                n = SIDE["ya"] + tt
                side_read(act, n)
                src, tok = side(n)[:, :].rearrange("p (a q) -> p a q", a=NB), slice(P * tt, P * tt + P)
                copy(ys[:, 0, :, tok], src, y0_whole)
                copy(ys_hi0[:, :, tok], src, side_out[n % 3])
            top(SLAB["merge"] + 1, kt=NB)
            with act.Fori(0, 2) as it:
                for step in range(6):
                    for q in range(2):
                        n = ACC["merge"] + 4 * step + q
                        act.wait_ge(acc_done, it * 24 + (n + 1))
                        act.wait_ge(acc_out[(n - 2) % 4], it * 6 + ((n - 2) // 4 + 1))
                        act.activation(msig[:, q], acc(n)[:, :], ACT.Sigmoid).then_inc(acc_out[n % 4], 1)
                    s = SLAB["merge"] + 2 * step + 2
                    top(s, 12, it)
                    top(s + 1, 12, it, NB)
            act.wait_ge(slab_in[(s + 1) % RING], 16 * ((SLAB["out"] + 1) // RING + 1))
            act.activation(w_hi[:, slot(s + 1), NB * SW:], ring[:, (s + 1) % RING, NB * SW:], ACT.Copy).then_inc(half_top, 1)
            for k in range(NK):
                n = ACC["out"] + k
                acc_read(act, n)
                if k == NK - 1:
                    load_root()
                if k < 2:
                    acc_copied(act, ACC["merge"] + 46 + k)
                squares(k, acc(n)[:, :], 1, acc_out[n % 4])
                copy(yT[:, k], acc(n)[:, :], y_copied)
                if k % 2 and k < NK - 1:
                    top(SLAB["out"] + 2 + k // 2)
            root("rms1")
            for k in range(NK):
                act.wait_ge(x1_ready, k + 1)
                if k < 2:
                    slow_read(act, SLOW["rms1"])
                squares(k, x1[:, k], 2, sq_ready)
            root("rms2")
            act.wait_ge(fmod_ready, 1)
            for k in range(NK):
                act.wait_ge(hx, NK + k + 1)
                for dst in (h_hi, hT):
                    act.activation(dst[:, k], hT[:, k], ACT.Identity, scale=fpre[:, k:k + 1],
                                   bias=fmod[:, k:k + 1]).then_inc(h2_top, 1)

            top(SLAB["up"] + 1)
            act.sem_inc(gelu_out, 2)

            def up_pair(it, pair, s):
                act.wait_ge(taps, it * 3 + (pair + 1))
                slab = SLAB["up"] + 2 * pair + 2
                for r in range(4):
                    n = ACC["up"] + 4 * pair + r
                    act.wait_ge(acc_done, it * 12 + (n + 1))
                    act.wait_ge(gelu_out if r < 2 else ff_ready, it * 6 + (2 * pair + r % 2 + 1))
                    act.activation(cb[:, r], acc(n)[:, :], ACT.Identity, scale=cs[:, s, 2, r:r + 1],
                                   bias=cs[:, s, 3, r:r + 1]).then_inc(conv_0, 1)
                    if r == 1:
                        top(slab, 6, it)
                        for q in range(2):
                            n = ACC["up"] + 4 * pair + q
                            act.wait_ge(acc_out[n % 4], it * 3 + (n // 4 + 1))
                            act.wait_ge(ff_ready, it * 6 + (2 * pair + q + 1))
                            act.activation(gl[:, q], cb[:, q], ACT.Gelu_apprx_tanh).then_inc(gelu_out, 1)
                top(slab + 1, 6, it)

            def ff_top_part(j):
                act.wait_ge(ff_ready, 2 + 2 * j + 2)
                act.activation(ff_hi[:, j % 2], arena[:, 2 * T * j:2 * T * j + 2 * T], ACT.Copy).then_inc(ff_top, 1)

            with act.Fori(0, 3) as it:
                for s in range(3):
                    up_pair(it, s, s)
            up_pair(0, 9, 0)
            for j in range(2):
                ff_top_part(j)
            up_pair(0, 10, 1)
            for j in range(2, NF // 2):
                top(SLAB["down"] + j)
                ff_top_part(j)
            load_root()
            for i, m in enumerate(DOWN_ORDER):
                if m < 4:
                    acc_read(act, ACC["down"] + m)
                    signal = acc_out[(ACC["down"] + m) % 4]
                elif m < 7:
                    side_read(act, SIDE["down"] + m - 4)
                    signal = side_out[(SIDE["down"] + m - 4) % 3]
                else:
                    slow_read(act, SLOW["down"])
                    signal = slow_out
                if i < 2:
                    slow_read(act, SLOW["rms2"])
                squares(i, down_bank(m)[:, :], 3, signal)
            root("rms3")
            for n in (0, 1, 2, 3, 5, 7):
                acc_copy(ACC["xo"] + n, xo[:, n % NT, BW * (n // NT):BW * (n // NT) + BW])

        @block.vector
        def _(dve):
            st = Steps(dve, vstep)
            tt_, ts, stt = dve.tensor_tensor, dve.tensor_scalar, dve.scalar_tensor_tensor

            def cmul(out_r, out_i, ar, ai, br, bi, t):
                st.do(tt_(t[0], ar, br, ALU.mult))
                st.do(tt_(t[1], ai, bi, ALU.mult))
                st.do(tt_(t[2], ar, bi, ALU.mult))
                st.do(tt_(t[3], ai, br, ALU.mult))
                st.settle()
                st.do(tt_(out_r, t[0], t[1], ALU.subtract))
                st.do(tt_(out_i, t[2], t[3], ALU.add))

            def inverse_rms(norm, n):
                slow_copied(dve, n)
                dve.reciprocal(rb, rb).then_inc(rinv, 1)
                dve.wait_ge(rinv, norm + 1)

            def modulate(part, slab, count, signal, it=0, per=0):
                for k in range(NK):
                    if k == 0:
                        ts(part, slab[:, 0, :], csil[:, 0:1], None, ALU.mult).then_inc(signal, 1)
                    else:
                        dve.wait_ge(signal, it * per + (count + k))
                        stt(part, slab[:, k, :], csil[:, k:k + 1], part, ALU.mult, ALU.add).then_inc(signal, 1)

            side_copied(dve, SIDE["c"])
            dve.wait_ge(c_sig, 1)
            tt_(csil[:, :], csil[:, :], c_col[:, :], ALU.mult).then_inc(c_silu, 1)
            dve.wait_ge(c_silu, 1)
            ts(csil_d[:, :], csil[:, :], 1.0 / D, None, ALU.mult).then_inc(c_silu, 1)
            for i, j in enumerate(MOD_DVE):
                s = SLAB["mod"] + j
                dve.wait_ge(slab_in[s % RING], 16 * (s // RING + 1))
                if i >= 2:
                    dve.wait_ge(slab_used, SLAB["mod"] + MOD_DVE[i - 2] + 1)
                modulate(gemv[:, i % 2], slab_k(s), NK * i, mod_k)
                if j == 5:
                    inverse_rms(0, SLOW["rms0"])
                    for k in range(NK):
                        tt_(hT[:, k], xT[:, k], rb, ALU.mult).then_inc(hx, 1)
            side_copied(dve, SIDE["vec"])
            side_read(dve, SIDE["mod"])
            stt(mod[:, 0:16], side(SIDE["mod"])[:, 0:16], float(D), vT[:, V_MB:V_MB + 16], ALU.mult, ALU.add
                ).then_inc(side_out[SIDE["mod"] % 3], 1)
            side_copied(dve, SIDE["mod"])
            stt(pre[:, :], mod[:, 8:16], 1.0, vT[:, V_PRE:V_PRE + NK], ALU.add, ALU.mult).then_inc(mod_ready, 1)
            S = [sc[:, i, :] for i in range(28)]
            lr, li = vT[:, V_LR:V_LR + GP], vT[:, V_LI:V_LI + GP]
            dve.wait_ge(dt_exp, 2)
            tt_(S[2], lr, S[1], ALU.mult).then_inc(s5_ang, 1)
            st.do(tt_(S[8], li, S[1], ALU.mult))
            st.do(tt_(S[10], lr, lr, ALU.mult))
            st.do(tt_(S[11], li, li, ALU.mult))
            st.settle()
            ROUND = 1.5 * 2.0 ** 23
            st.do(ts(S[9], S[8], 1.0 / (2.0 * math.pi), None, ALU.mult))
            st.do(tt_(S[10], S[10], S[11], ALU.add))
            st.settle()
            st.do(ts(S[9], S[9], ROUND, None, ALU.add))
            st.do(dve.reciprocal(S[11], S[10]))
            st.settle()
            st.do(ts(S[9], S[9], -ROUND, None, ALU.add))
            st.settle()
            for part in (6.28125, 0.001934051513671875, 1.2556659314782e-06):
                st.do(stt(S[8], S[9], -part, S[8], ALU.mult, ALU.add))
                st.settle()
            st.do(ts(S[3], S[8], 3.1415925, -3.1415925, ALU.min, ALU.max))
            st.settle()
            st.do(ts(S[7], S[3], -1.0, None, ALU.mult))
            st.settle()
            st.do(tt_(S[7], S[7], S[3], ALU.max))
            st.settle()
            ts(S[7], S[7], -1.0, math.pi / 2, ALU.mult, ALU.add).then_inc(s5_ang, 1)
            def first_rest(s):
                dve.wait_ge(w1_top, first_no(s) + 1)
                tt_(w_lo[:, s % RING], ring[:, s % RING], w1_hi[:, first_no(s) % 2].bitcast(F32), ALU.subtract
                    ).then_inc(w1_ready, 1)

            first_rest(SLAB["iq"])
            acc_read(dve, ACC["ik"])
            for k in range(NK):
                dve.wait_ge(h1_top, k + 1)
                tt_(h_lo[:, k], hT[:, k], h1_hi[:, k].bitcast(F32), ALU.subtract).then_inc(h1_split, 1)
            first_rest(SLAB["u"])
            dve.wait_ge(s5_trig, 3)
            apr, api = (apw[:, cc] for cc in range(2))
            st.do(dve.memset(apr[:, :, 0:1], 1.0))
            st.do(dve.memset(api[:, :, 0:1], 0.0))
            col = [s.unsqueeze(2) for s in S]
            st.do(tt_(apr[:, :, 1:2], col[4], col[6], ALU.mult))
            st.do(tt_(api[:, :, 1:2], col[4], col[5], ALU.mult))
            st.do(dve.memset(ph[:, 0, :, 0:1], 1.0))
            st.do(dve.memset(ph[:, 1, :, 0:1], 0.0))
            st.settle()
            for m in (1, 2, 4):
                t = [a_tmp[:, 64 * i:64 * i + GP * m].rearrange("p (g m) -> p g m", g=GP) for i in range(4)]
                a = [p[:, :, 1:m + 1] for p in (apr, api)]
                b = [p[:, :, m:m + 1].broadcast_to([P, GP, m]) for p in (apr, api)]
                cmul(apr[:, :, m + 1:2 * m + 1], api[:, :, m + 1:2 * m + 1], *a, *b, t)
                st.settle()
            st.do(ts(S[12], apr[:, :, 1], -1.0, None, ALU.add))
            st.settle()
            st.do(tt_(S[13], S[12], lr, ALU.mult))
            st.do(tt_(S[14], api[:, :, 1], li, ALU.mult))
            st.do(tt_(S[15], api[:, :, 1], lr, ALU.mult))
            st.do(tt_(S[16], S[12], li, ALU.mult))
            st.settle()
            st.do(tt_(S[13], S[13], S[14], ALU.add))
            st.do(tt_(S[15], S[15], S[16], ALU.subtract))
            st.settle()
            st.do(tt_(S[13], S[13], S[11], ALU.mult))
            tt_(S[15], S[15], S[11], ALU.mult).then_inc(s5_pow, 1)
            st.settle()
            dve.wait_ge(s5_pow, 1)
            dve.wait_ge(b_in, 32)
            f = [col[13].broadcast_to([P, GP, SP_]), col[15].broadcast_to([P, GP, SP_])]
            t = [a_tmp[:, 256 * i:256 * i + 256].rearrange("p (g q) -> p g q", g=GP) for i in range(4)]
            cmul(bb[:, 0], bb[:, 1], *f, brow[:, 0], brow[:, 1], t)
            st.settle()
            dve.wait_ge(x_in, 16)
            acc_copied(dve, ACC["x"] + NK - 1)
            for i in range(L):
                t = [a_tmp[:, 1024 * (i % 2) + 256 * n:1024 * (i % 2) + 256 * n + 256].rearrange(
                    "p (g q) -> p g q", g=GP) for n in range(4)]
                a = [p[:, :, L - 1 - i:L - i].broadcast_to([P, GP, SP_]) for p in (apr, api)]
                cmul(w1T[:, 0, :, i, :], w1T[:, 1, :, i, :], *a, bb[:, 0], bb[:, 1], t)
                if i in (1, 5):
                    first_rest(SLAB["u"] + 1 if i == 1 else SLAB["q"])
            st.settle()
            dve.sem_inc(s5_tables, 1)
            side_copied(dve, SIDE["iw"])
            for d in range(HI * (NT - 1)):
                if d % 6 == 3:
                    first_rest(SLAB["q"] + 1 + d // 6)
                tt, h = 1 + d // HI, d % HI
                w = P * (tt + 1)
                side_copied(dve, SIDE["dots"] + d)
                if h == 0:
                    ts(mb[:, tt, 0:w], relu[:, d % 2, 0:w], iw[:, tt, h:h + 1], None, ALU.mult).then_inc(score_mul, 1)
                else:
                    dve.wait_ge(score_mul, d)
                    stt(mb[:, tt, 0:w], relu[:, d % 2, 0:w], iw[:, tt, h:h + 1], mb[:, tt, 0:w],
                        ALU.mult, ALU.add).then_inc(score_mul, 1)
            first_rest(SLAB["v"] + 1)

            mag, pc, ps = S[17], S[18], S[19]
            st.do(tt_(mag, S[4], S[4], ALU.mult))
            src = (S[6], S[5])
            for n in range(3):
                st.do(tt_(S[20], src[0], src[0], ALU.mult))
                st.do(tt_(S[21], src[1], src[1], ALU.mult))
                st.do(tt_(S[22], src[0], src[1], ALU.mult))
                st.settle()
                st.do(tt_(pc, S[20], S[21], ALU.subtract))
                st.do(ts(ps, S[22], 2.0, None, ALU.mult))
                if n < 2:
                    st.do(tt_(mag, mag, mag, ALU.mult))
                st.settle()
                src = (pc, ps)
            st.do(dve.tensor_copy(rho, mag.unsqueeze(2).broadcast_to([P, GP, NM])))
            for m in (1, 2, 4, 8, 16, 32):
                t = [a_tmp[:, 512 * i:512 * i + GP * m].rearrange("p (g m) -> p g m", g=GP) for i in range(4)]
                a = [ph[:, cc, :, 0:m] for cc in range(2)]
                b = [s.unsqueeze(2).broadcast_to([P, GP, m]) for s in (pc, ps)]
                cmul(ph[:, 0, :, m:2 * m], ph[:, 1, :, m:2 * m], *a, *b, t)
                if m < 32:
                    st.do(tt_(S[20], pc, pc, ALU.mult))
                    st.do(tt_(S[21], ps, ps, ALU.mult))
                    st.do(tt_(S[22], pc, ps, ALU.mult))
                    st.settle()
                    st.do(tt_(pc, S[20], S[21], ALU.subtract))
                    st.do(ts(ps, S[22], 2.0, None, ALU.mult))
                st.settle()
            st.do(dve.memset(rho[:, :, 0:1], 0.0))

            def top8(tt, r):
                w = P * (tt + 1)
                src = work[:, 0:w] if r else mb[:, tt, 0:w]
                if r == 0:
                    dve.wait_ge(score_masked, tt)
                st.settle()
                st.do(dve.max(out=stat[:, 0:8], in_=src))
                st.settle()
                st.do(dve.match_replace(out=work[:, 0:w], in_to_replace=stat[:, 0:8], in_values=src,
                                        imm_value=TAKEN))

            def mask(tt):
                w = P * (tt + 1)
                st.settle()
                st.do(tt_(work[:, 0:w], work[:, 0:w], mb[:, tt, 0:w], ALU.not_equal))
                st.settle()
                ts(mb[:, tt, 0:w], work[:, 0:w], -1.0, BIG, ALU.add, ALU.mult).then_inc(mask_ready, 1)

            def topk(tt):
                for r in range(TOPK // 8):
                    top8(tt, r)
                mask(tt)

            topk(1)
            side_read(dve, SIDE["w1"] + 7)
            for hf in range(2):
                nr, ni = SIDE["state"] + 2 * hf, SIDE["state"] + 2 * hf + 1
                g = slice(8 * hf, 8 * hf + 8)
                vr, vi = (side(n)[:, :].rearrange("p (g m) -> p g m", g=8) for n in (nr, ni))
                t = [a_tmp[:, 512 * i:512 * i + 512].rearrange("p (g m) -> p g m", g=8) for i in range(4)]
                side_read(dve, ni)
                st.do(tt_(t[0], vr, ph[:, 0, g], ALU.mult))
                st.do(tt_(t[1], vi, ph[:, 1, g], ALU.mult))
                tt_(t[2], vr, ph[:, 1, g], ALU.mult).then_inc(side_out[nr % 3], 1)
                tt_(t[3], vi, ph[:, 0, g], ALU.mult).then_inc(side_out[ni % 3], 1)
                st.settle()
                side_copied(dve, nr)
                side_copied(dve, ni)
                st.do(tt_(zst[:, 0, g], t[0], t[1], ALU.add))
                st.do(tt_(zst[:, 1, g], t[3], t[2], ALU.subtract))
                st.settle()
            for cc in range(2):
                z = zst[:, cc].rearrange("p g m -> p (g m)")
                st.do(dve.tensor_tensor_scan(z, rho.rearrange("p g m -> p (g m)"), z, 0.0, ALU.mult, ALU.add))
            st.settle()
            for hf in range(2):
                g = slice(8 * hf, 8 * hf + 8)
                t = [a_tmp[:, 512 * i:512 * i + 512].rearrange("p (g m) -> p g m", g=8) for i in range(4)]
                cmul(xst[:, 0, g, 1:], xst[:, 1, g, 1:], zst[:, 0, g], zst[:, 1, g], ph[:, 0, g], ph[:, 1, g], t)
                st.settle()
            dve.memset(xst[:, :, :, 0:1], 0.0).then_inc(state_ready, 1)
            topk(2)
            dve.wait_ge(y_in, 16)
            for a in range(NB):
                stt(yback[:, a], tiles(a_u, NB)[:, a], vT[:, V_SD + a:V_SD + a + 1], yback[:, a],
                    ALU.mult, ALU.add).then_inc(yd_ready, 1)
            for a in range(GH):
                n = ACC["gr"] + a
                dve.wait_ge(r_sig, a + 1)
                tt_(sr[:, a], sr[:, a], acc(n)[:, :], ALU.mult).then_inc(acc_out[n % 4], 1)
            for a in range(2):
                n = SIDE["z"] + a
                side_read(dve, n)
                dve.wait_ge(f_abs, a + 1)
                ts(cum[:, a], side(n)[:, :], vT[:, V_GB + a:V_GB + a + 1], 0.0, ALU.add, ALU.min
                   ).then_inc(side_out[n % 3], 1)
            side_copied(dve, SIDE["z"])
            side_copied(dve, SIDE["z"] + 1)
            dve.wait_ge(f_exp, 2)
            st.do(tt_(cum, cum, e1, ALU.subtract))
            st.settle()
            dve.wait_ge(g_zero, 3)
            for a in range(2):
                dve.tensor_tensor_scan(cum[:, a], keep, cum[:, a], 0.0, ALU.mult, ALU.add).then_inc(f_cum, 1)
            dve.wait_ge(f_cum, 2)
            cc = cum.rearrange("p a t -> p (a t)").rearrange("p (c t) -> p c t", t=GC)
            tt_(tail.rearrange("p a t -> p (a t)").rearrange("p (c t) -> p c t", t=GC),
                cc[:, :, GC - 1:GC].broadcast_to([P, 2 * NC, GC]), cc, ALU.subtract).then_inc(f_tail, 1)
            for a in range(NB):
                n = ACC["glu"] + 2 * a
                acc_copied(dve, n + 1)
                tt_(ys[:, 1, a].rearrange("p (m j) -> p j m", j=L),
                    acc(n)[:, :].rearrange("p (j m) -> p j m", j=L),
                    msig[:, a % 2].rearrange("p (j m) -> p j m", j=L), ALU.mult).then_inc(acc_out[n % 4], 1)
            def gla(part, b):
                if part == "decay":
                    dve.wait_ge(g_dec, 3)
                    for a in range(2):
                        acc_copied(dve, ACC["gq"] + a)
                        acc_copied(dve, ACC["gk"] + a)
                    stt(gq, gq, GDK ** -0.5, e1, ALU.mult, ALU.mult).then_inc(g_k, 1)
                    tt_(e2, gk, e2, ALU.mult).then_inc(g_k, 1)
                    tt_(e3, gk, e3, ALU.mult).then_inc(g_k, 1)
                elif part == "gatt":
                    n = ACC["gatt"] + b
                    acc_read(dve, n)
                    dve.copy_predicated(gatt[:, b], chunkmask[:, :].bitcast(U32).unsqueeze(1).broadcast_to([P, NT, P]),
                                        acc(n)[:, :].rearrange("p (t q) -> p t q", t=NT)).then_inc(acc_out[n % 4], 1)
                elif part == "kv":
                    for pr in range(2):
                        n, cl = ACC["kv"] + 2 * pr + b % 2, b // 2
                        acc_read(dve, n)
                        if b == NC - 2:
                            acc_copied(dve, ACC["kv"] + 2 * pr + (b - 1) % 2)
                        elif b:
                            dve.wait_ge(carried, 2 * (b - 1) + pr + 1)
                        ins = stt(sprev[:, pr, b + 1, :], sprev[:, pr, b, :], e1[:, pr, GC * b + GC - 1:GC * b + GC],
                                  acc(n)[:, GDV * cl:GDV * cl + GDV], ALU.mult, ALU.add)
                        ins.then_inc(acc_out[n % 4] if b >= NC - 3 else carried, 1)
                elif part == "sum":
                    acc_copied(dve, ACC["o"] + b)
                    dve.tensor_reduce(stat[:, 16 + 4 * b:20 + 4 * b], osq.rearrange("p (h e) -> p h e", h=GH),
                                      AX.X, ALU.add).then_inc(o_sum, 1)
                    if b == 3:
                        dve.wait_ge(o_sum, NT)
                        ts(stat[:, 16:32], stat[:, 16:32], 1.0 / GDV, EPS, ALU.mult, ALU.add).then_inc(o_sum, 1)
                elif part == "inverse":
                    dve.wait_ge(o_root, 1)
                    dve.reciprocal(stat[:, 16:32], stat[:, 16:32]).then_inc(o_inv, 1)
                elif part == "norm":
                    dve.wait_ge(o_inv, 1)
                    for c in range(2 * b, 2 * b + 2):
                        for i in range(2):
                            v, col = o_part(c)[:, i], 16 + 4 * c + 2 * i
                            tt_(v, v, stat[:, col:col + 2].unsqueeze(2).broadcast_to([P, 2, GDV]), ALU.mult
                                ).then_inc(o_norm, 1)
                else:
                    n = ACC["ot"] + b
                    acc_read(dve, n)
                    stt(ys[:, 2, b], acc(n)[:, :], vT[:, V_GN + b:V_GN + b + 1], sr[:, b], ALU.mult, ALU.mult
                        ).then_inc(acc_out[n % 4], 1)

            def rest(s, per=0, it=0, kt=NK):
                dve.wait_ge(w_top, it * per + (split_no(s) + 1))
                tt_(w_lo[:, s % RING, 0:kt * SW], ring[:, s % RING, 0:kt * SW],
                    w_hi[:, slot(s), 0:kt * SW].bitcast(F32), ALU.subtract).then_inc(w_ready, 1)

            dve.wait_ge(mask0_ready, 1)
            for i in range(NT * HA + 2):
                if i >= 2 and (i - 2) % HA == HA - 1:
                    tt = (i - 2) // HA
                    dve.wait_ge(p_ready, HA * (tt + 1))
                    st.do(dve.reciprocal(asum[:, tt], asum[:, tt]))
                    st.settle()
                    slow_read(dve, SLOW["pv"] + tt)
                    tt_(ytok[:, tt].rearrange("p (h d) -> p h d", h=HA), slow[:, :].rearrange("p (h d) -> p h d", h=HA),
                        asum[:, tt].unsqueeze(2).broadcast_to([P, HA, DH]), ALU.mult).then_inc(slow_out, 1)
                if i < NT * HA:
                    tt, h = i // HA, i % HA
                    w, n = P * (tt + 1), s_use(i)
                    if h == 0 and tt:
                        dve.wait_ge(mask_ready, tt)
                    side_read(dve, n)
                    if i >= 2:
                        dve.wait_ge(p_ready, i - 1)
                    dve.tensor_tensor_reduce(logit[:, i % 2, 0:w], side(n)[:, 0:w], mb[:, tt, 0:w], -(DH ** -0.5),
                                             3.0e38, ALU.add, ALU.min, amax[:, tt, h:h + 1]).then_inc(side_out[n % 3], 1)
                if i in DVE_GLA:
                    gla(*DVE_GLA[i])
                if 2 <= i < 2 + TOPK // 8:
                    top8(NT - 1, i - 2)
                elif i == 2 + TOPK // 8:
                    mask(NT - 1)
            rest(SLAB["merge"])
            for k in range(NK):
                dve.wait_ge(h_top, k + 1)
                tt_(h_lo[:, k], hT[:, k], h_hi[:, k].bitcast(F32), ALU.subtract).then_inc(h_split, 1)
            rest(SLAB["merge"] + 1, kt=NB)
            dve.wait_ge(y0_whole, NT)
            side_copied(dve, SIDE["ya"] + NT - 1)
            tt_(ys_lo[:, 0], ys[:, 0], ys_hi0[:, :, :].bitcast(F32), ALU.subtract).then_inc(y0_split, 1)

            with dve.Fori(0, 2) as it:
                for step in range(6):
                    jj, i = step // NBR, step % NBR
                    dve.wait_ge(fmod_in, it * 96 + 16 * (step + 1))
                    n = SIDE["fmod"] + step
                    dve.wait_ge(side_out[(n - 2) % 3], it * 2 + ((n - 2) // 3 + 1))
                    modulate(gemv[:, step % 2], fmod_slab, NK * step, gemv_k, it, 6 * NK)
                    rest(SLAB["merge"] + 2 * step + 2, 12, it)
                    for q in range(2):
                        n = ACC["merge"] + 4 * step + q
                        m = merged[:, bass.ds(it * 4 + (2 * jj + q), 1), :].squeeze(1)
                        dve.wait_ge(acc_done, it * 24 + (n + 3))
                        dve.wait_ge(acc_out[n % 4], it * 6 + (n // 4 + 1))
                        dst = m if i == 0 else mtmp
                        tt_(dst, acc(n + 2)[:, :], msig[:, q], ALU.mult).then_inc(acc_out[(n + 2) % 4], 1)
                        dve.wait_ge(acc_out[(n + 2) % 4], it * 6 + ((n + 2) // 4 + 1))
                        if i:
                            tt_(m, m, mtmp, ALU.add).then_inc(merge_sum, 1)
                            dve.wait_ge(merge_sum, it * 8 + (4 * jj + 2 * (i - 1) + q + 1))
                        if i == 2:
                            hi, lo = (x[:, bass.ds(it * 4 + (2 * jj + q), 1), :].squeeze(1) for x in (m_hi, m_lo))
                            dve.tensor_copy(hi, m).then_inc(m_split, 1)
                            dve.wait_ge(m_split, it * 8 + (4 * jj + 2 * q + 1))
                            tt_(lo, m, hi.bitcast(F32), ALU.subtract).then_inc(m_split, 1)
                    rest(SLAB["merge"] + 2 * step + 3, 12, it, NB)
                    n = SIDE["fmod"] + step
                    dve.wait_ge(side_done, it * 6 + (n + 1))
                    stt(fmod[:, bass.ds(it * 12 + 2 * step, 2)], side(n)[:, 0:2], float(D),
                        vT[:, bass.ds(it * 12 + (V_FMB + 2 * step), 2)], ALU.mult, ALU.add).then_inc(side_out[n % 3], 1)
            dve.wait_ge(half_top, 1)
            s = SLAB["out"] + 1
            tt_(w_lo[:, s % RING, NB * SW:], ring[:, s % RING, NB * SW:], w_hi[:, slot(s), NB * SW:].bitcast(F32), ALU.subtract
                ).then_inc(half_ready, 1)
            rest(SLAB["out"] + 2)
            for j in range(4):
                dve.wait_ge(modg_in[j % 2], 16 * (j // 2 + 1))
                if j < 2:
                    side_copied(dve, SIDE["fmod"] + 10 + j)
                else:
                    dve.wait_ge(fmod_used, 12 + j)
                modulate(gemv[:, j % 2], (fmod_slab, modg_slab)[j % 2], NK * (12 + j), gemv_k)
                if j == 1:
                    rest(SLAB["out"] + 3)
            for step in range(9, 12):
                side_copied(dve, SIDE["fmod"] + step)
            st.do(tt_(fpost[:, :], fmod[:, 16:24], vT[:, V_FPOST:V_FPOST + NK], ALU.mult))
            stt(fpre[:, :], fmod[:, 8:16], 1.0, vT[:, V_FPRE:V_FPRE + NK], ALU.add, ALU.mult).then_inc(fmod_ready, 1)
            def residual(factor, signal):
                base = st.n
                for k in range(NK + 2):
                    if k < NK:
                        st.do(tt_(yT[:, k], yT[:, k], rb, ALU.mult))
                    if k >= 2:
                        dve.wait_ge(vstep, base + k - 1)
                        stt(x1[:, k - 2], yT[:, k - 2], factor[:, k - 2:k - 1], x1[:, k - 2], ALU.mult, ALU.add
                            ).then_inc(signal, 1)

            side_read(dve, SIDE["modg"])
            st.do(stt(mod[:, 16:24], side(SIDE["modg"])[:, 0:8], float(D), vT[:, V_MB + 16:V_MB + 24], ALU.mult, ALU.add))
            st.settle()
            tt_(post[:, :], mod[:, 16:24], vT[:, V_POST:V_POST + NK], ALU.mult).then_inc(side_out[SIDE["modg"] % 3], 1)
            side_copied(dve, SIDE["modg"])
            inverse_rms(1, SLOW["rms1"])
            dve.wait_ge(x_back, 16)
            dve.wait_ge(y_copied, NK)
            residual(post, x1_ready)
            rest(SLAB["up"])
            dve.wait_ge(x1_ready, NK)
            inverse_rms(2, SLOW["rms2"])
            for k in range(NK + 3):
                if k < NK:
                    tt_(hT[:, k], x1[:, k], rb, ALU.mult).then_inc(hx, 1)
                if k >= 3:
                    dve.wait_ge(h2_top, 2 * (k - 3) + 2)
                    tt_(h_lo[:, k - 3], hT[:, k - 3], h_hi[:, k - 3].bitcast(F32), ALU.subtract).then_inc(h2_ready, 1)
            rest(SLAB["up"] + 1)

            dve.sem_inc(ff_ready, 2)

            def up_pair(it, pair, s):
                for r in range(4):
                    n, j = ACC["up"] + 4 * pair + r, 4 * pair + r
                    dve.wait_ge(conv_0, it * 12 + (j + 1))
                    stt(cb[:, r, 1:], acc(n)[:, 0:T - 1], cs[:, s, 1, r:r + 1], cb[:, r, 1:], ALU.mult, ALU.add
                        ).then_inc(conv_1, 1)
                    dve.wait_ge(conv_1, it * 12 + (j + 1))
                    stt(cb[:, r, 2:], acc(n)[:, 0:T - 2], cs[:, s, 0, r:r + 1], cb[:, r, 2:], ALU.mult, ALU.add
                        ).then_inc(acc_out[n % 4], 1)
                    if r == 1:
                        rest(SLAB["up"] + 2 * pair + 2, 6, it)
                for q in range(2):
                    n = ACC["up"] + 4 * pair + 2 + q
                    dve.wait_ge(acc_out[n % 4], it * 3 + (n // 4 + 1))
                    dve.wait_ge(gelu_out, it * 6 + (2 * pair + q + 3))
                    dst = ff[:, bass.ds(it * 6 + (2 * pair + q), 1), :].squeeze(1) if pair < 9 else ff[:, 2 * pair + q]
                    tt_(dst, gl[:, q], cb[:, 2 + q], ALU.mult).then_inc(ff_ready, 1)
                rest(SLAB["up"] + 2 * pair + 3, 6, it)

            def ff_rest(j):
                dve.wait_ge(ff_top, j + 1)
                tt_(ff_lo[:, j % 2], arena[:, 2 * T * j:2 * T * j + 2 * T], ff_hi[:, j % 2].bitcast(F32), ALU.subtract
                    ).then_inc(ff_split, 1)

            with dve.Fori(0, 3) as it:
                for s in range(3):
                    up_pair(it, s, s)
            up_pair(0, 9, 0)
            for j in range(2):
                ff_rest(j)
            up_pair(0, 10, 1)
            for j in range(2, NF // 2):
                rest(SLAB["down"] + j)
                ff_rest(j)
            for m in DOWN_ORDER:
                if m < 4:
                    acc_copied(dve, ACC["down"] + m)
                elif m < 7:
                    side_copied(dve, SIDE["down"] + m - 4)
                else:
                    slow_copied(dve, SLOW["down"])
                dve.tensor_copy(yT[:, m], down_bank(m)[:, :]).then_inc(y_copied, 1)
            dve.wait_ge(y_copied, 2 * NK)
            inverse_rms(3, SLOW["rms3"])
            residual(fpost, x2_ready)
            for n in (4, 6):
                acc_read(dve, ACC["xo"] + n)
                dve.tensor_copy(xo[:, n - 4, BW:D], acc(ACC["xo"] + n)[:, :]).then_inc(acc_out[(ACC["xo"] + n) % 4], 1)

        @block.tensor
        def _(pe):
            def mm(dst, w, moving, start, stop, signal=None, **kw):
                ins = pe.matmul(dst, w, moving, start=start, stop=stop, **kw)
                if signal is not None:
                    ins.then_inc(signal, 1)

            def take(s):
                pe.wait_ge(slab_in[s % RING], 16 * (s // RING + 1))

            def acc_free(n):
                if n >= 4:
                    acc_copied(pe, n - 4)

            def side_free(n):
                if n >= 3:
                    side_copied(pe, n - 3)

            def channel_tile(n, s, q, moving, kt=NK, cols=SW):
                acc_free(n)
                for k in range(kt):
                    mm(acc(n)[:, :], slab_k(s, cols)[:, k, P * q:P * q + P], moving[:, k], k == 0, k == kt - 1,
                       slab_used if k == 0 and q == 0 else acc_done if k == kt - 1 else None)

            def first_tile(name, a):
                s, q, n = SLAB[name] + a // 2, a % 2, ACC[name] + a
                acc_free(n)
                if q == 0:
                    pe.wait_ge(w1_ready, first_no(s) + 1)
                for k in range(NK):
                    if name == "iq" and a == 0:
                        pe.wait_ge(h1_split, k + 1)
                    for i, (wp, mp) in enumerate(PARTS):
                        w = (w1_hi[:, first_no(s) % 2], w_lo[:, s % RING])[wp].rearrange("p (k n) -> p k n", n=SW)
                        first, last = k == i == 0, k == NK - 1 and i == 2
                        mm(acc(n)[:, :], w[:, k, P * q:P * q + P], (h1_hi, h_lo)[mp][:, k], first, last,
                           acc_done if last else slab_used if first and q == 0 and name != "iq" else None)

            def first_tokens(name):
                for half in range(2):
                    s = SLAB[name] + half
                    pe.wait_ge(w1_ready, first_no(s) + 1)
                    for tt in range(NT):
                        n = ACC[name] + tt
                        if half == 0:
                            acc_free(n)
                        for k in range(4):
                            for i, (wp, mp) in enumerate(PARTS):
                                w = (w1_hi[:, first_no(s) % 2], w_lo[:, s % RING])[wp].rearrange(
                                    "p (k n) -> p k n", n=BW)
                                last = half == 1 and k == 3 and i == 2
                                mm(acc(n)[:, :], (h1_hi, h_lo)[mp][:, 4 * half + k, P * tt:P * tt + P], w[:, k, :],
                                   half == k == i == 0, last, acc_done if last else slab_used if tt == k == i == 0
                                   else None)

            def split_tile(n, s, q, moving, kt=NK, ready=None, per=1):
                for k in range(kt):
                    if ready is not None:
                        pe.wait_ge(ready, per * (k + 1))
                    for i, (wp, mp) in enumerate(PARTS):
                        w = (w_hi[:, slot(s)], w_lo[:, s % RING])[wp].rearrange("p (k n) -> p k n", n=SW)
                        first, last = k == i == 0, k == kt - 1 and i == 2
                        mm(acc(n)[:, :], w[:, k, P * q:P * q + P], moving[mp][:, k], first, last,
                           acc_done if last else slab_used if first and q == 0 else None)

            def project(name, a):
                s = SLAB[name] + a // 2
                if a % 2 == 0:
                    take(s)
                channel_tile(ACC[name] + a, s, a % 2, hT)

            def token_tiles(name):
                for half in range(2):
                    s = SLAB[name] + half
                    take(s)
                    for tt in range(NT):
                        n = ACC[name] + tt
                        if half == 0:
                            acc_free(n)
                        for k in range(4):
                            mm(acc(n)[:, :], hT[:, 4 * half + k, P * tt:P * tt + P], slab_k(s, BW)[:, k, :],
                               half == k == 0, half == 1 and k == 3,
                               slab_used if tt == k == 0 else acc_done if half == 1 and k == 3 else None)

            def modulate(use, j, part, signal, last):
                for q in range(2):
                    mm(side(use)[:, 2 * j + q:2 * j + q + 1], part[:, P * q:P * q + P], mean[:, 0:1], True, True,
                       side_done if last and q else signal if last or q else None)

            def sum_squares(k, name):
                mm(slow[:, :], mean[:, :], sq[:, k % 2], k == 0, k == NK - 1,
                   slow_done if k == NK - 1 else sq_used)

            def dots(d):
                n, tt, h = SIDE["dots"] + d, 1 + d // HI, d % HI
                part, w = slice(DI * (h % 4), DI * (h % 4) + DI), P * (tt + 1)
                side_free(n)
                mm(side(n)[:, 0:w], iqT[part, h // 4, P * tt:P * tt + P], ikT[part, 0:w], True, True, side_done)

            pe.wait_ge(consts, 4)
            pe.wait_ge(c_row_in, 16)
            pe.transpose(side(SIDE["c"])[:, 0:NK], c_row, ident[0:NK, 0:NK]).then_inc(side_done, 1)
            pe.wait_ge(vec_in, 16 * 14)
            n = SIDE["vec"]
            pe.transpose(side(n)[:, 0:V_CW], vrow[0:V_CW, 0, :], ident[0:V_CW, 0:V_CW])
            pe.transpose(side(n)[:, V_CW:V_CW + P], vrow[:, 1, :], ident[:, :])
            pe.transpose(side(n)[:, V_CW + P:V_N], vrow[0:V_N - V_CW - P, 2, :],
                         ident[0:V_N - V_CW - P, 0:V_N - V_CW - P]).then_inc(side_done, 1)
            side_free(SIDE["mod"])
            def mod_slab(j):
                if j in MOD_DVE:
                    i = MOD_DVE.index(j)
                    pe.wait_ge(mod_k, NK * (i + 1))
                    modulate(SIDE["mod"], j, gemv[:, i % 2], slab_used, j == 7)
                else:
                    pe.wait_ge(c_silu, 2)
                    take(SLAB["mod"] + j)
                    for q in range(2):
                        for kk in range(NK):
                            mm(side(SIDE["mod"])[:, 2 * j + q:2 * j + q + 1],
                               slab_k(SLAB["mod"] + j)[:, kk, P * q:P * q + P], csil_d[:, kk:kk + 1], kk == 0,
                               kk == NK - 1, slab_used if q and kk == NK - 1 else None)

            for j in range(2):
                mod_slab(j)
            pe.wait_ge(x_in, 16)
            for k in range(NK + 1):
                if k < NK:
                    n = ACC["x"] + k
                    acc_free(n)
                    for tt in range(NT):
                        ins = pe.transpose(acc(n)[:, P * tt:P * tt + P], xtok[:, tt, P * k:P * k + P], ident[:, :])
                    ins.then_inc(acc_done, 1)
                if k:
                    acc_copied(pe, ACC["x"] + k - 1)
                    sum_squares(k - 1, "rms0")
                for j in {2: [2], 5: [3], 8: range(4, 8)}.get(k, ()):
                    mod_slab(j)
            pe.wait_ge(c_in, 64)
            for cc in range(2):
                n = SIDE["ctr"] + cc
                for r in range(4):
                    ins = pe.transpose(side(n)[:, P * r:P * r + P],
                                       crow[:, cc, r].rearrange("p d n -> p (d n)"), ident[:, :])
                ins.then_inc(side_done, 1)
            pe.wait_ge(small_in, 16 * 7)
            for name, c0, w in (("lr", 4 * DI, RANK + HI), ("ik", 0, P)):
                n = ACC[name]
                acc_free(n)
                for k in range(NK):
                    pe.wait_ge(h_ready, k + 1)
                    mm(acc(n)[0:w, :], wsmall[:, k, c0:c0 + w], hT[:, k], k == 0, k == NK - 1,
                       acc_done if k == NK - 1 else None)
            for a in range(2):
                first_tile("iq", a)
            acc_copied(pe, ACC["lr"])
            n = SIDE["iw"]
            side_free(n)
            for tt in range(NT):
                c0 = (RANK + HI) * tt
                ins = pe.transpose(side(n)[:, c0:c0 + RANK + HI], lrT[:, P * tt:P * tt + P],
                                   ident[0:RANK + HI, 0:RANK + HI])
            ins.then_inc(side_done, 1)
            for a in range(3 * NB):
                first_tile(("u", "q", "k")[a // NB], a % NB)
                if a == 4:
                    acc_copied(pe, ACC["iq"] + 1)
                    acc_copied(pe, ACC["ik"])
                for d in dots_after(a):
                    dots(d)
            first_tokens("v")
            pe.wait_ge(s5_tables, 1)
            pe.wait_ge(cpair_ready, 4)
            n = SIDE["lag"]
            side_free(n)
            for g in range(GP):
                for cc in range(2):
                    mm(side(n)[:, 2 * SP_ * g:2 * SP_ * g + 2 * SP_], w1T[:, cc, g].rearrange("p i q -> p (i q)"),
                       cpair[:, cc, g].rearrange("p d q -> p (d q)"), cc == 0, cc == 1,
                       side_done if g == GP - 1 and cc else None)
            for b in range(8):
                n, cc = SIDE["w1"] + b, b // 4
                side_free(n)
                for i in range(4):
                    ins = pe.transpose(side(n)[:, P * i:P * i + P],
                                       w1T[:, cc, 4 * (b % 4) + i].rearrange("p i q -> p (i q)"), ident[:, :])
                ins.then_inc(side_done, 1)
            side_copied(pe, SIDE["lag"])
            for j in range(L):
                n, c0 = SIDE["shift"] + j, SP_ * (L - 1 - j)
                side_free(n)
                mm(side(n)[:, :], wide[:, c0:c0 + P], lag, True, True, side_done)
            pe.wait_ge(ub_in, 16 * L)
            for hf in range(2):
                for cc in range(2):
                    n = SIDE["state"] + 2 * hf + cc
                    side_free(n)
                    for g in range(16 * hf, 16 * hf + 16):
                        part = slice(SN * (g % 2), SN * (g % 2) + SN)
                        col = NM * (g // 2 % 8)
                        mm(side(n)[part, col:col + NM], w1[:, cc, g // 2, part], ub[:, g], True, True,
                           side_done if g == 16 * hf + 15 else None)
            pe.wait_ge(h_back, NK)
            project("gq", 0)
            project("gq", 1)
            project("gk", 0)
            project("gk", 1)
            pe.wait_ge(state_ready, 1)
            for hf in range(2):
                for d in range(2):
                    n = SIDE["y"] + 2 * hf + d
                    side_free(n)
                    for i in range(8):
                        g = 2 * (8 * hf + i) + d
                        mm(side(n)[:, NM * i:NM * i + NM], toep[:, g].rearrange("p j q -> p (j q)"), ub[:, g],
                           i == 0, False, skip_group_check=True)
                for cc in range(2):
                    for i in range(8):
                        for d in range(2):
                            n, part, pair = SIDE["y"] + 2 * hf + d, slice(SN * d, SN * d + SN), 8 * hf + i
                            last = cc == 1 and i == 7
                            mm(side(n)[:, NM * i:NM * i + NM], w2[cc][part, pair].rearrange("p j q -> p (j q)"),
                               xst[part, cc, pair, 0:NM], False, last, side_done if last else None,
                               skip_group_check=True)
            token_tiles("gv")
            for a in range(GH):
                project("gr", a)
            for a in range(2):
                n = SIDE["z"] + a
                side_free(n)
                mm(side(n)[:, :], wgate[:, P * a:P * a + P], lrT[0:RANK, :], True, True, side_done)
            for half in range(2):
                take(SLAB["glu"] + half)
            pe.wait_ge(g_ready, NB)
            for a in range(NB):
                for half in range(2):
                    n, s = ACC["glu"] + 2 * a + half, SLAB["glu"] + half
                    acc_free(n)
                    for k in range(NB):
                        mm(acc(n)[:, :], slab_k(s, BW)[:, k, P * a:P * a + P], yback[:, k], k == 0, k == NB - 1,
                           acc_done if k == NB - 1 else slab_used if k == 0 and a == 0 and half == 0
                           else slab_used if k == 0 and a == NB - 1 and half == 1 else None)
            def gla(part, b):
                if part == "kt":
                    n = ACC["kt"] + b
                    acc_free(n)
                    pe.wait_ge(g_k, 3)
                    for tt in range(NT):
                        ins = pe.transpose(acc(n)[:, P * tt:P * tt + P], e3[:, b, P * tt:P * tt + P], ident[:, :])
                    ins.then_inc(acc_done, 1)
                elif part == "gatt":
                    n, half = ACC["gatt"] + b, slice(GDK * (b % 2), GDK * (b % 2) + GDK)
                    acc_free(n)
                    for tt in range(NT):
                        tok = slice(P * tt, P * tt + P)
                        mm(acc(n)[:, tok], e2[half, b // 2, tok], gq[half, b // 2, tok], True, True,
                           acc_done if tt == NT - 1 else None)
                elif part == "kv":
                    acc_copied(pe, ACC["kt"] + b)
                    for hf in range(2):
                        n, rws = ACC["kv"] + 2 * b + hf, slice(GC * hf, GC * hf + GC)
                        acc_free(n)
                        for cl in range(4 - hf):
                            ch = 2 * cl + hf
                            for d in range(2):
                                half = slice(GDK * d, GDK * d + GDK)
                                mm(acc(n)[half, GDV * cl:GDV * cl + GDV],
                                   ktok[rws, ch // 2, P * b + GDK * d:P * b + GDK * d + GDK],
                                   gv[rws, ch // 2, GDV * (2 * b + d):GDV * (2 * b + d) + GDV], True, True,
                                   acc_done if cl == 3 - hf and d else None)
                elif part == "o":
                    n, half = ACC["o"] + b, slice(GDK * (b % 2), GDK * (b % 2) + GDK)
                    if b == 0:
                        for h in range(GH):
                            acc_copied(pe, ACC["gatt"] + h)
                        for kv in range(4):
                            acc_copied(pe, ACC["kv"] + kv)
                    acc_free(n)
                    for i in range(4):
                        tt, h = 2 * (b // 2) + i // 2, b % 2 + 2 * (i % 2)
                        col = slice(GDV * i, GDV * i + GDV)
                        mm(acc(n)[:, col], gatt[:, h, tt, :], gv[:, tt, GDV * h:GDV * h + GDV], True, False,
                           skip_group_check=True)
                        for hf in range(2):
                            ch = 2 * tt + hf
                            if ch:
                                mm(acc(n)[GC * hf:GC * hf + GC, col], gq[half, h // 2, GC * ch:GC * ch + GC],
                                   sprev[half, h // 2, ch, :], False, True,
                                   acc_done if i == 3 and hf else None, skip_group_check=True)
                else:
                    n = ACC["ot"] + b
                    acc_free(n)
                    pe.wait_ge(o_norm, 8)
                    for tt in range(NT):
                        ins = pe.transpose(acc(n)[:, P * tt:P * tt + P], og[:, tt, GDV * b:GDV * b + GDV], ident[:, :])
                    ins.then_inc(acc_done, 1)

            pe.wait_ge(q_pad, 2)
            for i in range(NT * HA + 2):
                if i < NT * HA:
                    n, tt, h = s_use(i), i // HA, i % HA
                    w = P * (tt + 1)
                    side_free(n)
                    mm(side(n)[:, 0:w], (q_sb, q_odd)[h % 2][:, h // 2, P * tt:P * tt + P], k_sb[:, h // 2, 0:w],
                       True, True, side_done)
                turns, outputs = [], []
                if 1 <= i <= NT * HA:
                    side_free(pt_use(i - 1))
                    pe.wait_ge(p_ready, i)
                    turns = list(range((i - 1) // HA + 1))
                if i >= 2:
                    tt, h = (i - 2) // HA, (i - 2) % HA
                    if h == 0:
                        slow_copied(pe, SLOW["pv"] + tt - 1)
                    side_copied(pe, pt_use(i - 2))
                    outputs = list(range(tt + 1))
                for j in range(NT):
                    if j in turns:
                        ins = pe.transpose(side(pt_use(i - 1))[:, P * j:P * j + P],
                                           prob[:, (i - 1) % 2, P * j:P * j + P], ident[:, :])
                        if j == turns[-1]:
                            ins.then_inc(side_done, 1)
                    if j in outputs:
                        mm(slow[:, DH * h:DH * h + DH], probT[:, i % 2, P * j:P * j + P],
                           v_sb[:, j, DH * h:DH * h + DH], j == 0, j == tt,
                           slow_done if h == HA - 1 and j == tt else None)
                if i in PE_GLA:
                    gla(*PE_GLA[i])
            for tt in range(NT):
                n = SIDE["ya"] + tt
                side_free(n)
                slow_copied(pe, SLOW["pv"] + tt)
                for a in range(NB):
                    ins = pe.transpose(side(n)[:, P * a:P * a + P], ytok[:, tt, P * a:P * a + P], ident[:, :])
                ins.then_inc(side_done, 1)
            with pe.Fori(0, 2) as it:
                for step in range(6):
                    i, s = step % NBR, SLAB["merge"] + 2 * step
                    for m, moving, kt in ((0, (h_hi, h_lo), NK), (1, (ys_hi[i], ys_lo[:, i]), NB)):
                        pe.wait_ge(w_ready, it * 12 + (split_no(s) + m + 1))
                        if m:
                            pe.wait_ge(y_split if i else y0_split, max(i, 1))
                        for q in range(2):
                            n = ACC["merge"] + 4 * step + 2 * m + q
                            pe.wait_ge(acc_out[n % 4], it * 6 + n // 4)
                            split_tile(n, s + m, q, moving, kt, h_split if step == m == q == 0 else None)
                    n = SIDE["fmod"] + step
                    pe.wait_ge(gemv_k, it * (6 * NK) + NK * (step + 1))
                    pe.wait_ge(side_out[n % 3], it * 2 + n // 3)
                    for q in range(2):
                        mm(side(n)[:, q:q + 1], gemv[:, step % 2, P * q:P * q + P], mean[:, 0:1], True, True,
                           side_done if q else fmod_used)
            for k in range(NK + 1):
                if k < NK:
                    s = SLAB["out"] + k // 2
                    if k % 2 == 0:
                        pe.wait_ge(w_ready, split_no(s) + 1)
                    if k == 2:
                        pe.wait_ge(half_ready, 1)
                    acc_free(ACC["out"] + k)
                    if k >= 4:
                        pe.wait_ge(y_copied, k - 3)
                    split_tile(ACC["out"] + k, s, k % 2, (m_hi, m_lo), ready=None if k else m_split, per=2)
                if k:
                    acc_copied(pe, ACC["out"] + k - 1)
                    sum_squares(k - 1, "rms1")
                if k in (3, 5, 7, 8):
                    j = (3, 5, 7, 8).index(k)
                    if j == 0:
                        side_free(SIDE["modg"])
                    pe.wait_ge(gemv_k, NK * (12 + j + 1))
                    modulate(SIDE["modg"], j, gemv[:, j % 2], fmod_used, j == 3)
            for k in range(NK):
                pe.wait_ge(sq_ready, k + 1)
                if k == 0:
                    slow_copied(pe, SLOW["rms1"])
                sum_squares(k, "rms2")

            def up_pair(it, pair):
                for r in range(4):
                    n, s = ACC["up"] + 4 * pair + r, SLAB["up"] + 2 * pair + r // 2
                    if r % 2 == 0:
                        pe.wait_ge(w_ready, it * 6 + (split_no(s) + 1))
                    pe.wait_ge(acc_out[n % 4], it * 3 + n // 4)
                    split_tile(n, s, r % 2, (h_hi, h_lo), ready=h2_ready if pair == r == 0 else None)

            with pe.Fori(0, 3) as it:
                for pair in range(3):
                    up_pair(it, pair)
            for pair in range(9, 11):
                up_pair(0, pair)
            slow_copied(pe, SLOW["rms2"])
            for j in range(NF // 2):
                s = SLAB["down"] + j
                pe.wait_ge(w_ready, split_no(s) + 1)
                pe.wait_ge(ff_split, j + 1)
                for kk in range(2):
                    tok = slice(T * kk, T * kk + T)
                    for m in DOWN_ORDER:
                        if j == kk == 0 and m < 4:
                            acc_free(ACC["down"] + m)
                        elif j == kk == 0 and m < 7:
                            side_free(SIDE["down"] + m - 4)
                        col = slice(D * kk + P * m, D * kk + P * m + P)
                        done = acc_done if m < 4 else side_done if m < 7 else slow_done
                        for i, (wp, mp) in enumerate(PARTS):
                            w, f = (w_hi[:, slot(s)], w_lo[:, s % RING])[wp], (ff_hi, ff_lo)[mp][:, j % 2]
                            last = j == NF // 2 - 1 and kk == 1 and i == 2
                            mm(down_bank(m)[:, :], w[:, col], f[:, tok], j == kk == i == 0, last,
                               done if last else slab_used if kk == i == 0 and m == DOWN_ORDER[0] else None)
            for i, m in enumerate(DOWN_ORDER):
                if m < 4:
                    acc_copied(pe, ACC["down"] + m)
                elif m < 7:
                    side_copied(pe, SIDE["down"] + m - 4)
                else:
                    slow_copied(pe, SLOW["down"])
                    pe.wait_ge(y_copied, NK + 1)
                sum_squares(i, "rms3")
            for n in range(8):
                half, tt = n // NT, n % NT
                pe.wait_ge(x2_ready, 4 * half + 4)
                acc_free(ACC["xo"] + n)
                for i in range(4):
                    ins = pe.transpose(acc(ACC["xo"] + n)[:, P * i:P * i + P],
                                       x1[:, 4 * half + i, P * tt:P * tt + P], ident[:, :])
                ins.then_inc(acc_done, 1)


_INS = ['x', 'c', 'mix_mod_w', 'mix_mod_b', 'mix_pre_g', 'mix_post_g', 'w_in', 's5_lam_re', 's5_lam_im', 's5_log_dt', 's5_b_re', 's5_b_im', 's5_c_re', 's5_c_im', 's5_d', 's5_w_glu', 'gla_w_gate', 'gla_b_gate', 'gla_norm_g', 'w_branch', 'w_out', 'ffn_mod_w', 'ffn_mod_b', 'ffn_pre_g', 'ffn_post_g', 'ffn_w_up', 'ffn_conv_w', 'ffn_conv_b', 'ffn_w_down']
_OUTS = [((1, T, D), 'float32')]


def kernel(**inputs):
    import numpy as _np
    import concourse.bacc as _bacc
    from concourse import mybir as _mybir
    from concourse.bass_utils import run_bass_kernel_spmd as _run

    nc = _bacc.Bacc("TRN2", target_bir_lowering=False, num_devices=1)
    arrays, args = {}, []
    for name in _INS:
        a = _np.ascontiguousarray(inputs[name])
        arrays[f"in_{name}_dram"] = a
        args.append(nc.dram_tensor(f"in_{name}_dram", a.shape, _mybir.dt.from_np(a.dtype), kind="ExternalInput").ap())
    for i, (shape, dtype) in enumerate(_OUTS):
        dt = _mybir.dt.from_np(_np.dtype(dtype))
        args.append(nc.dram_tensor(f"out_{i}_dram", shape, dt, kind="ExternalOutput").ap())
    trunk_kernel(nc, *args)
    r = _run(nc, [arrays], core_ids=[0])
    return r.results[0]["out_0_dram"]
```
